# Optimizing a Trainium2 kernel written in Bass

```python
import math
import jax
import jax.numpy as jnp
from jax import lax
import numpy as np

D_MODEL = 1024
BATCH = 1
SEQ = 256
DEPTH = 2

N_MIXERS = 4
PLE_DIM = 256
EPS = 1e-6

DSA_PATTERNS = ((128, 1), (512, 4), (2048, 16))
DSA_GROUPS = len(DSA_PATTERNS)
DSA_HEADS = 8
DSA_HEAD_DIM = D_MODEL // DSA_HEADS
DSA_IN = DSA_GROUPS * 3 * DSA_HEADS * DSA_HEAD_DIM

MLA_HEADS = D_MODEL // 64
MLA_Q_LORA = D_MODEL // 4
MLA_KV_LORA = D_MODEL // 8
MLA_NOPE = 64
MLA_ROPE = 32
MLA_V = 64
MLA_IN = MLA_Q_LORA + MLA_KV_LORA + MLA_ROPE
MLA_THETA = 10000.0
Q_BLOCK = 128

RET_HEADS = D_MODEL // 256
RET_QK = 256
RET_V = 512
RET_IN = RET_HEADS * (2 * RET_QK + 2 * RET_V)
RET_CHUNK = 128
RET_THETA = 10000.0

SSD_D_INNER = 2 * D_MODEL
SSD_HEAD_DIM = 64
SSD_HEADS = SSD_D_INNER // SSD_HEAD_DIM
SSD_GROUPS = 4
SSD_HEADS_PER_GROUP = SSD_HEADS // SSD_GROUPS
SSD_STATE = 128
SSD_CONV = 4
SSD_CONV_DIM = SSD_D_INNER + 2 * SSD_GROUPS * SSD_STATE
SSD_IN = SSD_D_INNER + SSD_CONV_DIM + SSD_HEADS
SSD_CHUNK = 128

MOE_GROUPS = 4
MOE_EXPERTS_PER_GROUP = 8
MOE_EXPERTS = MOE_GROUPS * MOE_EXPERTS_PER_GROUP
MOE_TOPK = 2
MOE_D_FF = D_MODEL // 2
MOE_BLOCK = 256

kernel_name = 'hybrid_dsa_mla_retnet_ssd_hmoe'

def _rmsnorm(x, g):
    xf = x.astype(jnp.float32)
    y = xf * lax.rsqrt(jnp.mean(xf * xf, axis=-1, keepdims=True) + EPS)
    return (y * g.astype(jnp.float32)).astype(x.dtype)

def _rope(x, theta):
    S, d = x.shape[1], x.shape[-1]
    half = d // 2
    inv = theta ** (-jnp.arange(half, dtype=jnp.float32) / half)
    ang = jnp.arange(S, dtype=jnp.float32)[:, None] * inv
    cos = jnp.cos(ang)[:, None, :]
    sin = jnp.sin(ang)[:, None, :]
    xf = x.astype(jnp.float32)
    x1, x2 = xf[..., :half], xf[..., half:]
    return jnp.concatenate([x1 * cos - x2 * sin, x1 * sin + x2 * cos], axis=-1).astype(x.dtype)

def _alibi_slopes(n):
    return 2.0 ** (-8.0 * jnp.arange(1, n + 1, dtype=jnp.float32) / n)

def _causal_conv(x, w, b):
    k, c = w.shape
    y = lax.conv_general_dilated(x, w[:, None, :].astype(x.dtype), window_strides=(1,),
                                 padding=[(k - 1, 0)], dimension_numbers=('NWC', 'WIO', 'NWC'),
                                 feature_group_count=c)
    return y + b.astype(x.dtype)

def _dilated_group(q, k, v, window, dil, slopes):
    Bn, S, H, dh = q.shape
    W = window // dil
    L = S // dil
    nb = -(-L // W)
    Lp = nb * W

    def to_res(t):
        t = t.reshape(Bn, L, dil, H, dh).transpose(0, 2, 3, 1, 4)
        t = jnp.pad(t, ((0, 0), (0, 0), (0, 0), (0, Lp - L), (0, 0)))
        return t.reshape(Bn, dil, H, nb, W, dh)

    def with_prev(t):
        prev = jnp.concatenate([jnp.zeros_like(t[:, :, :, :1]), t[:, :, :, :-1]], axis=3)
        return jnp.concatenate([prev, t], axis=4)

    def from_res(t):
        t = t.reshape(Bn, dil, H, Lp, *t.shape[5:])[:, :, :, :L]
        t = jnp.moveaxis(t, 3, 1)
        return t.reshape(Bn, S, H, *t.shape[4:])

    qb = to_res(q)
    kb = with_prev(to_res(k))
    vb = with_prev(to_res(v))
    s = jnp.einsum('brhnqd,brhnkd->brhnqk', qb, kb).astype(jnp.float32) * (dh ** -0.5)
    qi = jnp.arange(W)[:, None]
    kj = jnp.arange(2 * W)[None, :]
    steps = W + qi - kj
    key_step = jnp.arange(nb)[:, None, None] * W - W + kj
    valid = (steps >= 0) & (steps <= W) & (key_step >= 0)
    alibi = -slopes.astype(jnp.float32)[:, None, None, None] * (dil * steps).astype(jnp.float32)
    s = jnp.where(valid, s + alibi, -jnp.inf)
    m = jnp.max(s, axis=-1)
    e = jnp.exp(s - m[..., None])
    den = jnp.sum(e, axis=-1)
    o = jnp.einsum('brhnqk,brhnkd->brhnqd', e, vb.astype(jnp.float32)) / den[..., None]
    return from_res(o), from_res(m), from_res(den)

def _dilated_attention(h, w_in, w_out):
    Bn, S, _ = h.shape
    qkv = (h @ w_in).reshape(Bn, S, DSA_GROUPS, 3, DSA_HEADS, DSA_HEAD_DIM)
    slopes = _alibi_slopes(DSA_GROUPS * DSA_HEADS).reshape(DSA_GROUPS, DSA_HEADS)
    outs, maxes, dens = [], [], []
    for g, (window, dil) in enumerate(DSA_PATTERNS):
        o, m, den = _dilated_group(qkv[:, :, g, 0], qkv[:, :, g, 1], qkv[:, :, g, 2], window, dil, slopes[g])
        outs.append(o)
        maxes.append(m)
        dens.append(den)
    o = jnp.stack(outs)
    m = jnp.stack(maxes)
    den = jnp.stack(dens)
    wgt = den * jnp.exp(m - jnp.max(m, axis=0, keepdims=True))
    o = jnp.sum(wgt[..., None] * o, axis=0) / jnp.sum(wgt, axis=0)[..., None]
    return o.reshape(Bn, S, DSA_HEADS * DSA_HEAD_DIM).astype(h.dtype) @ w_out

def _mla(h, w_in, q_norm, w_qb, kv_norm, w_kvb, w_out):
    Bn, S, _ = h.shape
    lat = h @ w_in
    q_lat = lat[..., :MLA_Q_LORA]
    kv_lat = lat[..., MLA_Q_LORA:MLA_Q_LORA + MLA_KV_LORA]
    k_rope = lat[..., MLA_Q_LORA + MLA_KV_LORA:]
    q = (_rmsnorm(q_lat, q_norm) @ w_qb).reshape(Bn, S, MLA_HEADS, MLA_NOPE + MLA_ROPE)
    kv = (_rmsnorm(kv_lat, kv_norm) @ w_kvb).reshape(Bn, S, MLA_HEADS, MLA_NOPE + MLA_V)
    q_nope = q[..., :MLA_NOPE]
    q_rope = _rope(q[..., MLA_NOPE:], MLA_THETA)
    k_nope = kv[..., :MLA_NOPE]
    v32 = kv[..., MLA_NOPE:].astype(jnp.float32)
    k_rope = _rope(k_rope[:, :, None, :], MLA_THETA)[:, :, 0]
    scale = (MLA_NOPE + MLA_ROPE) ** -0.5
    nq = S // Q_BLOCK
    kpos = jnp.arange(S)

    def blocks(t):
        return t.reshape(Bn, nq, Q_BLOCK, *t.shape[2:]).swapaxes(0, 1)

    def attend(args):
        bi, qn, qr = args
        s = (jnp.einsum('bqhd,bkhd->bhqk', qn, k_nope)
             + jnp.einsum('bqhr,bkr->bhqk', qr, k_rope)).astype(jnp.float32) * scale
        qpos = bi * Q_BLOCK + jnp.arange(Q_BLOCK)
        s = jnp.where(kpos[None, :] <= qpos[:, None], s, -jnp.inf)
        pr = jax.nn.softmax(s, axis=-1)
        return jnp.einsum('bhqk,bkhd->bqhd', pr, v32)

    o = lax.map(attend, (jnp.arange(nq), blocks(q_nope), blocks(q_rope)))
    o = o.swapaxes(0, 1).reshape(Bn, S, MLA_HEADS * MLA_V)
    return o.astype(h.dtype) @ w_out

def _retention(h, w_in, gn_w, w_out):
    Bn, S, _ = h.shape
    proj = h @ w_in
    nqk = RET_HEADS * RET_QK
    nv = RET_HEADS * RET_V
    q = proj[..., :nqk].reshape(Bn, S, RET_HEADS, RET_QK)
    k = proj[..., nqk:2 * nqk].reshape(Bn, S, RET_HEADS, RET_QK)
    v = proj[..., 2 * nqk:2 * nqk + nv].reshape(Bn, S, RET_HEADS, RET_V).astype(jnp.float32)
    g = proj[..., 2 * nqk + nv:]
    q = _rope(q, RET_THETA).astype(jnp.float32)
    k = _rope(k, RET_THETA).astype(jnp.float32) * (RET_QK ** -0.5)
    log_gamma = jnp.log1p(-(2.0 ** (-5.0 - jnp.arange(RET_HEADS, dtype=jnp.float32))))
    idx = jnp.arange(RET_CHUNK, dtype=jnp.float32)
    diff = idx[:, None] - idx[None, :]
    intra = jnp.exp(jnp.where(diff >= 0, log_gamma[:, None, None] * diff, -jnp.inf))
    q_dec = jnp.exp(log_gamma[:, None] * (idx + 1.0))
    k_dec = jnp.exp(log_gamma[:, None] * (RET_CHUNK - 1.0 - idx))
    c_dec = jnp.exp(log_gamma * RET_CHUNK)
    nc = S // RET_CHUNK

    def chunks(t):
        return t.reshape(Bn, nc, RET_CHUNK, RET_HEADS, -1).transpose(1, 0, 3, 2, 4)

    def step(state, inp):
        qc, kc, vc = inp
        o = jnp.einsum('bhij,bhjv->bhiv', jnp.einsum('bhid,bhjd->bhij', qc, kc) * intra, vc)
        o = o + jnp.einsum('bhid,bhdv->bhiv', qc * q_dec[..., None], state)
        state = state * c_dec[:, None, None] + jnp.einsum('bhjd,bhjv->bhdv', kc * k_dec[..., None], vc)
        return state, o

    state0 = jnp.zeros((Bn, RET_HEADS, RET_QK, RET_V), jnp.float32)
    _, o = lax.scan(step, state0, (chunks(q), chunks(k), chunks(v)))
    o = o.transpose(1, 0, 3, 2, 4).reshape(Bn, S, RET_HEADS, RET_V)
    mu = jnp.mean(o, axis=-1, keepdims=True)
    var = jnp.mean(jnp.square(o - mu), axis=-1, keepdims=True)
    o = ((o - mu) * lax.rsqrt(var + EPS)).reshape(Bn, S, nv) * gn_w.astype(jnp.float32)
    return (jax.nn.silu(g.astype(jnp.float32)) * o).astype(h.dtype) @ w_out

def _ssd(h, w_in, conv_w, conv_b, dt_bias, A_log, D_skip, norm_w, w_out):
    Bn, S, _ = h.shape
    G, Hg, P, N, C = SSD_GROUPS, SSD_HEADS_PER_GROUP, SSD_HEAD_DIM, SSD_STATE, SSD_CHUNK
    proj = h @ w_in
    z = proj[..., :SSD_D_INNER]
    xbc = jax.nn.silu(_causal_conv(proj[..., SSD_D_INNER:SSD_D_INNER + SSD_CONV_DIM], conv_w, conv_b))
    dt = proj[..., SSD_D_INNER + SSD_CONV_DIM:]
    xs = xbc[..., :SSD_D_INNER].reshape(Bn, S, G, Hg, P).astype(jnp.float32)
    bm = xbc[..., SSD_D_INNER:SSD_D_INNER + G * N].reshape(Bn, S, G, N).astype(jnp.float32)
    cm = xbc[..., SSD_D_INNER + G * N:].reshape(Bn, S, G, N).astype(jnp.float32)
    dt = jax.nn.softplus(dt.astype(jnp.float32) + dt_bias.astype(jnp.float32)).reshape(Bn, S, G, Hg)
    a_h = -jnp.exp(A_log.astype(jnp.float32)).reshape(G, Hg)
    nc = S // C
    causal = jnp.tril(jnp.ones((C, C), dtype=bool))

    def chunks(t):
        return t.reshape(Bn, nc, C, *t.shape[2:]).swapaxes(0, 1)

    def step(state, inp):
        xc, dtc, bc, cc = inp
        a_cs = jnp.cumsum(dtc * a_h, axis=1)
        seg = a_cs[:, :, None] - a_cs[:, None, :]
        decay = jnp.exp(jnp.where(causal[None, :, :, None, None], seg, -jnp.inf))
        cb = jnp.einsum('bign,bjgn->bijg', cc, bc)
        y = jnp.einsum('bijg,bijgh,bjgh,bjghp->bighp', cb, decay, dtc, xc)
        y = y + jnp.einsum('bign,bghpn,bigh->bighp', cc, state, jnp.exp(a_cs))
        a_end = a_cs[:, -1]
        w_end = jnp.exp(a_end[:, None] - a_cs) * dtc
        state = state * jnp.exp(a_end)[..., None, None] + jnp.einsum('bjgn,bjgh,bjghp->bghpn', bc, w_end, xc)
        return state, y

    state0 = jnp.zeros((Bn, G, Hg, P, N), jnp.float32)
    _, y = lax.scan(step, state0, (chunks(xs), chunks(dt), chunks(bm), chunks(cm)))
    y = y.swapaxes(0, 1).reshape(Bn, S, G, Hg, P) + D_skip.astype(jnp.float32).reshape(G, Hg, 1) * xs
    y = y.reshape(Bn, S, SSD_D_INNER) * jax.nn.silu(z.astype(jnp.float32))
    yg = y.reshape(Bn, S, G, SSD_D_INNER // G)
    yg = yg * lax.rsqrt(jnp.mean(yg * yg, axis=-1, keepdims=True) + EPS)
    y = yg.reshape(Bn, S, SSD_D_INNER) * norm_w.astype(jnp.float32)
    return y.astype(h.dtype) @ w_out

def _hier_moe(h, w_group, b_group, w_expert, b_expert, w_gate, w_up, w_down):
    Bn, S, D = h.shape
    T = Bn * S
    xt = h.reshape(T, D)
    gp = jax.nn.softmax((xt @ w_group + b_group).astype(jnp.float32), axis=-1)
    gval, gidx = lax.top_k(gp, 1)
    el = (xt @ w_expert + b_expert).astype(jnp.float32).reshape(T, MOE_GROUPS, MOE_EXPERTS_PER_GROUP)
    el = jnp.take_along_axis(el, gidx[:, :, None], axis=1)[:, 0]
    ev, eidx = lax.top_k(el, MOE_TOPK)
    ew = jax.nn.softmax(ev, axis=-1) * gval
    expert = (gidx * MOE_EXPERTS_PER_GROUP + eidx).reshape(-1)
    tok = jnp.repeat(jnp.arange(T, dtype=jnp.int32), MOE_TOPK)
    wts = ew.reshape(-1)
    A = T * MOE_TOPK
    order = jnp.argsort(expert)
    e_s, tok_s, w_s = expert[order], tok[order], wts[order]
    counts = jax.ops.segment_sum(jnp.ones((A,), jnp.int32), expert, num_segments=MOE_EXPERTS)
    padded = (counts + MOE_BLOCK - 1) // MOE_BLOCK * MOE_BLOCK
    pad_end = jnp.cumsum(padded)
    pad_start = pad_end - padded
    start = jnp.cumsum(counts) - counts
    pos = pad_start[e_s] + (jnp.arange(A, dtype=jnp.int32) - start[e_s])
    n_blocks = -(-A // MOE_BLOCK) + MOE_EXPERTS
    P = n_blocks * MOE_BLOCK
    tok_pad = jnp.zeros((P,), jnp.int32).at[pos].set(tok_s)
    w_pad = jnp.zeros((P,), xt.dtype).at[pos].set(w_s.astype(xt.dtype))
    blk_expert = jnp.minimum(jnp.searchsorted(pad_end, jnp.arange(n_blocks) * MOE_BLOCK, side='right'),
                             MOE_EXPERTS - 1)

    def run_block(args):
        e, tk, w = args
        xb = xt[tk]
        hb = jax.nn.silu(xb @ w_gate[e]) * (xb @ w_up[e])
        return (hb @ w_down[e]) * w[:, None]

    yb = lax.map(run_block, (blk_expert, tok_pad.reshape(n_blocks, MOE_BLOCK), w_pad.reshape(n_blocks, MOE_BLOCK)))
    y = jnp.zeros_like(xt).at[tok_pad].add(yb.reshape(P, D))
    return y.reshape(Bn, S, D)

def setup_inputs(seed: int = 0) -> dict:
    key = jax.random.key(seed)
    keys = jax.random.split(key, 40)
    ks = iter([keys[i] for i in range(40)])
    f32 = jnp.float32

    def w(shape, fan_in, scale=1.0):
        return jax.random.normal(next(ks), shape, f32) * (scale * fan_in ** -0.5)

    def gain(shape):
        return 1.0 + 0.02 * jax.random.normal(next(ks), shape, f32)

    def small(shape, s=0.02):
        return s * jax.random.normal(next(ks), shape, f32)

    out_s = 0.5
    x = jax.random.normal(next(ks), (BATCH, SEQ, D_MODEL), f32)
    p = jax.random.normal(next(ks), (DEPTH, BATCH, SEQ, PLE_DIM), f32)
    norm_mix = gain((DEPTH, D_MODEL))
    norm_moe = gain((DEPTH, D_MODEL))
    norm_ple = gain((DEPTH, D_MODEL))
    norm_final = gain((D_MODEL,))
    dsa_w_in = w((D_MODEL, DSA_IN), D_MODEL)
    dsa_w_out = w((DSA_HEADS * DSA_HEAD_DIM, D_MODEL), DSA_HEADS * DSA_HEAD_DIM, out_s)
    mla_w_in = w((D_MODEL, MLA_IN), D_MODEL)
    mla_q_norm = gain((MLA_Q_LORA,))
    mla_w_qb = w((MLA_Q_LORA, MLA_HEADS * (MLA_NOPE + MLA_ROPE)), MLA_Q_LORA)
    mla_kv_norm = gain((MLA_KV_LORA,))
    mla_w_kvb = w((MLA_KV_LORA, MLA_HEADS * (MLA_NOPE + MLA_V)), MLA_KV_LORA)
    mla_w_out = w((MLA_HEADS * MLA_V, D_MODEL), MLA_HEADS * MLA_V, out_s)
    ret_w_in = w((D_MODEL, RET_IN), D_MODEL)
    ret_gn_w = gain((RET_HEADS * RET_V,))
    ret_w_out = w((RET_HEADS * RET_V, D_MODEL), RET_HEADS * RET_V, out_s)
    ssd_w_in = w((D_MODEL, SSD_IN), D_MODEL)
    ssd_conv_w = w((SSD_CONV, SSD_CONV_DIM), SSD_CONV)
    ssd_conv_b = small((SSD_CONV_DIM,))
    dt0 = jnp.exp(jax.random.uniform(next(ks), (SSD_HEADS,), f32, math.log(1e-3), math.log(1e-1)))
    ssd_dt_bias = dt0 + jnp.log(-jnp.expm1(-dt0))
    ssd_A_log = jnp.log(jax.random.uniform(next(ks), (SSD_HEADS,), f32, 1.0, 16.0))
    ssd_D = gain((SSD_HEADS,))
    ssd_norm_w = gain((SSD_D_INNER,))
    ssd_w_out = w((SSD_D_INNER, D_MODEL), SSD_D_INNER, out_s)
    moe_w_group = w((DEPTH, D_MODEL, MOE_GROUPS), D_MODEL)
    moe_b_group = small((DEPTH, MOE_GROUPS), 0.01)
    moe_w_expert = w((DEPTH, D_MODEL, MOE_EXPERTS), D_MODEL)
    moe_b_expert = small((DEPTH, MOE_EXPERTS), 0.01)
    moe_w_gate = w((DEPTH, MOE_EXPERTS, D_MODEL, MOE_D_FF), D_MODEL)
    moe_w_up = w((DEPTH, MOE_EXPERTS, D_MODEL, MOE_D_FF), D_MODEL)
    moe_w_down = w((DEPTH, MOE_EXPERTS, MOE_D_FF, D_MODEL), MOE_D_FF, out_s)
    ple_w = w((DEPTH, PLE_DIM, D_MODEL), PLE_DIM, out_s)
    ple_w_gate = w((DEPTH, D_MODEL, D_MODEL), D_MODEL)
    return {'x': x, 'p': p, 'norm_mix': norm_mix, 'norm_moe': norm_moe, 'norm_ple': norm_ple,
            'norm_final': norm_final, 'dsa_w_in': dsa_w_in, 'dsa_w_out': dsa_w_out,
            'mla_w_in': mla_w_in, 'mla_q_norm': mla_q_norm, 'mla_w_qb': mla_w_qb,
            'mla_kv_norm': mla_kv_norm, 'mla_w_kvb': mla_w_kvb, 'mla_w_out': mla_w_out,
            'ret_w_in': ret_w_in, 'ret_gn_w': ret_gn_w, 'ret_w_out': ret_w_out,
            'ssd_w_in': ssd_w_in, 'ssd_conv_w': ssd_conv_w, 'ssd_conv_b': ssd_conv_b,
            'ssd_dt_bias': ssd_dt_bias, 'ssd_A_log': ssd_A_log, 'ssd_D': ssd_D,
            'ssd_norm_w': ssd_norm_w, 'ssd_w_out': ssd_w_out,
            'moe_w_group': moe_w_group, 'moe_b_group': moe_b_group,
            'moe_w_expert': moe_w_expert, 'moe_b_expert': moe_b_expert,
            'moe_w_gate': moe_w_gate, 'moe_w_up': moe_w_up, 'moe_w_down': moe_w_down,
            'ple_w': ple_w, 'ple_w_gate': ple_w_gate}

def reference(x, p, norm_mix, norm_moe, norm_ple, norm_final, dsa_w_in, dsa_w_out,
              mla_w_in, mla_q_norm, mla_w_qb, mla_kv_norm, mla_w_kvb, mla_w_out,
              ret_w_in, ret_gn_w, ret_w_out,
              ssd_w_in, ssd_conv_w, ssd_conv_b, ssd_dt_bias, ssd_A_log, ssd_D, ssd_norm_w, ssd_w_out,
              moe_w_group, moe_b_group, moe_w_expert, moe_b_expert, moe_w_gate, moe_w_up, moe_w_down,
              ple_w, ple_w_gate):
    for i in range(DEPTH):
        h = _rmsnorm(x, norm_mix[i])
        kind = i % N_MIXERS
        if kind == 0:
            y = _dilated_attention(h, dsa_w_in, dsa_w_out)
        elif kind == 1:
            y = _mla(h, mla_w_in, mla_q_norm, mla_w_qb, mla_kv_norm, mla_w_kvb, mla_w_out)
        elif kind == 2:
            y = _retention(h, ret_w_in, ret_gn_w, ret_w_out)
        else:
            y = _ssd(h, ssd_w_in, ssd_conv_w, ssd_conv_b, ssd_dt_bias, ssd_A_log, ssd_D, ssd_norm_w, ssd_w_out)
        x = x + y
        h = _rmsnorm(x, norm_moe[i])
        x = x + _hier_moe(h, moe_w_group[i], moe_b_group[i], moe_w_expert[i], moe_b_expert[i],
                          moe_w_gate[i], moe_w_up[i], moe_w_down[i])
        gate = jax.nn.sigmoid(_rmsnorm(x, norm_ple[i]) @ ple_w_gate[i])
        x = x + (p[i] @ ple_w[i]) * gate
    return _rmsnorm(x, norm_final)


_drawn_inputs = setup_inputs


def setup_inputs(seed=0):
    import zlib

    import numpy as np

    out = dict(_drawn_inputs(seed))
    spreads = {}
    factors = {'norm_mix': 4.673,
     'norm_moe': 2.81,
     'norm_ple': 8.0,
     'norm_final': 2.696,
     'mla_q_norm': 8.0,
     'mla_kv_norm': 8.0,
     'moe_b_group': 4.962,
     'moe_b_expert': 5.177}
    for name, (base, spread) in spreads.items():
        noise = np.random.default_rng([zlib.crc32(name.encode()), seed]).standard_normal(out[name].shape)
        drawn = base * np.exp(spread * noise) if base else spread * noise
        out[name] = jnp.asarray(drawn.astype(out[name].dtype))
    for name, factor in factors.items():
        out[name] = (out[name] * factor).astype(out[name].dtype)
    return out
```

```python
from contextlib import ExitStack

import numpy as np

import concourse.bass as bass
from concourse import mybir

F32 = mybir.dt.float32
I32 = mybir.dt.int32
U32 = mybir.dt.uint32
ALU = mybir.AluOpType
ACT = mybir.ActivationFunctionType
AX = mybir.AxisListType

P = 128
T = 256
TC = T // P
D = 1024
KD = D // P
EPS = 1e-6
BIG = 1.0e30

GROUPS, HEADS, DH = 3, 8, 128
PATTERNS = ((128, 1), (512, 4), (2048, 16))
DSA_SCALE = DH ** -0.5
MH, NOPE, ROPE, MV = 16, 64, 32, 64
QK = NOPE + ROPE
QL, KVL = 256, 128
MLA_IN = QL + KVL + ROPE
MLA_SCALE = QK ** -0.5
HALF = ROPE // 2
NG, EPG, NE, FF = 4, 8, 32, 512
NR = NG + NE
CW = 32
CAP = 32
GE = P // CW
NGRP = NE // GE
NSLOT = (NGRP + 1) * P
BODY = 8
ITERS = NE // BODY
PLE = 256

RING = 8
SLOT = 4096
DSLOTS = 6


class Tiles:
    DSA = 0
    DSA_OUT = DSA + HEADS * GROUPS
    MOE = [DSA_OUT + 2, 0]
    PLE = [MOE[0] + 3 * NE, 0]
    MLA = PLE[0] + 3
    MLA_OUT = MLA + 3
    MOE[1] = MLA_OUT + 2
    PLE[1] = MOE[1] + 3 * NE
    N = PLE[1] + 3

    @staticmethod
    def slot(t):
        return t % DSLOTS if t < Tiles.DSA_OUT else (t - Tiles.DSA_OUT + DSLOTS) % RING

    @staticmethod
    def fills(t):
        if t < Tiles.DSA_OUT:
            return t // DSLOTS + 1
        first = Tiles.DSA_OUT + (Tiles.slot(t) - DSLOTS) % RING
        return (t - first) // RING + 1

    @staticmethod
    def before(t):
        if t < Tiles.DSA_OUT:
            return t - DSLOTS if t >= DSLOTS else None
        if t < Tiles.DSA_OUT + RING:
            s = Tiles.slot(t)
            return Tiles.DSA_OUT - DSLOTS + s if s < DSLOTS else None
        return t - RING

    @staticmethod
    def used(t):
        if t < Tiles.DSA_OUT:
            return "v_ready", t + 1
        if t < Tiles.MOE[0]:
            return "mix_out", TC
        if Tiles.MLA <= t < Tiles.MLA_OUT:
            return ("lat_ready", "q_ready", "mv_ready")[t - Tiles.MLA], TC
        if Tiles.MLA_OUT <= t < Tiles.MOE[1]:
            return "mix_out", 2 * TC
        l = 1 if t >= Tiles.MOE[1] else 0
        if t < Tiles.PLE[l]:
            n = t - Tiles.MOE[l]
            return ("gate_ready", "up_ready", "down_ready")[n % 3], NE * l + n // 3 + 1
        return ("pw_ready" if t == Tiles.PLE[l] else "pg_ready"), 2 * TC * (l + 1)


C_ID, C_LOW, C_CAUSAL = 0, 128, 256
C_SLOPE = C_CAUSAL + 384
C_SLOT = C_SLOPE + GROUPS * HEADS
C_EID = C_SLOT + NGRP
C_GID = C_EID + NE
C_COS = C_GID + NE
C_SIN = C_COS + TC * HALF
C_END = C_SIN + TC * HALF
W_GAIN = 0
W_QG = 6 * KD
W_KVG = W_QG + QL // P
W_END = W_KVG + 1


def shape_constants():
    c = np.zeros((P, C_END), np.float32)
    p = np.arange(P)
    c[:, C_ID:C_ID + P] = np.eye(P)
    c[:, C_LOW:C_LOW + P] = p[:, None] < p[None, :]
    tri = np.where(p[None, :] <= p[:, None], 0.0, -BIG)
    c[:, C_CAUSAL:C_CAUSAL + P] = tri
    c[:, C_CAUSAL + 2 * P:C_CAUSAL + 3 * P] = tri
    n = GROUPS * HEADS
    slopes = 2.0 ** (-8.0 * np.arange(1, n + 1) / n)
    c[:, C_SLOPE:C_SLOPE + n] = (slopes / DSA_SCALE).reshape(GROUPS, HEADS).T.reshape(1, n)
    c[:, C_SLOT:C_SLOT + NGRP] = p[:, None] + P * np.arange(NGRP)[None, :]
    c[:, C_EID:C_EID + NE] = np.arange(NE)
    c[:, C_GID:C_GID + NE] = np.arange(NE) // EPG
    inv = 10000.0 ** (-np.arange(HALF, dtype=np.float32) / HALF)
    ang = (np.arange(T, dtype=np.float32)[:, None] * inv.astype(np.float32)).reshape(TC, P, HALF).transpose(1, 0, 2)
    c[:, C_COS:C_COS + TC * HALF] = np.cos(ang).reshape(P, -1)
    c[:, C_SIN:C_SIN + TC * HALF] = np.sin(ang).reshape(P, -1)
    return c


def distance_table():
    d = np.zeros((P, GROUPS, 2 * P), np.float32)
    delta = np.arange(P)[:, None] + P - np.arange(2 * P)[None, :]
    for g, (window, dil) in enumerate(PATTERNS):
        seen = (delta >= 0) & (delta <= window) & (delta % dil == 0)
        d[:, g] = np.where(seen, -delta, -BIG)
    return d.reshape(P, -1)


class Link:

    def __init__(self, eng, sem):
        self.eng, self.sem, self.n, self.base = eng, sem, 0, 0

    def __call__(self, ins):
        self.n += 1
        ins.then_inc(self.sem, 1)
        self.eng.wait_ge(self.sem, self.base + self.n)

    def enter(self, it, per):
        self.base, self.before, self.per = it * per, self.n, per

    def leave(self, passes):
        assert self.n - self.before == self.per, (self.n - self.before, self.per)
        self.base, self.n = 0, self.before + passes * self.per


def build(nc, x, out, consts, distances, gains, routers, rows, p_t, dsa_w_in, dsa_w_out, mla_w_in, mla_w_qb,
          mla_w_kvb, mla_w_out, moe_w_gate, moe_w_up, moe_w_down, ple_w, ple_w_gate):
    ctx = ExitStack()
    with ctx:
        def sb(name, shape, dt=F32):
            return ctx.enter_context(nc.sbuf_tensor(name, shape, dt))

        sems = {}

        def S(name):
            if name not in sems:
                sems[name] = ctx.enter_context(nc.semaphore(name))
            return sems[name]

        ring = sb("ring", [P, RING, SLOT])
        x_sb = sb("x_sb", [P, TC, D])
        hs = sb("hs", [P, TC, KD, P])
        hT = sb("hT", [P, KD, T])
        cst = sb("cst", [P, C_END])
        wts = sb("wts", [P, W_END])
        small = sb("small", [P, 256])
        small_u = sb("small_u", [P, 64], U32)
        flag = sb("flag", [1, 2], I32)
        SCR = 13056
        scr = sb("scr", [P, SCR])
        ps = ctx.enter_context(nc.psum_tensor("ps", [P, 8, 512], F32))

        ident = cst[:, C_ID:C_ID + P]

        def part(ap, at, *dims):
            n = 1
            for d in dims:
                n *= d
            v = ap[:, at:at + n]
            if len(dims) == 2:
                v = v.rearrange("p (a b) -> p a b", b=dims[1])
            elif len(dims) == 3:
                v = v.rearrange("p (a b c) -> p a b c", b=dims[1], c=dims[2])
            return v

        def scratch(at, *dims):
            return part(scr, at, *dims)

        def tile(t, k, n, at=0):
            return ring[:, Tiles.slot(t), :][:, at:at + k * n].rearrange("p (k n) -> p k n", n=n)

        landed = [S(f"landed_{s}") for s in range(RING)]
        landed_dsa = [S(f"landed_dsa_{s}") for s in range(DSLOTS)]

        def wait_tile(eng, t, more=0):
            eng.wait_ge(landed[Tiles.slot(t)], 16 * (Tiles.fills(t) + more))

        a_qk = [scratch(0, GROUPS, 512), scratch(1536, GROUPS, 512)]
        a_v = [scratch(3072, GROUPS, T), scratch(3840, GROUPS, T)]
        a_s0 = scratch(4608, GROUPS, P)
        a_s1 = scratch(4992, GROUPS, 2 * P)
        a_pT = scratch(5760, 9, P)
        a_o = scratch(6912, HEADS, T)
        a_dist = scratch(8960, GROUPS, 2 * P)
        m_qT = scratch(0, MH, T)
        m_kT = scratch(4096, MH, T)
        m_q = scratch(8192, TC, MH * QK)
        m_s = [scratch(8192, 2, 384), scratch(8960, 2, 384)]
        m_pT = [scratch(9728, 2, 384), scratch(10496, 2, 384)]
        m_lat = scratch(11264, TC, MLA_IN)
        m_ln = scratch(12096, TC, QL + KVL)
        m_kr = scratch(12864, TC, QK)
        hs_flat = hs[:, :, :, :].rearrange("p c k t -> p (c k t)")
        m_qlT = part(hs_flat, 0, QL // P, T)
        m_kvT = hs_flat[:, 512:512 + T]
        m_rope = [scratch(11264 + T * j, MH, HALF) for j in range(4)]
        m_o = part(hs_flat, 0, KD, T)
        m_v = hT[:, :, :].rearrange("p k t -> p (k t)").rearrange("p (c n) -> p c n", c=TC)
        e_oneh = scratch(0, TC, NSLOT)
        e_xT = [scratch(2304, KD, P), scratch(3328, KD, P)]
        e_wide = scratch(0, KD, 512)
        e_wide_d = scratch(0, FF // P, D)
        e_y = scratch(4352, D)
        e_iota = scratch(5376, NSLOT)
        e_rows = scratch(6528, 4, T)
        e_sc = scratch(7552, T)
        e_sc2 = scratch(9224, T)
        e_sil = scratch(7808, P)
        e_h = scratch(7936, P)
        e_hT = scratch(8064, P)
        r_lg = scratch(8192, TC, NR)
        r_em = scratch(8264, TC, NE)
        r_m0 = scratch(8328, TC, NE)
        r_m1 = scratch(8392, TC, NE)
        r_m = scratch(8456, TC, NE)
        r_wo = scratch(8520, TC, NE)
        r_junk = scratch(8584, P)
        e_pT = scratch(8712, PLE // P, T)
        p_gate = scratch(9224, TC, D)
        o_sil = scratch(9224, TC, 512)
        o_hT = scratch(10248, 4, P)
        r_w = scratch(10760, KD, NR)
        r_b = scratch(11048, NR)
        f_gain = scratch(11272, D)

        ss = small[:, 0:2]
        rstd = small[:, 2:4]
        a_mx, a_nmx, a_den = small[:, 4:6], small[:, 6:8], small[:, 8:10]
        m_ss = part(small, 12, 2, TC)
        m_rs = part(small, 16, 2, TC)
        m_mx = part(small, 20, 2, 2)
        m_nmx = part(small, 24, 2, 2)
        m_den = [part(small, 28, 2, 2), part(small, 32, 2, 2)]
        gp8 = part(small, 40, TC, 8)
        gm8 = part(small, 56, TC, 8)
        ev8 = part(small, 72, TC, 8)
        ngm = small[:, 88:90]
        gsum = small[:, 90:92]
        eg4 = small[:, 92:96]
        gif = small[:, 96:98]
        ef = part(small, 98, TC, 2)
        dif = small[:, 102:104]
        rr = part(small, 104, TC, 2)
        fits = part(small, 108, TC, 2)
        wgt = part(small, 112, TC, 2)
        wov = part(small, 116, TC, 2)
        slot_of = part(small, 120, TC, 2)
        cmax = small[:, 124:125]
        w_in = part(small, 128, TC, 2)
        den1 = small[:, 132:134]
        ones = small[:, 136:137]
        m_t = [part(small, 140, TC, HALF), part(small, 172, TC, HALF)]
        gi8 = part(small_u, 0, TC, 8)
        ei8 = part(small_u, 16, TC, 8)

        def bank(b, *dims):
            v = ps[:, b, :]
            return v if not dims else part(v, 0, *dims)

        block = ctx.enter_context(nc.Block())

        dsa_in_v = dsa_w_in.rearrange("(p k) (g w n) -> g p k w n", k=KD, g=GROUPS, w=3)
        kp = lambda w, n: w.rearrange("(p k) (n j) -> n p k j", k=KD, j=n)
        dsa_out_v = dsa_w_out.rearrange("(k p) (n j) -> n p k j", p=P, j=512)
        mla_out_v = mla_w_out.rearrange("(k p) (n j) -> n p k j", p=P, j=512)

        @block.sync
        def _(sp):
            def wait_free(t, more=0):
                if Tiles.before(t) is not None:
                    sem, value = Tiles.used(Tiles.before(t))
                    sp.wait_ge(S(sem), value + more)

            def load(t, src, k, n):
                wait_free(t)
                sp.dma_start(tile(t, k, n), src).then_inc(landed[Tiles.slot(t)], 16)

            def load_dsa(t, h, g, more=0):
                wait_free(t, more)
                for w in range(3):
                    sp.dma_start(tile(t, KD, 3 * DH)[:, :, w * DH:(w + 1) * DH],
                                 dsa_in_v[g][:, :, w, bass.ds(DH * h, DH)]
                                 ).then_inc(landed_dsa[Tiles.slot(t)], 16)

            sp.dma_start(x_sb[:, :, :], x.rearrange("b (c p) d -> p (b c) d", p=P)).then_inc(S("x_in"), 16)
            for t in range(DSLOTS):
                load_dsa(t, t // GROUPS, t % GROUPS)
            for n in range(2):
                load(Tiles.DSA_OUT + n, dsa_out_v[n], KD, 512)
            with sp.Fori(0, HEADS // 2 - 1) as it:
                for j in range(DSLOTS):
                    load_dsa(DSLOTS + j, 2 * it + 2 + j // GROUPS, j % GROUPS, more=DSLOTS * it)

            def expert_weights(l, e, j):
                one = (moe_w_gate, moe_w_up, moe_w_down)[j][l, bass.ds(e, 1), :, :]
                if j == 2:
                    return one.rearrange("e (j p) n -> p (e j) n", p=P)
                return one.rearrange("e (p k) n -> p (e k) n", k=KD)

            def load_expert_tile(l, n, it=0):
                t, j = Tiles.MOE[l] + n, n % 3
                wait_free(t, BODY * it)
                k, width = (FF // P, D) if j == 2 else (KD, FF)
                sp.dma_start(tile(t, k, width), expert_weights(l, n // 3 + BODY * it, j)
                             ).then_inc(landed[Tiles.slot(t)], 16)

            def load_experts(l):
                for n in range(RING):
                    load_expert_tile(l, n)
                with sp.Fori(0, ITERS - 1) as it:
                    for n in range(RING, RING + 3 * BODY):
                        load_expert_tile(l, n, it)
                for n in range(RING + 3 * BODY * (ITERS - 1), 3 * NE):
                    load_expert_tile(l, n)

            def load_ple(l):
                load(Tiles.PLE[l], ple_w[l].rearrange("(k p) n -> p k n", p=P), PLE // P, D)
                for n in range(2):
                    load(Tiles.PLE[l] + 1 + n, kp(ple_w_gate[l], 512)[n], KD, 512)

            def load_overflow(l):
                sp.wait_ge(S("flag_ready"), l + 1)
                count = sp.value_load(flag[0:1, l:l + 1], min_val=0, max_val=T)
                with sp.If(count > CAP):
                    sp.wait_ge(S("scattered"), (NGRP + 1) * (l + 1))
                    sp.sem_inc(S(f"o_down{l}"), 1)
                    with sp.Fori(0, NE) as e:
                        for j in range(3):
                            if j == 0:
                                sp.wait_ge(S(f"o_down{l}"), e + 1)
                            else:
                                sp.wait_ge(S(f"o_gate{l}" if j == 1 else f"o_up{l}"), TC * e + TC)
                            sp.dma_start(e_wide_d if j == 2 else e_wide, expert_weights(l, e, j)
                                         ).then_inc(S(f"o_landed{l}"), 16)

            load_experts(0)
            load_overflow(0)
            load_ple(0)
            load(Tiles.MLA, mla_w_in.rearrange("(p k) n -> p k n", k=KD), KD, MLA_IN)
            load(Tiles.MLA + 1, mla_w_qb.rearrange("(k p) n -> p k n", p=P), QL // P, MH * QK)
            load(Tiles.MLA + 2, mla_w_kvb.rearrange("(k p) n -> p k n", p=P), 1, MH * (NOPE + MV))
            for n in range(2):
                load(Tiles.MLA_OUT + n, mla_out_v[n], KD, 512)
            load_experts(1)
            load_overflow(1)
            load_ple(1)
            for c in range(TC):
                sp.wait_ge(S("final_ready"), c + 1)
                sp.dma_start(out[0, c * P:(c + 1) * P, :], x_sb[:, c, :]).then_inc(S("stored"), 16)
            sp.wait_ge(S("stored"), 16 * TC)

        @block.gpsimd
        def _(pool):
            pool.dma_start(wts[:, :], gains).then_inc(S("wts_in"), 16)
            pool.dma_start(cst[:, :], consts).then_inc(S("cst_in"), 16)
            pool.dma_start(a_dist, distances.rearrange("p (g n) -> p g n", g=GROUPS)).then_inc(S("dist_in"), 16)
            pool.memset(gp8, -BIG).then_inc(S("fills"), 1)
            pool.memset(ones, 1.0).then_inc(S("fills"), 1)
            for l in range(2):
                pool.wait_ge(S("mixed"), 2 * (l + 1))
                pool.dma_start(r_w, routers[l].rearrange("p (k n) -> p k n", k=KD)).then_inc(S("router_in"), 16)
                pool.dma_start(r_b, rows[0:1, NR * l:NR * l + NR].partition_broadcast(P)).then_inc(S("bias_in"), 16)
                pool.iota(e_iota, [[1, NSLOT]], base=0, channel_multiplier=0,
                          allow_small_or_imprecise_dtypes=True).then_inc(S("iota_ready"), 1)
                pool.dma_start(e_pT, p_t[l].rearrange("(k p) t -> p k t", p=P)).then_inc(S("pT_in"), 16)
                if l == 1:
                    pool.dma_start(f_gain, rows[0:1, 2 * NR:2 * NR + D].partition_broadcast(P)
                                   ).then_inc(S("f_gain_in"), 16)

        X_READY = {
            0: [("x_in", 16), ("x_in", 16)],
            1: [("mixed", 1), ("mixed", 2)],
            2: [("y_taken_d", 1), ("y_taken_a", 1)],
            3: [("ple_added", 1), ("ple_added", 2)],
            4: [("mixed", 3), ("mixed", 4)],
            5: [("y_taken_d", 2), ("y_taken_a", 2)],
            6: [("ple_added", 3), ("ple_added", 4)],
        }

        @block.scalar
        def _(act):
            link = Link(act, S("act_link"))

            def norm(i):
                s, v = X_READY[i][1]
                act.wait_ge(S(s), v)
                if i == 4:
                    act.wait_ge(S("mix_out"), 2 * TC)
                act.activation(hs[:, 1, :, :].rearrange("p k t -> p (k t)"), x_sb[:, 1, :], ACT.Square,
                               accum_out=ss[:, 1:2]).then_inc(S("sq_a"), 1)
                act.wait_ge(S("var_ready"), i + 1)
                act.activation(ss, ss, ACT.Sqrt).then_inc(S("root_ready"), 1)
                act.wait_ge(S("rstd_ready"), i + 1)
                if i < 6:
                    act.activation(hs[:, 1, :, :], x_sb[:, 1, :].rearrange("p (t k) -> p k t", k=KD), ACT.Copy,
                                   scale=rstd[:, 1:2]).then_inc(S("hs_a"), 1)

            def copy_qk(h, g, buf, first=False):
                act.wait_ge(S("qk_ready"), GROUPS * h + g + 1)
                if g == 0 and not first:
                    act.wait_ge(S("s_ready"), h - 1)
                act.copy(a_qk[buf][:, g, :], bank(0)).then_inc(S("qk_copied"), 1)

            def attend(h):
                act.wait_ge(S("nmx_ready"), h + 1)
                s0 = a_s0.rearrange("p g n -> p (g n)")
                s1 = a_s1.rearrange("p g n -> p (g n)")
                act.activation(s0, s0, ACT.Exp, bias=a_nmx[:, 0:1], scale=DSA_SCALE,
                               accum_out=a_den[:, 0:1]).then_inc(S("e_ready"), 1)
                act.activation(s1, s1, ACT.Exp, bias=a_nmx[:, 1:2], scale=DSA_SCALE,
                               accum_out=a_den[:, 1:2]).then_inc(S("e_ready"), 1)

            def copy_pT(h):
                for b in (0, 2):
                    act.wait_ge(S("pT_ready"), 3 * h + b + 1)
                    act.copy(a_pT[:, 3 * b:3 * b + 3, :], bank(5, 4, P)[:, 0:3, :]).then_inc(S("pT_copied_a"), 1)

            def copy_o(h):
                act.wait_ge(S("o_ready"), h + 1)
                act.copy(a_o[:, bass.ds(h, 1), :].rearrange("p h t -> p (h t)"),
                         bank(7)[:, 0:T]).then_inc(S("o_copied"), 1)

            def step(h_att, h_proj, buf, first=False):
                copy_qk(h_proj, 0, buf, first)
                attend(h_att)
                copy_pT(h_att)
                copy_qk(h_proj, 1, buf)
                copy_o(h_att)
                copy_qk(h_proj, 2, buf)

            norm(0)
            for g in range(GROUPS):
                copy_qk(0, g, 0, first=True)
            step(0, 1, 1, first=True)
            with act.Fori(0, HEADS // 2 - 1) as it:
                step(2 * it + 1, 2 * it + 2, 0)
                step(2 * it + 2, 2 * it + 3, 1)
            attend(HEADS - 1)
            copy_pT(HEADS - 1)
            copy_o(HEADS - 1)

            def experts(l):
                for c in range(TC):
                    act.wait_ge(S("ngm_ready"), 2 * l + c + 1)
                    act.activation(eg4, r_lg[:, c, 0:NG], ACT.Exp, bias=ngm[:, c:c + 1],
                                   accum_out=gsum[:, c:c + 1]).then_inc(S("gsum_ready"), 1)
                    act.wait_ge(S("gsum_ready"), 2 * l + c + 1)
                act.wait_ge(S("dif_ready"), l + 1)
                act.activation(dif, dif, ACT.Exp).then_inc(S("dexp_ready"), 1)
                with act.Fori(0, ITERS) as it:
                    for i in range(BODY):
                        e = NE * l + BODY * it + i
                        act.wait_ge(S("gate_ready"), e + 1)
                        act.activation(e_sil, bank(4)[:, 0:P], ACT.Silu).then_inc(S("silu_ready"), 1)
                        act.wait_ge(S("down_ready"), e + 1)
                        if i % GE == 0:
                            grp = (NGRP + 1) * l + (BODY // GE) * it + i // GE
                            act.wait_ge(S("scattered"), grp + 1)
                        for q in (2, 3):
                            ins = act.copy(e_y[CW * (i % GE):CW * (i % GE) + CW, T * q:T * q + T],
                                           bank(6)[CW * q:CW * q + CW, 0:T])
                        ins.then_inc(S("y_copied_a"), 1)
                act.wait_ge(S("flag_ready"), l + 1)
                count = act.value_load(flag[0:1, l:l + 1], min_val=0, max_val=T)
                with act.If(count > CAP):
                    with act.Fori(0, NE) as e:
                        for c in range(TC):
                            act.wait_ge(S(f"o_gate{l}"), TC * e + c + 1)
                            act.activation(o_sil[:, c, :], bank(4 + c), ACT.Silu).then_inc(S(f"o_silu{l}"), 1)
                    act.wait_ge(S(f"o_down{l}"), NE + 1)
                act.wait_ge(S("scattered"), (NGRP + 1) * (l + 1))
                act.copy(x_sb[:, 1, :], ps[:, 2:4, :].rearrange("p a b -> p (a b)")).then_inc(S("y_taken_a"), 1)

            def ple(l):
                norm(3 * l + 2)
                for c in range(TC):
                    for n in range(2):
                        act.wait_ge(S("pg_ready"), 4 * l + 2 * c + n + 1)
                        act.activation(p_gate[:, c, 512 * n:512 * n + 512], bank(4 + 2 * c + n),
                                       ACT.Sigmoid).then_inc(S("sig_ready"), 1)

            norm(1)
            experts(0)
            ple(0)

            norm(3)
            for c in range(TC):
                act.wait_ge(S("lat_ready"), c + 1)
                act.copy(m_lat[:, c, :], bank(c)[:, 0:MLA_IN]).then_inc(S("lat_copied"), 1)
                act.wait_ge(S("lat_copied"), c + 1)
                for j, (a, b) in enumerate(((0, QL), (QL, QL + KVL))):
                    act.activation(m_ln[:, c, a:b], m_lat[:, c, a:b], ACT.Square,
                                   accum_out=m_ss[:, j, c:c + 1]).then_inc(S("lat_sq"), 1)
            act.wait_ge(S("lat_var"), 2)
            act.activation(m_rs, m_ss, ACT.Sqrt).then_inc(S("lat_root"), 1)
            act.wait_ge(S("q_ready"), 2)
            act.copy(m_q[:, 1, :], ps[:, 0:3, :].rearrange("p a b -> p (a b)")).then_inc(S("q_copied_a"), 1)
            for j in range(MH // 2):
                act.wait_ge(S("k_ready"), j + 1)
                act.copy(m_kT[0:NOPE, 2 * j:2 * j + 2, :], bank(3 + 4 * (j % 2), 2, T)[0:NOPE, :, :]).then_inc(S("k_copied"), 1)
            for j in range(MH // 2):
                if j % 2 == 1:
                    act.wait_ge(S("qT_ready"), j + 1)
                    act.copy(m_qT[0:QK, 2 * j:2 * j + 2, :], bank(6, 2, T)[0:QK, :, :]).then_inc(S("qT_copied_a"), 1)

            def m_exps(j):
                act.wait_ge(S("m_nmx"), j + 1)
                for h2 in range(2):
                    for c, (a, b) in enumerate(((0, P), (P, 3 * P))):
                        ins = act.activation(m_s[j % 2][:, h2, a:b], m_s[j % 2][:, h2, a:b], ACT.Exp,
                                             bias=m_nmx[:, c, h2:h2 + 1], scale=MLA_SCALE,
                                             accum_out=m_den[j % 2][:, c, h2:h2 + 1])
                ins.then_inc(S("m_exp"), 1)

            m_exps(0)
            for j in range(MH // 2):
                if j + 1 < MH // 2:
                    m_exps(j + 1)
                act.wait_ge(S("m_pT_ready"), j + 1)
                act.copy(m_pT[j % 2][:, 1, :], bank(3)[:, 0:384]).then_inc(S("m_pT_copied_a"), 1)
                act.wait_ge(S("m_o_ready"), j + 1)
                act.copy(m_o[:, j, :], bank(4)[:, 0:T]).then_inc(S("m_o_copied"), 1)

            norm(4)
            experts(1)
            ple(1)
            norm(6)

        @block.vector
        def _(dve):
            link = Link(dve, S("dve_link"))

            def norm(i):
                s, v = X_READY[i][0]
                dve.wait_ge(S(s), v)
                if i == 4:
                    dve.wait_ge(S("mix_out"), 2 * TC)
                if i == 0:
                    dve.wait_ge(S("wts_in"), 16)
                dve.tensor_tensor_reduce(out=hs[:, 0, :, :].rearrange("p k t -> p (k t)"), in0=x_sb[:, 0, :],
                                         in1=x_sb[:, 0, :], scale=1.0, scalar=0.0, op0=ALU.mult, op1=ALU.add,
                                         accum_out=ss[:, 0:1]).then_inc(S("sq_d"), 1)
                dve.wait_ge(S("sq_d"), i + 1)
                dve.wait_ge(S("sq_a"), i + 1)
                dve.tensor_scalar(ss, ss, 1.0 / D, EPS, ALU.mult, ALU.add).then_inc(S("var_ready"), 1)
                dve.wait_ge(S("root_ready"), i + 1)
                dve.reciprocal(rstd, ss).then_inc(S("rstd_ready"), 1)
                dve.wait_ge(S("rstd_ready"), i + 1)
                if i == 6:
                    return
                dve.tensor_scalar(hs[:, 0, :, :], x_sb[:, 0, :].rearrange("p (t k) -> p k t", k=KD),
                                  rstd[:, 0:1], None, ALU.mult).then_inc(S("hs_d"), 1)
                gain = part(wts, W_GAIN + i * KD, KD)
                for c in range(TC):
                    for b in range(2):
                        dve.wait_ge(S("hT_turned"), 4 * i + 2 * c + b + 1)
                        dve.tensor_tensor(hT[:, 4 * b:4 * b + 4, c * P:(c + 1) * P], bank(4 + 2 * c + b, 4, P),
                                          gain[:, 4 * b:4 * b + 4].unsqueeze(2).to_broadcast([P, 4, P]),
                                          ALU.mult).then_inc(S("hT_ready"), 1)

            def copy_v(h, g, buf, first=False):
                dve.wait_ge(S("v_ready"), GROUPS * h + g + 1)
                if g == 0 and not first:
                    dve.wait_ge(S("o_ready"), h - 1)
                dve.tensor_copy(a_v[buf][:, g, :], bank(1)[:, 0:T]).then_inc(S("v_copied"), 1)

            def softmax_head(h):
                dve.wait_ge(S("s_ready"), h + 1)
                for g in range(GROUPS):
                    slope = cst[:, bass.ds(C_SLOPE + GROUPS * h + g, 1)]
                    src = bank(3)[:, 2 * P * g:2 * P * g + 2 * P] if g < 2 else bank(4)[:, 0:2 * P]
                    dve.scalar_tensor_tensor(out=a_s0[:, g, :], in0=a_dist[:, g, P:2 * P], scalar=slope,
                                             in1=bank(2)[:, P * g:P * g + P], op0=ALU.mult, op1=ALU.add)
                    ins = dve.scalar_tensor_tensor(out=a_s1[:, g, :], in0=a_dist[:, g, :], scalar=slope,
                                                   in1=src, op0=ALU.mult, op1=ALU.add)
                ins.then_inc(S("s_taken"), 1)
                dve.wait_ge(S("s_taken"), h + 1)
                dve.tensor_reduce(a_mx[:, 0:1], a_s0.rearrange("p g n -> p (g n)"), AX.X, ALU.max)
                link(dve.tensor_reduce(a_mx[:, 1:2], a_s1.rearrange("p g n -> p (g n)"), AX.X, ALU.max))
                dve.tensor_scalar(a_nmx, a_mx, -DSA_SCALE, None, ALU.mult).then_inc(S("nmx_ready"), 1)

            def softmax_tail(h):
                dve.wait_ge(S("e_ready"), 2 * h + 2)
                link(dve.reciprocal(a_den, a_den))
                s0 = a_s0.rearrange("p g n -> p (g n)")
                s1 = a_s1.rearrange("p g n -> p (g n)")
                dve.tensor_scalar(s0, s0, a_den[:, 0:1], None, ALU.mult).then_inc(S("p_ready"), 1)
                dve.tensor_scalar(s1, s1, a_den[:, 1:2], None, ALU.mult).then_inc(S("p_ready"), 1)

            def copy_pT(h):
                dve.wait_ge(S("pT_ready"), 3 * h + 2)
                dve.tensor_copy(a_pT[:, 3:6, :], bank(6, 4, P)[:, 0:3, :]).then_inc(S("pT_copied_d"), 1)

            def step(h_att, h_proj, buf, first=False):
                softmax_head(h_att)
                softmax_tail(h_att)
                copy_v(h_proj, 0, buf, first)
                copy_pT(h_att)
                copy_v(h_proj, 1, buf)
                copy_v(h_proj, 2, buf)

            norm(0)
            dve.wait_ge(S("cst_in"), 16)
            dve.wait_ge(S("dist_in"), 16)
            for g in range(GROUPS):
                copy_v(0, g, 0, first=True)
            step(0, 1, 1, first=True)
            with dve.Fori(0, HEADS // 2 - 1) as it:
                link.enter(it, 4)
                step(2 * it + 1, 2 * it + 2, 0)
                step(2 * it + 2, 2 * it + 3, 1)
            link.leave(HEADS // 2 - 1)
            softmax_head(HEADS - 1)
            softmax_tail(HEADS - 1)
            copy_pT(HEADS - 1)

            def add_mixed(l):
                for c in range(TC):
                    dve.wait_ge(S("mix_out"), TC * l + c + 1)
                    dve.tensor_tensor(x_sb[:, c, :], x_sb[:, c, :],
                                      ps[:, 2 * c:2 * c + 2, :].rearrange("p a b -> p (a b)"),
                                      ALU.add).then_inc(S("mixed"), 1)
                    dve.wait_ge(S("mixed"), TC * l + c + 1)

            def route(l):
                dve.wait_ge(S("bias_in"), 16 * (l + 1))
                dve.wait_ge(S("fills"), 2)
                dve.wait_ge(S("logits_ready"), l + 1)
                bias_l = r_b.unsqueeze(1).to_broadcast([P, TC, NR])
                link(dve.tensor_tensor(r_lg, bank(0)[:, 0:TC * NR].rearrange("p (c n) -> p c n", n=NR), bias_l, ALU.add))
                link(dve.tensor_copy(gp8[:, :, 0:NG], r_lg[:, :, 0:NG]))
                for c in range(TC):
                    link(dve.max(gm8[:, c, :], gp8[:, c, :]))
                    dve.tensor_scalar(ngm[:, c:c + 1], gm8[:, c, 0:1], -1.0, None, ALU.mult).then_inc(S("ngm_ready"), 1)
                    link(dve.max_index(gi8[:, c, :], gm8[:, c, :], gp8[:, c, :]))
                link(dve.tensor_copy(gif, gi8[:, :, 0]))
                for c in range(TC):
                    link(dve.tensor_scalar(r_em[:, c, :], cst[:, C_GID:C_GID + NE], gif[:, c:c + 1], BIG,
                                           ALU.is_equal, ALU.mult))
                    link(dve.scalar_tensor_tensor(out=r_em[:, c, :], in0=r_em[:, c, :], scalar=-BIG,
                                                  in1=r_lg[:, c, NG:NR], op0=ALU.add, op1=ALU.add))
                    link(dve.max(ev8[:, c, :], r_em[:, c, :]))
                    link(dve.max_index(ei8[:, c, :], ev8[:, c, :], r_em[:, c, :]))
                dve.tensor_tensor(dif, ev8[:, :, 1], ev8[:, :, 0], ALU.subtract).then_inc(S("dif_ready"), 1)
                link(dve.tensor_copy(ef, ei8[:, :, 0:2]))
                for c in range(TC):
                    for a, m in enumerate((r_m0, r_m1)):
                        link(dve.tensor_scalar(m[:, c, :], cst[:, C_EID:C_EID + NE], ef[:, c, a:a + 1], None,
                                               ALU.is_equal))
                dve.tensor_tensor(r_m, r_m0, r_m1, ALU.add).then_inc(S("choice_ready"), 1)
                dve.wait_ge(S("dexp_ready"), l + 1)
                dve.wait_ge(S("gsum_ready"), 2 * l + 2)
                link(dve.scalar_tensor_tensor(out=den1, in0=dif, scalar=1.0, in1=gsum, op0=ALU.add, op1=ALU.mult))
                link(dve.reciprocal(w_in[:, :, 0], den1))
                link(dve.tensor_tensor(w_in[:, :, 1], w_in[:, :, 0], dif, ALU.mult))
                dve.wait_ge(S("ranks_ready"), l + 1)
                for c in range(TC):
                    for a, m in enumerate((r_m0, r_m1)):
                        link(dve.tensor_tensor_reduce(out=r_junk[:, 0:NE], in0=bank(1)[:, NE * c:NE * c + NE],
                                                      in1=m[:, c, :], scale=1.0, scalar=0.0, op0=ALU.mult,
                                                      op1=ALU.add, accum_out=rr[:, c, a:a + 1]))
                link(dve.tensor_reduce(cmax[0:1, :], bank(1)[0:1, 2 * NE:3 * NE], AX.X, ALU.max))
                dve.tensor_copy(flag[0:1, l:l + 1], cmax[0:1, :]).then_inc(S("flag_ready"), 1)
                link(dve.tensor_scalar(fits, rr, float(CAP), None, ALU.is_lt))
                link(dve.scalar_tensor_tensor(out=slot_of, in0=ef, scalar=float(CW), in1=rr, op0=ALU.mult, op1=ALU.add))
                link(dve.scalar_tensor_tensor(out=slot_of, in0=slot_of, scalar=1.0, in1=fits, op0=ALU.add, op1=ALU.mult))
                link(dve.tensor_scalar(slot_of, slot_of, -1.0, None, ALU.add))
                link(dve.tensor_tensor(wgt, w_in, fits, ALU.mult))
                dve.tensor_tensor(wov, w_in, wgt, ALU.subtract).then_inc(S("slots_ready"), 1)
                dve.wait_ge(S("slots_ready"), l + 1)
                dve.wait_ge(S("iota_ready"), l + 1)
                for c in range(TC):
                    link(dve.tensor_scalar(e_oneh[:, c, :], e_iota, slot_of[:, c, 0:1], None, ALU.is_equal))
                    dve.scalar_tensor_tensor(out=e_oneh[:, c, :], in0=e_iota, scalar=slot_of[:, c, 1:2],
                                             in1=e_oneh[:, c, :], op0=ALU.is_equal,
                                             op1=ALU.add).then_inc(S("oneh_ready"), 1)
                dve.wait_ge(S("rows_ready"), l + 1)
                dve.tensor_copy(e_rows.rearrange("p a t -> p (a t)"),
                                ps[:, 2:4, :].rearrange("p a b -> p (a b)")).then_inc(S("y_free"), 1)
                dve.wait_ge(S("y_free"), l + 1)
                for c in range(TC):
                    link(dve.tensor_scalar(r_wo[:, c, :], r_m0[:, c, :], wov[:, c, 0:1], None, ALU.mult))
                    link(dve.scalar_tensor_tensor(out=r_wo[:, c, :], in0=r_m1[:, c, :], scalar=wov[:, c, 1:2],
                                                  in1=r_wo[:, c, :], op0=ALU.mult, op1=ALU.add))

            def take_gathered(l, grp, half, buf):
                gain = part(wts, W_GAIN + (3 * l + 1) * KD, KD)
                dve.wait_ge(S("gathered"), (2 * (NGRP + 1)) * l + 2 * grp + half + 1)
                dve.tensor_tensor(e_xT[buf][:, 4 * half:4 * half + 4, :], bank(7, 4, P),
                                  gain[:, 4 * half:4 * half + 4].unsqueeze(2).to_broadcast([P, 4, P]),
                                  ALU.mult).then_inc(S("xT_ready"), 1)

            def experts(l):
                route(l)
                for half in range(2):
                    take_gathered(l, 0, half, 0)
                with dve.Fori(0, ITERS) as it:
                    link.enter(it, 2 * BODY // GE)
                    for i in range(BODY):
                        e = NE * l + BODY * it + i
                        grp = (BODY // GE) * it + i // GE
                        dve.wait_ge(S("silu_ready"), e + 1)
                        dve.wait_ge(S("up_ready"), e + 1)
                        dve.tensor_tensor(e_h, e_sil, bank(5)[:, 0:P], ALU.mult).then_inc(S("h_ready"), 1)
                        dve.wait_ge(S("hT_e"), e + 1)
                        dve.tensor_copy(e_hT, bank(5)[:, P:2 * P]).then_inc(S("hT_copied"), 1)
                        dve.wait_ge(S("down_ready"), e + 1)
                        if i % GE == 0:
                            dve.wait_ge(S("scattered"), (NGRP + 1) * l + grp + 1)
                        for q in (0, 1):
                            ins = dve.tensor_copy(e_y[CW * (i % GE):CW * (i % GE) + CW, T * q:T * q + T],
                                                  bank(6)[CW * q:CW * q + CW, 0:T])
                        ins.then_inc(S("y_copied_d"), 1)
                        if i % GE in (1, 2):
                            take_gathered(l, grp + 1, i % GE - 1, (i // GE + 1) % 2)
                        if i % GE == 2:
                            slot_id = cst[:, bass.ds(C_SLOT + grp, 1)]
                            link(dve.scalar_tensor_tensor(out=e_sc2, in0=e_rows[:, 0, :], scalar=slot_id,
                                                          in1=e_rows[:, 2, :], op0=ALU.is_equal, op1=ALU.mult))
                            link(dve.scalar_tensor_tensor(out=e_sc, in0=e_rows[:, 1, :], scalar=slot_id,
                                                          in1=e_rows[:, 3, :], op0=ALU.is_equal, op1=ALU.mult))
                            dve.tensor_tensor(e_sc, e_sc, e_sc2, ALU.add).then_inc(S("sc_ready"), 1)
                link.leave(ITERS)
                count = dve.value_load(flag[0:1, l:l + 1], min_val=0, max_val=T)
                with dve.If(count > CAP):
                    with dve.Fori(0, NE) as e:
                        for c in range(TC):
                            dve.wait_ge(S(f"o_silu{l}"), TC * e + c + 1)
                            dve.wait_ge(S(f"o_up{l}"), TC * e + c + 1)
                            dve.scalar_tensor_tensor(out=o_sil[:, c, :], in0=o_sil[:, c, :],
                                                     scalar=r_wo[:, c, bass.ds(e, 1)], in1=bank(6 + c),
                                                     op0=ALU.mult, op1=ALU.mult).then_inc(S(f"o_h{l}"), 1)
                            dve.wait_ge(S(f"o_turned{l}"), TC * e + c + 1)
                            dve.tensor_copy(o_hT, bank(4, 4, P)).then_inc(S(f"o_hT{l}"), 1)
                    dve.wait_ge(S(f"o_down{l}"), NE + 1)
                dve.wait_ge(S("scattered"), (NGRP + 1) * (l + 1))
                dve.tensor_copy(x_sb[:, 0, :], ps[:, 0:2, :].rearrange("p a b -> p (a b)")).then_inc(S("y_taken_d"), 1)

            def ple(l):
                norm(3 * l + 2)
                for c in range(TC):
                    for n in range(2):
                        dve.wait_ge(S("sig_ready"), 4 * l + 2 * c + n + 1)
                        dve.wait_ge(S("pw_ready"), 4 * l + 2 * c + n + 1)
                        g = p_gate[:, c, 512 * n:512 * n + 512]
                        link(dve.tensor_tensor(g, g, bank(2 * c + n), ALU.mult))
                    dve.tensor_tensor(x_sb[:, c, :], x_sb[:, c, :], p_gate[:, c, :], ALU.add).then_inc(S("ple_added"), 1)
                    dve.wait_ge(S("ple_added"), 2 * l + c + 1)

            add_mixed(0)
            norm(1)
            experts(0)
            ple(0)

            norm(3)
            dve.wait_ge(S("lat_sq"), 4)
            link(dve.tensor_scalar(m_ss[:, 0, :], m_ss[:, 0, :], 1.0 / QL, EPS, ALU.mult, ALU.add))
            dve.tensor_scalar(m_ss[:, 1, :], m_ss[:, 1, :], 1.0 / KVL, EPS, ALU.mult, ALU.add).then_inc(S("lat_var"), 2)
            dve.wait_ge(S("lat_root"), 1)
            link(dve.reciprocal(m_rs, m_rs))
            for c in range(TC):
                for j, (a, b) in enumerate(((0, QL), (QL, QL + KVL))):
                    dve.tensor_scalar(m_ln[:, c, a:b], m_lat[:, c, a:b], m_rs[:, j, c:c + 1], None,
                                      ALU.mult).then_inc(S("ln_ready"), 1)
            cos = part(cst, C_COS, TC, HALF)
            sin = part(cst, C_SIN, TC, HALF)
            link(dve.memset(m_kr[:, :, 0:NOPE], 0.0))
            k1, k2 = m_lat[:, :, QL + KVL:QL + KVL + HALF], m_lat[:, :, QL + KVL + HALF:MLA_IN]
            for o, (u, v, op) in enumerate((((k1, cos), (k2, sin), ALU.subtract), ((k1, sin), (k2, cos), ALU.add))):
                link(dve.tensor_tensor(m_t[0], u[0], u[1], ALU.mult))
                link(dve.tensor_tensor(m_t[1], v[0], v[1], ALU.mult))
                ins = dve.tensor_tensor(m_kr[:, :, NOPE + HALF * o:NOPE + HALF * o + HALF], m_t[0], m_t[1], op)
                if o == 0:
                    link(ins)
            ins.then_inc(S("kr_ready"), 1)
            dve.wait_ge(S("lnT"), 1)
            qg, kvg = part(wts, W_QG, QL // P), wts[:, W_KVG:W_KVG + 1]
            dve.tensor_tensor(m_qlT, bank(2, 2, T), qg.unsqueeze(2).to_broadcast([P, 2, T]),
                              ALU.mult).then_inc(S("lnT_copied"), 1)
            dve.tensor_scalar(m_kvT, bank(3)[:, 0:T], kvg, None, ALU.mult).then_inc(S("lnT_copied"), 1)
            dve.tensor_copy(m_kT[NOPE:QK, :, :],
                            bank(3)[NOPE:QK, T:2 * T].unsqueeze(1).to_broadcast([ROPE, MH, T])
                            ).then_inc(S("lnT_copied"), 1)
            dve.wait_ge(S("q_ready"), 1)
            dve.tensor_copy(m_q[:, 0, :], ps[:, 4:7, :].rearrange("p a b -> p (a b)")).then_inc(S("q_copied_d"), 1)
            dve.wait_ge(S("q_copied_d"), 1)
            for c in range(TC):
                if c == 1:
                    dve.wait_ge(S("q_copied_a"), 1)
                qh = m_q[:, c, :].rearrange("p (h n) -> p h n", n=QK)
                q1, q2 = qh[:, :, NOPE:NOPE + HALF], qh[:, :, NOPE + HALF:QK]
                cb = cos[:, c, :].unsqueeze(1).to_broadcast([P, MH, HALF])
                sn = sin[:, c, :].unsqueeze(1).to_broadcast([P, MH, HALF])
                t = m_rope
                link(dve.tensor_tensor(t[0], q1, cb, ALU.mult))
                link(dve.tensor_tensor(t[1], q2, sn, ALU.mult))
                link(dve.tensor_tensor(t[2], q1, sn, ALU.mult))
                link(dve.tensor_tensor(t[3], q2, cb, ALU.mult))
                dve.tensor_tensor(q1, t[0], t[1], ALU.subtract).then_inc(S("q_rot"), 1)
                dve.tensor_tensor(q2, t[2], t[3], ALU.add).then_inc(S("q_rot"), 1)
                dve.wait_ge(S("q_rot"), 2 * (c + 1))
            for c in range(TC):
                dve.wait_ge(S("mv_ready"), c + 1)
                b = 4 if c == 0 else 0
                dve.tensor_copy(m_v[:, c, :], ps[:, b:b + 2, :].rearrange("p a b -> p (a b)")).then_inc(S("mv_copied"), 1)
            for j in range(0, MH // 2, 2):
                dve.wait_ge(S("qT_ready"), j + 1)
                dve.tensor_copy(m_qT[0:QK, 2 * j:2 * j + 2, :], bank(2, 2, T)[0:QK, :, :]).then_inc(S("qT_copied_d"), 1)
            causal = cst[:, C_CAUSAL:C_CAUSAL + 384].unsqueeze(1).to_broadcast([P, 2, 384])

            def m_scores(j):
                dve.wait_ge(S("m_s_ready"), j + 1)
                src = ps[:, 0:2, 0:384] if j % 2 == 0 else ps[:, 5:7, 0:384]
                link(dve.tensor_tensor(m_s[j % 2], src, causal, ALU.add))
                link(dve.tensor_reduce(m_mx[:, 0, :], m_s[j % 2][:, :, 0:P], AX.X, ALU.max))
                link(dve.tensor_reduce(m_mx[:, 1, :], m_s[j % 2][:, :, P:3 * P], AX.X, ALU.max))
                if j >= 1:
                    dve.wait_ge(S("m_exp"), j)
                dve.tensor_scalar(m_nmx, m_mx, -MLA_SCALE, None, ALU.mult).then_inc(S("m_nmx"), 1)

            m_scores(0)
            for j in range(MH // 2):
                if j + 1 < MH // 2:
                    m_scores(j + 1)
                dve.wait_ge(S("m_exp"), j + 1)
                link(dve.reciprocal(m_den[j % 2], m_den[j % 2]))
                for h2 in range(2):
                    for c, (a, b) in enumerate(((0, P), (P, 3 * P))):
                        ins = dve.tensor_scalar(m_s[j % 2][:, h2, a:b], m_s[j % 2][:, h2, a:b],
                                                m_den[j % 2][:, c, h2:h2 + 1], None, ALU.mult)
                ins.then_inc(S("m_p"), 1)
                dve.wait_ge(S("m_pT_ready"), j + 1)
                dve.tensor_copy(m_pT[j % 2][:, 0, :], bank(2)[:, 0:384]).then_inc(S("m_pT_copied_d"), 1)

            add_mixed(1)
            norm(4)
            experts(1)
            ple(1)
            norm(6)
            dve.wait_ge(S("f_gain_in"), 16)
            for c in range(TC):
                dve.scalar_tensor_tensor(out=x_sb[:, c, :], in0=x_sb[:, c, :], scalar=rstd[:, c:c + 1], in1=f_gain,
                                         op0=ALU.mult, op1=ALU.mult).then_inc(S("final_ready"), 1)

        @block.tensor
        def _(pe):
            def norm(i):
                for c in range(TC):
                    pe.wait_ge(S("hs_d" if c == 0 else "hs_a"), (i if c == 0 else i) + 1)
                    if i == 0 and c == 0:
                        pe.wait_ge(S("cst_in"), 16)
                    for b in range(2):
                        for k in range(4):
                            mm = pe.transpose(bank(4 + 2 * c + b)[:, k * P:(k + 1) * P], hs[:, c, 4 * b + k, :], ident)
                        mm.then_inc(S("hT_turned"), 1)

            def project(t, h, g, buf, more=0, first=False):
                pe.wait_ge(landed_dsa[Tiles.slot(t)], 3 * 16 * (Tiles.fills(t) + more))
                w = tile(t, KD, 3 * DH)
                n = GROUPS * h + g
                if not first:
                    pe.wait_ge(S("qk_copied"), n)
                for which in range(2):
                    for k in range(KD):
                        mm = pe.matmul(bank(0)[:, which * T:which * T + T], w[:, k, which * DH:(which + 1) * DH],
                                       hT[:, k, :], start=(k == 0), stop=(k == KD - 1))
                mm.then_inc(S("qk_ready"), 1)
                if not first:
                    pe.wait_ge(S("v_copied"), n)
                for c in range(TC):
                    for k in range(KD):
                        mm = pe.matmul(bank(1)[:, c * P:(c + 1) * P], hT[:, k, c * P:(c + 1) * P],
                                       w[:, k, 2 * DH:3 * DH], start=(k == 0), stop=(k == KD - 1))
                mm.then_inc(S("v_ready"), 1)

            def scores(h, buf, first=False):
                pe.wait_ge(S("qk_copied"), GROUPS * h + GROUPS)
                if not first:
                    pe.wait_ge(S("s_taken"), h)
                for g in range(GROUPS):
                    q, k = a_qk[buf][:, g, 0:T], a_qk[buf][:, g, T:2 * T]
                    dst = bank(3)[:, 2 * P * g:2 * P * g + 2 * P] if g < 2 else bank(4)[:, 0:2 * P]
                    pe.matmul(bank(2)[:, P * g:P * g + P], q[:, 0:P], k[:, 0:P], start=True, stop=True)
                    mm = pe.matmul(dst, q[:, P:T], k, start=True, stop=True)
                mm.then_inc(S("s_ready"), 1)

            def turn(h, first=False):
                pe.wait_ge(S("p_ready"), 2 * h + 2)
                for b in range(3):
                    if b == 2:
                        pe.wait_ge(S("pT_copied_a"), 2 * h + 1)
                    elif not first:
                        pe.wait_ge(S("pT_copied_a" if b == 0 else "pT_copied_d"), 2 * h if b == 0 else h)
                    for g in range(GROUPS):
                        src = a_s0[:, g, :] if b == 0 else a_s1[:, g, (b - 1) * P:b * P]
                        mm = pe.transpose(bank(6 if b == 1 else 5)[:, g * P:(g + 1) * P], src, ident)
                    mm.then_inc(S("pT_ready"), 1)

            def weigh(h, buf, first=False):
                pe.wait_ge(S("v_copied"), GROUPS * h + GROUPS)
                pe.wait_ge(S("pT_copied_a"), 2 * h + 2)
                pe.wait_ge(S("pT_copied_d"), h + 1)
                if not first:
                    pe.wait_ge(S("o_copied"), h)
                for g in range(GROUPS):
                    pe.matmul(bank(7)[:, 0:P], a_v[buf][:, g, 0:P], a_pT[:, g, :], start=(g == 0), stop=(g == GROUPS - 1))
                for g in range(GROUPS):
                    for kc in range(2):
                        mm = pe.matmul(bank(7)[:, P:2 * P], a_v[buf][:, g, kc * P:(kc + 1) * P],
                                       a_pT[:, 3 + 3 * kc + g, :], start=(g == 0 and kc == 0),
                                       stop=(g == GROUPS - 1 and kc == 1))
                mm.then_inc(S("o_ready"), 1)

            norm(0)
            pe.wait_ge(S("hT_ready"), 4)

            def step(h_att, h_proj, buf, t, more=0, first=False):
                scores(h_att, 1 - buf, first)
                project(t, h_proj, 0, buf, more)
                turn(h_att, first)
                project(t + 1, h_proj, 1, buf, more)
                weigh(h_att, 1 - buf, first)
                project(t + 2, h_proj, 2, buf, more)

            for g in range(GROUPS):
                project(g, 0, g, 0, first=(g == 0))
            step(0, 1, 1, 3, first=True)
            with pe.Fori(0, HEADS // 2 - 1) as it:
                step(2 * it + 1, 2 * it + 2, 0, DSLOTS, it)
                step(2 * it + 2, 2 * it + 3, 1, DSLOTS + 3, it)
            scores(HEADS - 1, 1)
            turn(HEADS - 1)
            weigh(HEADS - 1, 1)
            pe.wait_ge(S("o_copied"), HEADS)

            def mix_out(l, t, o):
                for c in range(TC):
                    for n in range(2):
                        if c == 0:
                            wait_tile(pe, t + n)
                        for k in range(KD):
                            mm = pe.matmul(bank(2 * c + n), o[:, k, c * P:(c + 1) * P], tile(t + n, KD, 512)[:, k, :],
                                           start=(k == 0), stop=(k == KD - 1))
                    mm.then_inc(S("mix_out"), 1)

            def gather(l, grp, half):
                pe.wait_ge(S("oneh_ready"), TC * (l + 1))
                for k in range(4):
                    for c in range(TC):
                        mm = pe.matmul(bank(7)[:, k * P:(k + 1) * P], hs[:, c, 4 * half + k, :],
                                       e_oneh[:, c, bass.ds(P * grp, P)], start=(c == 0), stop=(c == TC - 1))
                mm.then_inc(S("gathered"), 1)

            def experts(l):
                pe.wait_ge(S("hT_ready"), 4 * (3 * l + 2))
                pe.wait_ge(S("router_in"), 16 * (l + 1))
                for c in range(TC):
                    for k in range(KD):
                        mm = pe.matmul(bank(0)[:, c * NR:(c + 1) * NR], hT[:, k, c * P:(c + 1) * P], r_w[:, k, :],
                                       start=(k == 0), stop=(k == KD - 1))
                mm.then_inc(S("logits_ready"), 1)
                pe.wait_ge(S("choice_ready"), l + 1)
                low = cst[:, C_LOW:C_LOW + P]
                all_ones = ones.to_broadcast([P, P])
                pe.matmul(bank(1)[:, 0:NE], low, r_m[:, 0, :], start=True, stop=True)
                pe.matmul(bank(1)[:, NE:2 * NE], all_ones, r_m[:, 0, :], start=True, stop=False)
                pe.matmul(bank(1)[:, NE:2 * NE], low, r_m[:, 1, :], start=False, stop=True)
                pe.matmul(bank(1)[:, 2 * NE:3 * NE], all_ones, r_m[:, 0, :], start=True, stop=False)
                pe.matmul(bank(1)[:, 2 * NE:3 * NE], all_ones, r_m[:, 1, :], start=False,
                          stop=True).then_inc(S("ranks_ready"), 1)
                pe.wait_ge(S("slots_ready"), l + 1)
                for a in range(4):
                    for c in range(TC):
                        col = (slot_of, wgt)[a // 2][:, c, a % 2:a % 2 + 1]
                        mm = pe.matmul(bank(2 + a // 2)[:, (a % 2) * T + c * P:(a % 2) * T + (c + 1) * P],
                                       col.to_broadcast([P, P]), ident, start=True, stop=True)
                mm.then_inc(S("rows_ready"), 1)
                gather(l, 0, 0)
                pe.wait_ge(S("xT_ready"), 2 * (NGRP + 1) * l + 1)
                gather(l, 0, 1)
                pe.wait_ge(S("y_free"), l + 1)
                for c in range(TC):
                    for n in range(2):
                        mm = pe.matmul(bank(2 * c + n), ident, x_sb[:, c, 512 * n:512 * n + 512], start=True,
                                       stop=True)
                mm.then_inc(S("scattered"), 1)
                base = Tiles.MOE[l]
                xt0 = 2 * (NGRP + 1) * l
                with pe.Fori(0, ITERS) as it:
                    for i in range(BODY):
                        e = NE * l + BODY * it + i
                        grp = (BODY // GE) * it + i // GE
                        t = base + 3 * i
                        more = (3 * BODY // RING) * it
                        xT = e_xT[(i // GE) % 2][:, :, CW * (i % GE):CW * (i % GE) + CW]
                        if i % GE == 0:
                            pe.wait_ge(S("xT_ready"), xt0 + 2 * grp + 2)
                        for j, b in ((0, 4), (1, 5)):
                            wait_tile(pe, t + j, more)
                            for k in range(KD):
                                for q in range(4):
                                    mm = pe.matmul(bank(b)[CW * q:CW * q + CW, 0:P], xT[:, k, :],
                                                   tile(t + j, KD, FF)[:, k, P * q:P * q + P],
                                                   start=(k == 0), stop=(k == KD - 1))
                            mm.then_inc(S("gate_ready" if j == 0 else "up_ready"), 1)
                        pe.wait_ge(S("h_ready"), e + 1)
                        pe.transpose(bank(5)[:, P:2 * P], e_h, ident).then_inc(S("hT_e"), 1)
                        pe.wait_ge(S("hT_copied"), e + 1)
                        wait_tile(pe, t + 2, more)
                        for j in range(FF // P):
                            for q in range(4):
                                mm = pe.matmul(bank(6)[CW * q:CW * q + CW, 0:T], e_hT[:, CW * j:CW * j + CW],
                                               tile(t + 2, FF // P, D)[:, j, T * q:T * q + T],
                                               start=(j == 0), stop=(j == FF // P - 1))
                        mm.then_inc(S("down_ready"), 1)
                        if i % GE in (1, 2):
                            pe.wait_ge(S("xT_ready"), xt0 + 2 * grp + 2 + (i % GE - 1))
                            gather(l, grp + 1, i % GE - 1)
                        pe.wait_ge(S("y_copied_d"), e + 1)
                        pe.wait_ge(S("y_copied_a"), e + 1)
                        if i % GE == GE - 1:
                            pe.wait_ge(S("sc_ready"), NGRP * l + grp + 1)
                            for c in range(TC):
                                for n in range(2):
                                    mm = pe.matmul(bank(2 * c + n), e_sc[:, c * P:(c + 1) * P],
                                                   e_y[:, 512 * n:512 * n + 512], start=False, stop=True,
                                                   skip_group_check=True)
                            mm.then_inc(S("scattered"), 1)

                pe.wait_ge(S("flag_ready"), l + 1)
                count = pe.value_load(flag[0:1, l:l + 1], min_val=0, max_val=T)
                with pe.If(count > CAP):
                    with pe.Fori(0, NE) as e:
                        for j, b in ((0, 4), (1, 6)):
                            pe.wait_ge(S(f"o_landed{l}"), 16 * (3 * e + j + 1))
                            for c in range(TC):
                                for k in range(KD):
                                    mm = pe.matmul(bank(b + c), hT[:, k, c * P:(c + 1) * P], e_wide[:, k, :],
                                                   start=(k == 0), stop=(k == KD - 1))
                                mm.then_inc(S(f"o_gate{l}" if j == 0 else f"o_up{l}"), 1)
                        pe.wait_ge(S(f"o_landed{l}"), 16 * (3 * e + 3))
                        for c in range(TC):
                            pe.wait_ge(S(f"o_h{l}"), TC * e + c + 1)
                            for j in range(FF // P):
                                mm = pe.transpose(bank(4)[:, j * P:(j + 1) * P], o_sil[:, c, j * P:(j + 1) * P], ident)
                            mm.then_inc(S(f"o_turned{l}"), 1)
                            pe.wait_ge(S(f"o_hT{l}"), TC * e + c + 1)
                            for n in range(2):
                                for j in range(FF // P):
                                    mm = pe.matmul(bank(2 * c + n), o_hT[:, j, :], e_wide_d[:, j, 512 * n:512 * n + 512],
                                                   start=False, stop=True, skip_group_check=True)
                        mm.then_inc(S(f"o_down{l}"), 1)

            def ple(l):
                pe.wait_ge(S("y_taken_d"), l + 1)
                pe.wait_ge(S("y_taken_a"), l + 1)
                pe.wait_ge(S("pT_in"), 16 * (l + 1))
                wait_tile(pe, Tiles.PLE[l])
                for c in range(TC):
                    for n in range(2):
                        for k in range(PLE // P):
                            mm = pe.matmul(bank(2 * c + n), e_pT[:, k, c * P:(c + 1) * P],
                                           tile(Tiles.PLE[l], PLE // P, D)[:, k, 512 * n:512 * n + 512],
                                           start=(k == 0), stop=(k == PLE // P - 1))
                        mm.then_inc(S("pw_ready"), 1)
                norm(3 * l + 2)
                pe.wait_ge(S("hT_ready"), 4 * (3 * l + 3))
                for c in range(TC):
                    for n in range(2):
                        if c == 0:
                            wait_tile(pe, Tiles.PLE[l] + 1 + n)
                        for k in range(KD):
                            mm = pe.matmul(bank(4 + 2 * c + n), hT[:, k, c * P:(c + 1) * P],
                                           tile(Tiles.PLE[l] + 1 + n, KD, 512)[:, k, :],
                                           start=(k == 0), stop=(k == KD - 1))
                        mm.then_inc(S("pg_ready"), 1)

            mix_out(0, Tiles.DSA_OUT, a_o)
            norm(1)
            experts(0)
            ple(0)

            pe.wait_ge(S("ple_added"), TC)
            norm(3)
            pe.wait_ge(S("hT_ready"), 16)
            wait_tile(pe, Tiles.MLA)
            for c in range(TC):
                for k in range(KD):
                    mm = pe.matmul(bank(c)[:, 0:MLA_IN], hT[:, k, c * P:(c + 1) * P],
                                   tile(Tiles.MLA, KD, MLA_IN)[:, k, :], start=(k == 0), stop=(k == KD - 1))
                mm.then_inc(S("lat_ready"), 1)
            pe.wait_ge(S("ln_ready"), 4)
            for c in range(TC):
                for k in range(QL // P):
                    pe.transpose(bank(2, 2, T)[:, k, c * P:(c + 1) * P], m_ln[:, c, k * P:(k + 1) * P], ident)
                pe.transpose(bank(3)[:, c * P:(c + 1) * P], m_ln[:, c, QL:QL + KVL], ident)
            pe.wait_ge(S("kr_ready"), 1)
            for c in range(TC):
                mm = pe.transpose(bank(3)[0:QK, T + c * P:T + (c + 1) * P], m_kr[:, c, :], ident)
            mm.then_inc(S("lnT"), 1)
            pe.wait_ge(S("lnT_copied"), 3)
            wait_tile(pe, Tiles.MLA + 1)
            for c in range(TC):
                b = 4 if c == 0 else 0
                for n in range(3):
                    for k in range(QL // P):
                        mm = pe.matmul(bank(b + n), m_qlT[:, k, c * P:(c + 1) * P],
                                       tile(Tiles.MLA + 1, QL // P, MH * QK)[:, k, 512 * n:512 * n + 512],
                                       start=(k == 0), stop=(k == QL // P - 1))
                mm.then_inc(S("q_ready"), 1)
            wait_tile(pe, Tiles.MLA + 2)
            kvb = tile(Tiles.MLA + 2, MH, NOPE + MV)
            for j in range(MH // 2):
                if j >= 2:
                    pe.wait_ge(S("k_copied"), j - 1)
                for h2 in range(2):
                    mm = pe.matmul(bank(3 + 4 * (j % 2), 2, T)[0:NOPE, h2, :], kvb[:, 2 * j + h2, 0:NOPE], m_kvT,
                                   start=True, stop=True)
                mm.then_inc(S("k_ready"), 1)
            for c in range(TC):
                b = 4 if c == 0 else 0
                pe.wait_ge(S("q_copied_d" if c == 0 else "q_copied_a"), 1)
                for n in range(2):
                    mm = pe.matmul(bank(b + n), m_kvT[:, c * P:(c + 1) * P],
                                   kvb[:, 8 * n:8 * n + 8, NOPE:NOPE + MV], start=True, stop=True)
                mm.then_inc(S("mv_ready"), 1)
            pe.wait_ge(S("q_rot"), 4)
            for j in range(MH // 2):
                if j >= 2:
                    pe.wait_ge(S("qT_copied_a" if j % 2 else "qT_copied_d"), j // 2)
                for h2 in range(2):
                    for c in range(TC):
                        mm = pe.transpose(bank(6 if j % 2 else 2, 2, T)[0:QK, h2, c * P:(c + 1) * P],
                                          m_q[:, c, QK * (2 * j + h2):QK * (2 * j + h2) + QK], ident)
                mm.then_inc(S("qT_ready"), 1)
            pe.wait_ge(S("qT_copied_a"), MH // 4)
            pe.wait_ge(S("qT_copied_d"), MH // 4)
            pe.wait_ge(S("k_copied"), MH // 2)
            pe.wait_ge(S("mv_copied"), TC)

            def m_scores(j):
                for h2 in range(2):
                    q, k = m_qT[0:QK, 2 * j + h2, :], m_kT[0:QK, 2 * j + h2, :]
                    b = (5 if j % 2 else 0) + h2
                    pe.matmul(bank(b)[:, 0:P], q[:, 0:P], k[:, 0:P], start=True, stop=True)
                    mm = pe.matmul(bank(b)[:, P:3 * P], q[:, P:T], k, start=True, stop=True)
                mm.then_inc(S("m_s_ready"), 1)

            m_scores(0)
            for j in range(MH // 2):
                if j + 1 < MH // 2:
                    m_scores(j + 1)
                pe.wait_ge(S("m_p"), j + 1)
                if j >= 1:
                    pe.wait_ge(S("m_pT_copied_a"), j)
                    pe.wait_ge(S("m_pT_copied_d"), j)
                for h2 in range(2):
                    for b in range(3):
                        mm = pe.transpose(bank(2 + h2)[:, b * P:(b + 1) * P], m_s[j % 2][:, h2, b * P:(b + 1) * P], ident)
                mm.then_inc(S("m_pT_ready"), 1)
                pe.wait_ge(S("m_pT_copied_a"), j + 1)
                pe.wait_ge(S("m_pT_copied_d"), j + 1)
                if j >= 1:
                    pe.wait_ge(S("m_o_copied"), j)
                for h2 in range(2):
                    dst = bank(4)[MV * h2:MV * h2 + MV, :]
                    v = [m_v[:, c, MV * (2 * j + h2):MV * (2 * j + h2) + MV] for c in range(TC)]
                    pT = m_pT[j % 2][:, h2, :]
                    pe.matmul(dst[:, 0:P], v[0], pT[:, 0:P], start=True, stop=True)
                    pe.matmul(dst[:, P:T], v[0], pT[:, P:2 * P], start=True, stop=False)
                    mm = pe.matmul(dst[:, P:T], v[1], pT[:, 2 * P:3 * P], start=False, stop=True)
                mm.then_inc(S("m_o_ready"), 1)
            pe.wait_ge(S("m_o_copied"), MH // 2)
            mix_out(1, Tiles.MLA_OUT, m_o)
            norm(4)
            experts(1)
            ple(1)


def kernel(**inputs):
    import concourse.bacc as bacc
    from concourse.bass_utils import run_bass_kernel_spmd

    a = {n: np.ascontiguousarray(v) for n, v in inputs.items()}
    gains = [a[n][l] for l in range(2) for n in ("norm_mix", "norm_moe", "norm_ple")]
    routers = [np.concatenate([a["moe_w_group"][l], a["moe_w_expert"][l]], axis=1) for l in range(2)]
    arrays = {
        "x": a["x"],
        "consts": shape_constants(),
        "distances": distance_table(),
        "gains": np.ascontiguousarray(np.concatenate(
            [g.reshape(P, KD) for g in gains]
            + [a["mla_q_norm"].reshape(-1, P).T, a["mla_kv_norm"].reshape(-1, P).T], axis=1)),
        "routers": np.stack([r.reshape(P, KD * NR) for r in routers]),
        "rows": np.concatenate([a["moe_b_group"][0], a["moe_b_expert"][0], a["moe_b_group"][1],
                                a["moe_b_expert"][1], a["norm_final"]]).reshape(1, -1),
        "p_t": np.ascontiguousarray(a["p"][:, 0].transpose(0, 2, 1)),
    }
    for n in ("dsa_w_in", "dsa_w_out", "mla_w_in", "mla_w_qb", "mla_w_kvb", "mla_w_out", "moe_w_gate", "moe_w_up",
              "moe_w_down", "ple_w", "ple_w_gate"):
        arrays[n] = a[n]
    nc = bacc.Bacc("TRN2", target_bir_lowering=False, num_devices=1)
    args = {n: nc.dram_tensor(n, v.shape, mybir.dt.from_np(v.dtype), kind="ExternalInput").ap()
            for n, v in arrays.items()}
    args["out"] = nc.dram_tensor("out", a["x"].shape, F32, kind="ExternalOutput").ap()
    build(nc, **args)
    r = run_bass_kernel_spmd(nc, [arrays], core_ids=[0])
    return r.results[0]["out"]
```

```python
from contextlib import ExitStack

import numpy as np

import concourse.bass as bass
from concourse import mybir

F32 = mybir.dt.float32
F32R = mybir.dt.float32r
I32 = mybir.dt.int32
U32 = mybir.dt.uint32
ALU = mybir.AluOpType
ACT = mybir.ActivationFunctionType
AX = mybir.AxisListType

P = 128
T = 256
TC = T // P
D = 1024
KD = D // P
EPS = 1e-6
BIG = 1.0e30

GROUPS, HEADS, DH = 3, 8, 128
PATTERNS = ((128, 1), (512, 4), (2048, 16))
DSA_SCALE = DH ** -0.5
MH, NOPE, ROPE, MV = 16, 64, 32, 64
QK = NOPE + ROPE
QL, KVL = 256, 128
MLA_IN = QL + KVL + ROPE
MLA_SCALE = QK ** -0.5
HALF = ROPE // 2
NG, EPG, NE, FF = 4, 8, 32, 512
NR = NG + NE
CW = 32
CAP = 32
GE = P // CW
NGRP = NE // GE
NSLOT = (NGRP + 1) * P
BODY = 8
ITERS = NE // BODY
PLE = 256

RING = 8
SLOT = 4096
DSLOTS = 6
DTILES = GROUPS + 1
QK_TILE = KD * 2 * DH
V_TILE = KD * GROUPS * DH
HEAD_AREA = GROUPS * QK_TILE + V_TILE
HI_V = 2 * HEAD_AREA
HI_QK = HI_V + V_TILE
assert HI_QK + QK_TILE <= DSLOTS * SLOT


class Tiles:
    DSA_OUT = 0
    MOE = [DSA_OUT + 2, 0]
    PLE = [MOE[0] + 3 * NE, 0]
    MLA = PLE[0] + 3
    MLA_OUT = MLA + 3
    MOE[1] = MLA_OUT + 2
    PLE[1] = MOE[1] + 3 * NE
    N = PLE[1] + 3

    @staticmethod
    def slot(t):
        return (t + DSLOTS) % RING

    @staticmethod
    def fills(t):
        return t // RING + 1

    @staticmethod
    def free(t):
        if t >= RING:
            return Tiles.used(t - RING)
        if t < Tiles.MOE[0]:
            return None
        head = HEADS - 1 if (Tiles.slot(t) + 1) * SLOT <= HEAD_AREA else HEADS
        return "v_ready", TC * head

    @staticmethod
    def used(t):
        if t < Tiles.MOE[0]:
            return "mix_out", TC + 1 + t - Tiles.DSA_OUT
        if Tiles.MLA <= t < Tiles.MLA_OUT:
            return ("lat_ready", "q_ready", "mv_ready")[t - Tiles.MLA], TC
        if Tiles.MLA_OUT <= t < Tiles.MOE[1]:
            return "mix_out", 3 * TC + 1 + t - Tiles.MLA_OUT
        l = 1 if t >= Tiles.MOE[1] else 0
        if t < Tiles.PLE[l]:
            n = t - Tiles.MOE[l]
            return ("gate_ready", "up_ready", "down_ready")[n % 3], NE * l + n // 3 + 1
        return ("pw_ready" if t == Tiles.PLE[l] else "pg_ready"), 2 * TC * (l + 1)


C_ID, C_LOW, C_CAUSAL = 0, 128, 256
C_SLOPE = C_CAUSAL + 384
C_SLOT = C_SLOPE + GROUPS * HEADS
C_EID = C_SLOT + NGRP
C_GID = C_EID + NE
C_COS = C_GID + NE
C_SIN = C_COS + TC * HALF
C_END = C_SIN + TC * HALF
W_GAIN = 0
W_QG = 6 * KD
W_KVG = W_QG + QL // P
W_END = W_KVG + 1


def shape_constants():
    c = np.zeros((P, C_END), np.float32)
    p = np.arange(P)
    c[:, C_ID:C_ID + P] = np.eye(P)
    c[:, C_LOW:C_LOW + P] = p[:, None] < p[None, :]
    tri = np.where(p[None, :] <= p[:, None], 0.0, -BIG)
    c[:, C_CAUSAL:C_CAUSAL + P] = tri
    c[:, C_CAUSAL + 2 * P:C_CAUSAL + 3 * P] = tri
    n = GROUPS * HEADS
    slopes = 2.0 ** (-8.0 * np.arange(1, n + 1) / n)
    c[:, C_SLOPE:C_SLOPE + n] = (slopes / DSA_SCALE).reshape(GROUPS, HEADS).T.reshape(1, n)
    c[:, C_SLOT:C_SLOT + NGRP] = 1 + p[:, None] + P * np.arange(NGRP)[None, :]
    c[:, C_EID:C_EID + NE] = np.arange(NE)
    c[:, C_GID:C_GID + NE] = np.arange(NE) // EPG
    inv = 10000.0 ** (-np.arange(HALF, dtype=np.float32) / HALF)
    ang = (np.arange(T, dtype=np.float32)[:, None] * inv.astype(np.float32)).reshape(TC, P, HALF).transpose(1, 0, 2)
    c[:, C_COS:C_COS + TC * HALF] = np.cos(ang).reshape(P, -1)
    c[:, C_SIN:C_SIN + TC * HALF] = np.sin(ang).reshape(P, -1)
    return c


def distance_table():
    d = np.zeros((P, GROUPS, 2 * P), np.float32)
    delta = np.arange(P)[:, None] + P - np.arange(2 * P)[None, :]
    for g, (window, dil) in enumerate(PATTERNS):
        seen = (delta >= 0) & (delta <= window) & (delta % dil == 0)
        d[:, g] = np.where(seen, -delta, -BIG)
    return d.reshape(P, -1)


class Link:

    def __init__(self, eng, sem):
        self.eng, self.sem, self.n, self.base = eng, sem, 0, 0

    def __call__(self, ins):
        self.n += 1
        ins.then_inc(self.sem, 1)
        self.eng.wait_ge(self.sem, self.base + self.n)

    def enter(self, it, per):
        self.base, self.before, self.per = it * per, self.n, per

    def leave(self, passes):
        assert self.n - self.before == self.per, (self.n - self.before, self.per)
        self.base, self.n = 0, self.before + passes * self.per


def build(nc, x, out, consts, distances, gains, routers, rows, p_t, dsa_w_in, dsa_w_out, mla_w_in, mla_w_qb,
          mla_w_kvb, mla_w_out, moe_w_gate, moe_w_up, moe_w_down, ple_w, ple_w_gate):
    ctx = ExitStack()
    with ctx:
        def sb(name, shape, dt=F32):
            return ctx.enter_context(nc.sbuf_tensor(name, shape, dt))

        sems = {}

        def S(name):
            if name not in sems:
                sems[name] = ctx.enter_context(nc.semaphore(name))
            return sems[name]

        def sb_at(name, shape):
            at = -(-nc.sbuf_base // 32) * 32
            return sb(name, shape), at

        def one_pass(name, base, at, *dims):
            return nc.alloc_sbuf_tensor_at(name, [P, *dims], F32R, offset=base + 4 * at)[:, :, :]

        ring, ring_at = sb_at("ring", [P, RING, SLOT])
        x_sb = sb("x_sb", [P, TC, D])
        hs, hs_at = sb_at("hs", [P, TC, KD, P])
        hT, hT_at = sb_at("hT", [P, KD, T])
        cst = sb("cst", [P, C_END])
        wts = sb("wts", [P, W_END])
        small = sb("small", [P, 256])
        small_u = sb("small_u", [P, 64], U32)
        flag = sb("flag", [1, 2], I32)
        SCR = 13056
        scr, scr_at = sb_at("scr", [P, SCR])
        ps = ctx.enter_context(nc.psum_tensor("ps", [P, 8, 512], F32))

        ident = cst[:, C_ID:C_ID + P]

        def part(ap, at, *dims):
            n = 1
            for d in dims:
                n *= d
            v = ap[:, at:at + n]
            if len(dims) == 2:
                v = v.rearrange("p (a b) -> p a b", b=dims[1])
            elif len(dims) == 3:
                v = v.rearrange("p (a b c) -> p a b c", b=dims[1], c=dims[2])
            return v

        def scratch(at, *dims):
            return part(scr, at, *dims)

        def tile(t, k, n, at=0):
            return ring[:, Tiles.slot(t), :][:, at:at + k * n].rearrange("p (k n) -> p k n", n=n)

        landed = [S(f"landed_{s}") for s in range(RING)]
        landed_dsa = [S(f"landed_dsa_{s}") for s in range(2 * DTILES)]

        def wait_tile(eng, t, more=0):
            eng.wait_ge(landed[Tiles.slot(t)], 16 * (Tiles.fills(t) + more))

        a_qk = [scratch(0, GROUPS, 512), scratch(1536, GROUPS, 512)]
        a_v = [scratch(3072, GROUPS, T), scratch(3840, GROUPS, T)]
        a_s0 = scratch(4608, GROUPS, P)
        a_s1 = scratch(4992, GROUPS, 2 * P)
        a_o = scratch(5760, HEADS, T)
        a_pT = scratch(7808, 9, P)
        a_dist = scratch(8960, GROUPS, 2 * P)
        ring_flat = ring[:, :, :].rearrange("p s n -> p (s n)")

        def qk_at(par, g):
            return HEAD_AREA * par + QK_TILE * g

        def v_at(par):
            return HEAD_AREA * par + GROUPS * QK_TILE

        w_qk = [[part(ring_flat, qk_at(par, g), KD, 2 * DH) for g in range(GROUPS)] for par in range(2)]
        w_v = [part(ring_flat, v_at(par), KD, GROUPS * DH) for par in range(2)]
        w_qk_lo = [[one_pass(f"w_qk_lo_{par}_{g}", ring_at, qk_at(par, g), KD, 2 * DH) for g in range(GROUPS)]
                   for par in range(2)]
        w_v_lo = [one_pass(f"w_v_lo_{par}", ring_at, v_at(par), KD, GROUPS * DH) for par in range(2)]
        w_qk_hi = [one_pass("w_qk_hi_0", ring_at, HI_QK, KD, 2 * DH), one_pass("w_qk_hi_1", scr_at, 10496, KD, 2 * DH)]
        w_v_hi = one_pass("w_v_hi", ring_at, HI_V, KD, GROUPS * DH)
        hT_hi = one_pass("hT_hi", hs_at, 0, KD, T)
        hT_lo = one_pass("hT_lo", hT_at, 0, KD, T)
        m_qT = scratch(0, MH, T)
        m_kT = scratch(4096, MH, T)
        m_q = scratch(8192, TC, MH * QK)
        m_pT = [scratch(8192, 2, 384), scratch(8960, 2, 384)]
        m_o = scratch(9728, KD, T)
        m_lat = scratch(11264, TC, MLA_IN)
        m_kr = scratch(12096, TC, QK)
        hs_flat = hs[:, :, :, :].rearrange("p c k t -> p (c k t)")
        m_qlT = part(hs_flat, 0, QL // P, T)
        m_kvT = hs_flat[:, 512:512 + T]
        m_s = [part(hs_flat, 0, 2, 384), part(hs_flat, 768, 2, 384)]
        m_rope = [scratch(11264 + T * j, MH, HALF) for j in range(4)]
        m_v = hT[:, :, :].rearrange("p k t -> p (k t)").rearrange("p (c n) -> p c n", c=TC)
        e_oneh = scratch(0, TC, NSLOT)
        e_xT = [scratch(2304, KD, P), scratch(3328, KD, P)]
        e_wide = scratch(0, KD, 512)
        e_wide_d = scratch(0, FF // P, D)
        e_y = scratch(4352, D)
        e_iota = scratch(5376, NSLOT)
        e_rows = scratch(6528, 4, T)
        e_sc = scratch(7552, T)
        e_sc2 = scratch(9224, T)
        e_sil = scratch(7808, P)
        e_h = scratch(7936, P)
        e_hT = scratch(8064, P)
        r_lg = scratch(8192, TC, NR)
        r_em = scratch(8264, TC, NE)
        r_m0 = scratch(8328, TC, NE)
        r_m1 = scratch(8392, TC, NE)
        r_wo = scratch(8520, TC, NE)
        r_junk = scratch(8584, P)
        e_pT = scratch(8712, PLE // P, T)
        p_gate = scratch(9224, TC, D)
        o_sil = scratch(9224, TC, 512)
        o_hT = scratch(10248, 4, P)
        r_w = scratch(12544, KD, NR)
        r_b = scratch(12544 + KD * NR, 2 * NR)
        junk_d, junk_a = [scratch(1024 * c, 512) for c in range(TC)], [scratch(1024 * c + 512, 512) for c in range(TC)]
        f_gain = scratch(11272, D)

        ss = part(small, 0, TC, 2)
        rstd = small[:, 134:136]
        root = small[:, 138:140]
        spare = iter(range(204, 256))
        a_mx, a_nmx, a_den = small[:, 4:6], small[:, 6:8], small[:, 8:10]
        m_ss = part(small, 12, 2, TC)
        m_rs = part(small, 16, 2, TC)
        m_mx = part(small, 20, 2, 2)
        m_nmx = part(small, 24, 2, 2)
        m_den = [part(small, 28, 2, 2), part(small, 32, 2, 2)]
        gp8 = part(small, 40, TC, 8)
        gm8 = part(small, 56, TC, 8)
        ev8 = part(small, 72, TC, 8)
        ngm = small[:, 88:90]
        gsum = small[:, 90:92]
        eg4 = small[:, 92:96]
        gif = small[:, 96:98]
        ef = part(small, 98, TC, 2)
        dif = small[:, 102:104]
        rr = part(small, 104, TC, 2)
        fits = part(small, 108, TC, 2)
        wgt = part(small, 112, TC, 2)
        wov = part(small, 116, TC, 2)
        slot_of = part(small, 120, TC, 2)
        cmax = small[:, 124:125]
        w_in = part(small, 128, TC, 2)
        den1 = small[:, 132:134]
        ones = small[:, 136:137]
        m_t = [part(small, 140, TC, HALF), part(small, 172, TC, HALF)]
        gi8 = part(small_u, 0, TC, 8)
        ei8 = part(small_u, 16, TC, 8)

        def bank(b, *dims):
            v = ps[:, b, :]
            return v if not dims else part(v, 0, *dims)

        block = ctx.enter_context(nc.Block())

        dsa_in_v = dsa_w_in.rearrange("(p k) (g w n) -> g p k w n", k=KD, g=GROUPS, w=3)
        kp = lambda w, n: w.rearrange("(p k) (n j) -> n p k j", k=KD, j=n)
        dsa_out_v = dsa_w_out.rearrange("(k p) (n j) -> n p k j", p=P, j=512)
        mla_out_v = mla_w_out.rearrange("(k p) (n j) -> n p k j", p=P, j=512)

        @block.sync
        def _(sp):
            def wait_free(t, more=0):
                if Tiles.free(t) is not None:
                    sem, value = Tiles.free(t)
                    sp.wait_ge(S(sem), value + more)

            def load(t, src, k, n):
                wait_free(t)
                sp.dma_start(tile(t, k, n), src).then_inc(landed[Tiles.slot(t)], 16)

            def load_head(par, h, before=None):
                for g in range(GROUPS):
                    if before is not None:
                        sp.wait_ge(S("qk_ready"), GROUPS * before + g + 1)
                    for w in range(2):
                        sp.dma_start(w_qk[par][g][:, :, w * DH:(w + 1) * DH],
                                     dsa_in_v[g][:, :, w, bass.ds(DH * h, DH)]
                                     ).then_inc(landed_dsa[DTILES * par + g], 16)
                if before is not None:
                    sp.wait_ge(S("v_ready"), TC * before + TC)
                for g in range(GROUPS):
                    sp.dma_start(w_v[par][:, :, g * DH:(g + 1) * DH],
                                 dsa_in_v[g][:, :, 2, bass.ds(DH * h, DH)]
                                 ).then_inc(landed_dsa[DTILES * par + GROUPS], 16)

            for c in range(TC):
                sp.dma_start(x_sb[:, c, :], x[0, c * P:(c + 1) * P, :]).then_inc(S(f"x_in_{c}"), 16)
            for h in range(2):
                load_head(h, h)
            for n in range(2):
                load(Tiles.DSA_OUT + n, dsa_out_v[n], KD, 512)
            with sp.Fori(0, HEADS // 2 - 1) as it:
                for par in range(2):
                    load_head(par, 2 * it + 2 + par, before=2 * it + par)

            def expert_weights(l, e, j):
                one = (moe_w_gate, moe_w_up, moe_w_down)[j][l, bass.ds(e, 1), :, :]
                if j == 2:
                    return one.rearrange("e (j p) n -> p (e j) n", p=P)
                return one.rearrange("e (p k) n -> p (e k) n", k=KD)

            def load_expert_tile(l, n, it=0):
                t, j = Tiles.MOE[l] + n, n % 3
                wait_free(t, BODY * it)
                k, width = (FF // P, D) if j == 2 else (KD, FF)
                sp.dma_start(tile(t, k, width), expert_weights(l, n // 3 + BODY * it, j)
                             ).then_inc(landed[Tiles.slot(t)], 16)

            def load_experts(l):
                for n in range(RING):
                    load_expert_tile(l, n)
                with sp.Fori(0, ITERS - 1) as it:
                    for n in range(RING, RING + 3 * BODY):
                        load_expert_tile(l, n, it)
                for n in range(RING + 3 * BODY * (ITERS - 1), 3 * NE):
                    load_expert_tile(l, n)

            def load_ple(l):
                load(Tiles.PLE[l], ple_w[l].rearrange("(k p) n -> p k n", p=P), PLE // P, D)
                for n in range(2):
                    load(Tiles.PLE[l] + 1 + n, kp(ple_w_gate[l], 512)[n], KD, 512)

            def load_overflow(l):
                sp.wait_ge(S("flag_ready"), l + 1)
                count = sp.value_load(flag[0:1, l:l + 1], min_val=0, max_val=T)
                with sp.If(count > CAP):
                    sp.wait_ge(S("scattered"), (NGRP + 1) * (l + 1))
                    sp.sem_inc(S(f"o_down{l}"), 1)
                    with sp.Fori(0, NE) as e:
                        for j in range(3):
                            if j == 0:
                                sp.wait_ge(S(f"o_down{l}"), e + 1)
                            else:
                                sp.wait_ge(S(f"o_gate{l}" if j == 1 else f"o_up{l}"), TC * e + TC)
                            sp.dma_start(e_wide_d if j == 2 else e_wide, expert_weights(l, e, j)
                                         ).then_inc(S(f"o_landed{l}"), 16)

            load_experts(0)
            load_overflow(0)
            load_ple(0)
            load(Tiles.MLA, mla_w_in.rearrange("(p k) n -> p k n", k=KD), KD, MLA_IN)
            load(Tiles.MLA + 1, mla_w_qb.rearrange("(k p) n -> p k n", p=P), QL // P, MH * QK)
            load(Tiles.MLA + 2, mla_w_kvb.rearrange("(k p) n -> p k n", p=P), 1, MH * (NOPE + MV))
            for n in range(2):
                load(Tiles.MLA_OUT + n, mla_out_v[n], KD, 512)
            load_experts(1)
            load_overflow(1)
            load_ple(1)
            for c in range(TC):
                sp.wait_ge(S("final_ready"), c + 1)
                sp.dma_start(out[0, c * P:(c + 1) * P, :], x_sb[:, c, :]).then_inc(S("stored"), 16)
            sp.wait_ge(S("stored"), 16 * TC)

        @block.gpsimd
        def _(pool):
            pool.dma_start(wts[:, :], gains).then_inc(S("wts_in"), 16)
            pool.dma_start(cst[:, :], consts).then_inc(S("cst_in"), 16)
            pool.dma_start(a_dist, distances.rearrange("p (g n) -> p g n", g=GROUPS)).then_inc(S("dist_in"), 16)
            pool.memset(gp8, -BIG).then_inc(S("fills"), 1)
            pool.memset(ones, 1.0).then_inc(S("fills"), 1)
            pool.dma_start(r_b, rows[0:1, 0:2 * NR].partition_broadcast(P)).then_inc(S("bias_in"), 16)
            for l in range(2):
                if l == 1:
                    pool.wait_ge(S("logits_ready"), TC)
                pool.dma_start(r_w, routers[l].rearrange("p (k n) -> p k n", k=KD)).then_inc(S("router_in"), 16)
                pool.wait_ge(S("mix_out"), 4 * (l + 1))
                pool.iota(e_iota, [[1, NSLOT]], base=1, channel_multiplier=0,
                          allow_small_or_imprecise_dtypes=True).then_inc(S("iota_ready"), 1)
                pool.dma_start(e_pT, p_t[l].rearrange("(k p) t -> p k t", p=P)).then_inc(S("pT_in"), 16)
                if l == 1:
                    pool.dma_start(f_gain, rows[0:1, 2 * NR:2 * NR + D].partition_broadcast(P)
                                   ).then_inc(S("f_gain_in"), 16)

        def dsa_fills(h, par, dmas):
            return 16 * dmas if isinstance(h, int) and h < 2 else 16 * dmas // 2 * (h - par) + 16 * dmas

        def proj_bank(par, n):
            return ((GROUPS + TC) * par + n) % 2

        def wait_x(eng, i, c, n):
            if i == 0:
                eng.wait_ge(S(f"x_in_{c}"), 16)
            elif i in (2, 5):
                eng.wait_ge(S("y_taken_a" if n else "y_taken_d"), TC * (i // 3) + c + 1)
            else:
                eng.wait_ge(S("x_added"), 4 * {1: 0, 3: 1, 4: 2, 6: 3}[i] + 2 * c + n + 1)

        @block.scalar
        def _(act):
            def table(func):
                at = next(spare)
                act.activation(small[0:1, at:at + 1], ones[0:1, :], func)

            def square(i, c):
                wait_x(act, i, c, 1)
                act.activation(junk_a[c], x_sb[:, c, 512:D], ACT.Square, accum_out=ss[:, c, 1:2]).then_inc(S("sq_a"), 1)

            def scale(i, c):
                act.activation(hs[:, c, 4:8, :], x_sb[:, c, :].rearrange("p (t k) -> p k t", k=KD)[:, 4:8, :],
                               ACT.Copy, scale=rstd[:, c:c + 1]).then_inc(S("hs_a"), 1)

            def norm_together(i):
                for c in range(TC):
                    square(i, c)
                act.wait_ge(S("var_ready"), TC * i + TC)
                act.activation(root, root, ACT.Sqrt, scale=1.0 / D).then_inc(S("root_ready"), TC)
                act.wait_ge(S("rstd_ready"), TC * i + TC)
                for c in range(TC):
                    scale(i, c)

            def norm_chunk(i, c):
                square(i, c)
                act.wait_ge(S("var_ready"), TC * i + c + 1)
                act.activation(root[:, c:c + 1], root[:, c:c + 1], ACT.Sqrt, scale=1.0 / D).then_inc(S("root_ready"), 1)
                if i < 6:
                    act.wait_ge(S("rstd_ready"), TC * i + c + 1)
                    scale(i, c)

            def high_qk(h, g, par, first=False):
                n = GROUPS * h + g
                act.wait_ge(landed_dsa[DTILES * par + g], dsa_fills(h, par, 2))
                if not first:
                    act.wait_ge(S("qk_ready"), n - 1)
                act.copy(w_qk_hi[(GROUPS * par + g) % 2], w_qk[par][g]).then_inc(S("w_qk_high"), 1)

            def high_v(h, par, first=False):
                act.wait_ge(landed_dsa[DTILES * par + GROUPS], dsa_fills(h, par, GROUPS))
                if not first:
                    act.wait_ge(S("v_ready"), TC * h)
                act.copy(w_v_hi, w_v[par]).then_inc(S("w_v_high"), 1)

            def copy_qk(h, g, buf, first=False):
                act.wait_ge(S("qk_ready"), GROUPS * h + g + 1)
                if g == 0 and not first:
                    act.wait_ge(S("s_ready"), h - 1)
                act.copy(a_qk[buf][:, g, :], bank(proj_bank(buf, g))).then_inc(S("qk_copied"), 1)

            def attend(h):
                act.wait_ge(S("nmx_ready"), h + 1)
                s0 = a_s0.rearrange("p g n -> p (g n)")
                s1 = a_s1.rearrange("p g n -> p (g n)")
                act.activation(s0, s0, ACT.Exp, bias=a_nmx[:, 0:1], scale=DSA_SCALE,
                               accum_out=a_den[:, 0:1]).then_inc(S("e_ready"), 1)
                act.activation(s1, s1, ACT.Exp, bias=a_nmx[:, 1:2], scale=DSA_SCALE,
                               accum_out=a_den[:, 1:2]).then_inc(S("e_ready"), 1)

            def copy_pT(h):
                for b in (0, 2):
                    act.wait_ge(S("pT_ready"), 3 * h + b + 1)
                    act.copy(a_pT[:, 3 * b:3 * b + 3, :], bank(5, 4, P)[:, 0:3, :]).then_inc(S("pT_copied_a"), 1)

            def copy_o(h):
                act.wait_ge(S("o_ready"), h + 1)
                act.copy(a_o[:, bass.ds(h, 1), :].rearrange("p h t -> p (h t)"),
                         bank(7)[:, 0:T]).then_inc(S("o_copied"), 1)

            def step(h_att, h_proj, buf, first=False, last=False):
                attend(h_att)
                copy_qk(h_proj, 0, buf, first)
                high_qk(h_proj, 2, buf)
                high_v(h_proj, buf)
                copy_qk(h_proj, 1, buf)
                copy_pT(h_att)
                if not last:
                    high_qk(h_proj + 1, 0, 1 - buf)
                copy_qk(h_proj, 2, buf)
                if not last:
                    high_qk(h_proj + 1, 1, 1 - buf)
                copy_o(h_att)

            act.wait_ge(S("fills"), 2)
            table(ACT.Sqrt)
            norm_together(0)
            act.wait_ge(S("hT_turned"), 4)
            for c in range(TC):
                act.wait_ge(S("hT_ready"), 2 * c + 2)
                act.copy(hT_hi[:, :, c * P:(c + 1) * P], hT[:, :, c * P:(c + 1) * P]).then_inc(S("hT_high"), 1)
            high_qk(0, 0, 0, first=True)
            high_qk(0, 1, 0, first=True)
            copy_qk(0, 0, 0, first=True)
            high_qk(0, 2, 0)
            high_v(0, 0, first=True)
            copy_qk(0, 1, 0, first=True)
            high_qk(1, 0, 1)
            copy_qk(0, 2, 0, first=True)
            high_qk(1, 1, 1)
            step(0, 1, 1, first=True)
            with act.Fori(0, HEADS // 2 - 2) as it:
                step(2 * it + 1, 2 * it + 2, 0)
                step(2 * it + 2, 2 * it + 3, 1)
            step(HEADS - 3, HEADS - 2, 0)
            step(HEADS - 2, HEADS - 1, 1, last=True)
            attend(HEADS - 1)
            copy_pT(HEADS - 1)
            copy_o(HEADS - 1)

            def experts(l):
                for c in range(TC):
                    act.wait_ge(S("ngm_ready"), 2 * l + c + 1)
                    act.activation(eg4, r_lg[:, c, 0:NG], ACT.Exp, bias=ngm[:, c:c + 1],
                                   accum_out=gsum[:, c:c + 1]).then_inc(S("gsum_ready"), 1)
                    act.wait_ge(S("gsum_ready"), 2 * l + c + 1)
                act.wait_ge(S("dif_ready"), l + 1)
                act.activation(dif, dif, ACT.Exp).then_inc(S("dexp_ready"), 1)
                act.wait_ge(S("rows_ready"), l + 1)
                act.copy(e_rows.rearrange("p a t -> p (a t)"),
                         ps[:, 5:7, :].rearrange("p a b -> p (a b)")).then_inc(S("rows_copied"), 1)
                table(ACT.Silu)
                with act.Fori(0, ITERS) as it:
                    for i in range(BODY):
                        e = NE * l + BODY * it + i
                        act.wait_ge(S("gate_ready"), e + 1)
                        act.activation(e_sil, bank(4)[:, 0:P], ACT.Silu).then_inc(S("silu_ready"), 1)
                        act.wait_ge(S("down_ready"), e + 1)
                        if i % GE == 0:
                            grp = (NGRP + 1) * l + (BODY // GE) * it + i // GE
                            act.wait_ge(S("scattered"), grp + 1)
                        for q in (2, 3):
                            ins = act.copy(e_y[CW * (i % GE):CW * (i % GE) + CW, T * q:T * q + T],
                                           bank(6)[CW * q:CW * q + CW, 0:T])
                        ins.then_inc(S("y_copied_a"), 1)
                act.wait_ge(S("flag_ready"), l + 1)
                count = act.value_load(flag[0:1, l:l + 1], min_val=0, max_val=T)
                with act.If(count > CAP):
                    with act.Fori(0, NE) as e:
                        for c in range(TC):
                            act.wait_ge(S(f"o_gate{l}"), TC * e + c + 1)
                            act.activation(o_sil[:, c, :], bank(4 + c), ACT.Silu).then_inc(S(f"o_silu{l}"), 1)
                    act.wait_ge(S(f"o_down{l}"), NE + 1)
                table(ACT.Sqrt)
                act.wait_ge(S("scattered"), (NGRP + 1) * (l + 1))
                for c in range(TC):
                    act.copy(x_sb[:, c, 512:D], bank(2 * c + 1)).then_inc(S("y_taken_a"), 1)

            def ple(l):
                norm_together(3 * l + 2)
                table(ACT.Sigmoid)
                for c in range(TC):
                    for n in range(2):
                        act.wait_ge(S("pg_ready"), 4 * l + 2 * c + n + 1)
                        act.activation(p_gate[:, c, 512 * n:512 * n + 512], bank(4 + 2 * c + n),
                                       ACT.Sigmoid).then_inc(S("sig_ready"), 1)
                    table(ACT.Sqrt)
                    norm_chunk(3 * l + 3, c)

            table(ACT.Sqrt)
            for c in range(TC):
                norm_chunk(1, c)
            experts(0)
            ple(0)

            for c in range(TC):
                act.wait_ge(S("lat_ready"), c + 1)
                act.copy(m_lat[:, c, :], bank(c)[:, 0:MLA_IN]).then_inc(S("lat_copied"), 1)
                act.wait_ge(S("lat_copied"), c + 1)
                for j, (a, b) in enumerate(((0, QL), (QL, QL + KVL))):
                    act.activation(junk_a[c][:, a:b], m_lat[:, c, a:b], ACT.Square,
                                   accum_out=m_ss[:, j, c:c + 1]).then_inc(S("lat_sq"), 1)
            act.wait_ge(S("lat_var"), 2)
            act.activation(m_rs, m_ss, ACT.Sqrt).then_inc(S("lat_root"), 1)
            table(ACT.Exp)
            act.wait_ge(S("q_ready"), 2)
            act.copy(m_q[:, 1, :], ps[:, 0:3, :].rearrange("p a b -> p (a b)")).then_inc(S("q_copied_a"), 1)
            for j in range(MH // 2):
                act.wait_ge(S("k_ready"), j + 1)
                act.copy(m_kT[0:NOPE, 2 * j:2 * j + 2, :], bank(3 + 4 * (j % 2), 2, T)[0:NOPE, :, :]).then_inc(S("k_copied"), 1)
            for j in range(MH // 2):
                if j % 2 == 1:
                    act.wait_ge(S("qT_ready"), j + 1)
                    act.copy(m_qT[0:QK, 2 * j:2 * j + 2, :], bank(6, 2, T)[0:QK, :, :]).then_inc(S("qT_copied_a"), 1)

            def m_exps(j):
                act.wait_ge(S("m_nmx"), j + 1)
                for h2 in range(2):
                    for c, (a, b) in enumerate(((0, P), (P, 3 * P))):
                        ins = act.activation(m_s[j % 2][:, h2, a:b], m_s[j % 2][:, h2, a:b], ACT.Exp,
                                             bias=m_nmx[:, c, h2:h2 + 1], scale=MLA_SCALE,
                                             accum_out=m_den[j % 2][:, c, h2:h2 + 1])
                ins.then_inc(S("m_exp"), 1)

            m_exps(0)
            for j in range(MH // 2):
                if j + 1 < MH // 2:
                    m_exps(j + 1)
                act.wait_ge(S("m_pT_ready"), j + 1)
                act.copy(m_pT[j % 2][:, 1, :], bank(3)[:, 0:384]).then_inc(S("m_pT_copied_a"), 1)
                act.wait_ge(S("m_o_ready"), j + 1)
                act.copy(m_o[:, j, :], bank(4)[:, 0:T]).then_inc(S("m_o_copied"), 1)

            table(ACT.Sqrt)
            for c in range(TC):
                norm_chunk(4, c)
            experts(1)
            ple(1)

        @block.vector
        def _(dve):
            link = Link(dve, S("dve_link"))

            def square(i, c):
                wait_x(dve, i, c, 0)
                dve.tensor_tensor_reduce(out=junk_d[c], in0=x_sb[:, c, 0:512], in1=x_sb[:, c, 0:512], scale=1.0,
                                         scalar=0.0, op0=ALU.mult, op1=ALU.add,
                                         accum_out=ss[:, c, 0:1]).then_inc(S("sq_d"), 1)

            def roots(i, a, b):
                dve.wait_ge(S("sq_d"), TC * i + b)
                dve.wait_ge(S("sq_a"), TC * i + b)
                dve.scalar_tensor_tensor(out=root[:, a:b], in0=ss[:, a:b, 0], scalar=EPS * D, in1=ss[:, a:b, 1],
                                         op0=ALU.add, op1=ALU.add).then_inc(S("var_ready"), b - a)
                dve.wait_ge(S("root_ready"), TC * i + b)
                dve.reciprocal(rstd[:, a:b], root[:, a:b]).then_inc(S("rstd_ready"), b - a)
                dve.wait_ge(S("rstd_ready"), TC * i + b)

            def scale(i, c):
                dve.tensor_scalar(hs[:, c, 0:4, :], x_sb[:, c, :].rearrange("p (t k) -> p k t", k=KD)[:, 0:4, :],
                                  rstd[:, c:c + 1], None, ALU.mult).then_inc(S("hs_d"), 1)

            def gains_on(i, c):
                if i == 0:
                    dve.wait_ge(S("wts_in"), 16)
                gain = part(wts, W_GAIN + i * KD, KD)
                for b in range(2):
                    dve.wait_ge(S("hT_turned"), 4 * i + 2 * c + b + 1)
                    dve.tensor_tensor(hT[:, 4 * b:4 * b + 4, c * P:(c + 1) * P], bank(4 + 2 * c + b, 4, P),
                                      gain[:, 4 * b:4 * b + 4].unsqueeze(2).to_broadcast([P, 4, P]),
                                      ALU.mult).then_inc(S("hT_ready"), 1)

            def norm_together(i):
                for c in range(TC):
                    square(i, c)
                roots(i, 0, TC)
                for c in range(TC):
                    scale(i, c)
                for c in range(TC):
                    gains_on(i, c)

            def norm_staged(i, add, between, after=None):
                for c in range(TC):
                    for n in range(2):
                        add(c, n)
                        if n == 0:
                            square(i, c)
                        if c == 1 and n == 0:
                            gains_on(i, 0)
                            between()
                    roots(i, c, c + 1)
                    scale(i, c)
                if after is not None:
                    after()
                gains_on(i, 1)

            def low_qk(h, g, par):
                dve.wait_ge(S("w_qk_high"), GROUPS * h + g + 1)
                dve.tensor_tensor(w_qk_lo[par][g], w_qk[par][g],
                                  w_qk_hi[(GROUPS * par + g) % 2].bitcast(F32), ALU.subtract).then_inc(S("w_qk_low"), 1)

            def low_v(h, par):
                dve.wait_ge(S("w_v_high"), h + 1)
                dve.tensor_tensor(w_v_lo[par], w_v[par], w_v_hi.bitcast(F32),
                                  ALU.subtract).then_inc(S("w_v_low"), 1)

            def copy_v(h, buf, first=False):
                for c in range(TC):
                    dve.wait_ge(S("v_ready"), TC * h + c + 1)
                    if c == 0 and not first:
                        dve.wait_ge(S("o_ready"), h - 1)
                    dve.tensor_copy(a_v[buf][:, :, c * P:(c + 1) * P],
                                    bank(proj_bank(buf, GROUPS + c), 4, P)[:, 0:GROUPS, :]).then_inc(S("v_copied"), 1)

            def softmax_head(h):
                dve.wait_ge(S("s_ready"), h + 1)
                for g in range(GROUPS):
                    slope = cst[:, bass.ds(C_SLOPE + GROUPS * h + g, 1)]
                    src = bank(3)[:, 2 * P * g:2 * P * g + 2 * P] if g < 2 else bank(4)[:, 0:2 * P]
                    dve.scalar_tensor_tensor(out=a_s0[:, g, :], in0=a_dist[:, g, P:2 * P], scalar=slope,
                                             in1=bank(2)[:, P * g:P * g + P], op0=ALU.mult, op1=ALU.add)
                    ins = dve.scalar_tensor_tensor(out=a_s1[:, g, :], in0=a_dist[:, g, :], scalar=slope,
                                                   in1=src, op0=ALU.mult, op1=ALU.add)
                ins.then_inc(S("s_taken"), 1)
                dve.wait_ge(S("s_taken"), h + 1)
                dve.tensor_reduce(a_mx[:, 0:1], a_s0.rearrange("p g n -> p (g n)"), AX.X, ALU.max)
                link(dve.tensor_reduce(a_mx[:, 1:2], a_s1.rearrange("p g n -> p (g n)"), AX.X, ALU.max))
                dve.tensor_scalar(a_nmx, a_mx, -DSA_SCALE, None, ALU.mult).then_inc(S("nmx_ready"), 1)

            def softmax_tail(h):
                dve.wait_ge(S("e_ready"), 2 * h + 2)
                link(dve.reciprocal(a_den, a_den))
                s0 = a_s0.rearrange("p g n -> p (g n)")
                s1 = a_s1.rearrange("p g n -> p (g n)")
                dve.tensor_scalar(s0, s0, a_den[:, 0:1], None, ALU.mult).then_inc(S("p_ready"), 1)
                dve.tensor_scalar(s1, s1, a_den[:, 1:2], None, ALU.mult).then_inc(S("p_ready"), 1)

            def copy_pT(h):
                dve.wait_ge(S("pT_ready"), 3 * h + 2)
                dve.tensor_copy(a_pT[:, 3:6, :], bank(6, 4, P)[:, 0:3, :]).then_inc(S("pT_copied_d"), 1)

            def step(h_att, h_proj, buf, first=False, last=False):
                softmax_head(h_att)
                softmax_tail(h_att)
                low_qk(h_proj, 2, buf)
                low_v(h_proj, buf)
                copy_pT(h_att)
                if not last:
                    low_qk(h_proj + 1, 0, 1 - buf)
                    low_qk(h_proj + 1, 1, 1 - buf)
                copy_v(h_proj, buf, first)

            norm_together(0)
            for c in range(TC):
                dve.wait_ge(S("hT_high"), c + 1)
                dve.tensor_tensor(hT_lo[:, :, c * P:(c + 1) * P], hT[:, :, c * P:(c + 1) * P],
                                  hT_hi[:, :, c * P:(c + 1) * P].bitcast(F32), ALU.subtract).then_inc(S("hT_low"), 1)
            for g in range(GROUPS):
                low_qk(0, g, 0)
            low_v(0, 0)
            low_qk(1, 0, 1)
            low_qk(1, 1, 1)
            copy_v(0, 0, first=True)
            dve.wait_ge(S("cst_in"), 16)
            dve.wait_ge(S("dist_in"), 16)
            step(0, 1, 1, first=True)
            with dve.Fori(0, HEADS // 2 - 2) as it:
                link.enter(it, 4)
                step(2 * it + 1, 2 * it + 2, 0)
                step(2 * it + 2, 2 * it + 3, 1)
            link.leave(HEADS // 2 - 2)
            step(HEADS - 3, HEADS - 2, 0)
            step(HEADS - 2, HEADS - 1, 1, last=True)
            softmax_head(HEADS - 1)
            softmax_tail(HEADS - 1)
            copy_pT(HEADS - 1)

            def add_mixed(l):
                def add(c, n):
                    dve.wait_ge(S("mix_out"), 4 * l + 2 * c + n + 1)
                    x_half = x_sb[:, c, 512 * n:512 * n + 512]
                    dve.tensor_tensor(x_half, x_half, bank(2 * c + n), ALU.add).then_inc(S("x_added"), 1)
                return add

            def choose(l, c):
                if c == 0:
                    dve.wait_ge(S("bias_in"), 16)
                    dve.wait_ge(S("fills"), 2)
                dve.wait_ge(S("logits_ready"), TC * l + c + 1)
                lg, bias = bank(4)[:, c * NR:(c + 1) * NR], r_b[:, l * NR:(l + 1) * NR]
                dve.tensor_tensor(r_lg[:, c, :], lg, bias, ALU.add)
                link(dve.tensor_tensor(gp8[:, c, 0:NG], lg[:, 0:NG], bias[:, 0:NG], ALU.add))
                link(dve.max(gm8[:, c, :], gp8[:, c, :]))
                dve.tensor_scalar(ngm[:, c:c + 1], gm8[:, c, 0:1], -1.0, None, ALU.mult).then_inc(S("ngm_ready"), 1)
                link(dve.max_index(gi8[:, c, :], gm8[:, c, :], gp8[:, c, :]))
                link(dve.tensor_copy(gif[:, c:c + 1], gi8[:, c, 0:1]))
                link(dve.tensor_scalar(r_em[:, c, :], cst[:, C_GID:C_GID + NE], gif[:, c:c + 1], BIG,
                                       ALU.is_equal, ALU.mult))
                link(dve.scalar_tensor_tensor(out=r_em[:, c, :], in0=r_em[:, c, :], scalar=-BIG,
                                              in1=r_lg[:, c, NG:NR], op0=ALU.add, op1=ALU.add))
                link(dve.max(ev8[:, c, :], r_em[:, c, :]))
                link(dve.max_index(ei8[:, c, :], ev8[:, c, :], r_em[:, c, :]))
                link(dve.tensor_copy(ef[:, c, :], ei8[:, c, 0:2]))
                for a, m in enumerate((r_m0, r_m1)):
                    ins = dve.tensor_scalar(m[:, c, :], cst[:, C_EID:C_EID + NE], ef[:, c, a:a + 1], None, ALU.is_equal)
                ins.then_inc(S("choice_ready"), 1)

            def one_hot(c, a, b):
                link(dve.tensor_scalar(e_oneh[:, c, a:b], e_iota[:, a:b], slot_of[:, c, 0:1], None, ALU.is_equal))
                return dve.scalar_tensor_tensor(out=e_oneh[:, c, a:b], in0=e_iota[:, a:b], scalar=slot_of[:, c, 1:2],
                                                in1=e_oneh[:, c, a:b], op0=ALU.is_equal, op1=ALU.add)

            def place(l, c):
                dve.wait_ge(S("choice_ready"), TC * l + c + 1)
                dve.wait_ge(S("ranks_ready"), TC * l + c + 1)
                for a, m in enumerate((r_m0, r_m1)):
                    ins = dve.tensor_tensor_reduce(out=r_junk[:, NE * a:NE * a + NE], in0=bank(5)[:, NE * c:NE * c + NE],
                                                   in1=m[:, c, :], scale=1.0, scalar=0.0, op0=ALU.mult,
                                                   op1=ALU.add, accum_out=rr[:, c, a:a + 1])
                link(ins)
                dve.tensor_scalar(fits[:, c, :], rr[:, c, :], float(CAP), None, ALU.is_lt)
                link(dve.scalar_tensor_tensor(out=slot_of[:, c, :], in0=ef[:, c, :], scalar=float(CW), in1=rr[:, c, :],
                                              op0=ALU.mult, op1=ALU.add))
                link(dve.scalar_tensor_tensor(out=slot_of[:, c, :], in0=slot_of[:, c, :], scalar=1.0,
                                              in1=fits[:, c, :], op0=ALU.add, op1=ALU.mult))
                if c == 0:
                    dve.wait_ge(S("iota_ready"), l + 1)
                one_hot(c, 0, P).then_inc(S("oneh_first"), 1)

            def weigh_choices(l):
                dve.wait_ge(S("dexp_ready"), l + 1)
                dve.wait_ge(S("gsum_ready"), 2 * l + 2)
                link(dve.scalar_tensor_tensor(out=den1, in0=dif, scalar=1.0, in1=gsum, op0=ALU.add, op1=ALU.mult))
                link(dve.reciprocal(w_in[:, :, 0], den1))
                link(dve.tensor_tensor(w_in[:, :, 1], w_in[:, :, 0], dif, ALU.mult))
                link(dve.tensor_tensor(wgt, w_in, fits, ALU.mult))
                dve.tensor_tensor(wov, w_in, wgt, ALU.subtract)
                link(dve.tensor_reduce(cmax[0:1, :], bank(5)[0:1, 2 * NE:3 * NE], AX.X, ALU.max))
                dve.tensor_copy(flag[0:1, l:l + 1], cmax[0:1, :]).then_inc(S("flag_ready"), 1)
                dve.wait_ge(S("flag_ready"), l + 1)

            def later_slots(l):
                for c in range(TC):
                    one_hot(c, P, NSLOT).then_inc(S("oneh_ready"), 1)
                for c in range(TC):
                    link(dve.tensor_scalar(r_wo[:, c, :], r_m0[:, c, :], wov[:, c, 0:1], None, ALU.mult))
                    link(dve.scalar_tensor_tensor(out=r_wo[:, c, :], in0=r_m1[:, c, :], scalar=wov[:, c, 1:2],
                                                  in1=r_wo[:, c, :], op0=ALU.mult, op1=ALU.add))

            def take_gathered(l, grp, half, buf):
                gain = part(wts, W_GAIN + (3 * l + 1) * KD, KD)
                dve.wait_ge(S("gathered"), (2 * (NGRP + 1)) * l + 2 * grp + half + 1)
                dve.tensor_tensor(e_xT[buf][:, 4 * half:4 * half + 4, :], bank(7, 4, P),
                                  gain[:, 4 * half:4 * half + 4].unsqueeze(2).to_broadcast([P, 4, P]),
                                  ALU.mult).then_inc(S("xT_ready"), 1)

            def experts(l):
                norm_staged(3 * l + 1, add_mixed(l), lambda: choose(l, 0), lambda: place(l, 0))
                choose(l, 1)
                dve.tensor_tensor(dif, ev8[:, :, 1], ev8[:, :, 0], ALU.subtract).then_inc(S("dif_ready"), 1)
                place(l, 1)
                weigh_choices(l)
                for half in range(2):
                    take_gathered(l, 0, half, 0)
                later_slots(l)
                dve.wait_ge(S("rows_copied"), l + 1)
                with dve.Fori(0, ITERS) as it:
                    link.enter(it, 2 * BODY // GE)
                    for i in range(BODY):
                        e = NE * l + BODY * it + i
                        grp = (BODY // GE) * it + i // GE
                        dve.wait_ge(S("silu_ready"), e + 1)
                        dve.wait_ge(S("up_ready"), e + 1)
                        dve.tensor_tensor(e_h, e_sil, bank(5)[:, 0:P], ALU.mult).then_inc(S("h_ready"), 1)
                        dve.wait_ge(S("hT_e"), e + 1)
                        dve.tensor_copy(e_hT, bank(5)[:, P:2 * P]).then_inc(S("hT_copied"), 1)
                        dve.wait_ge(S("down_ready"), e + 1)
                        if i % GE == 0:
                            dve.wait_ge(S("scattered"), (NGRP + 1) * l + grp + 1)
                        for q in (0, 1):
                            ins = dve.tensor_copy(e_y[CW * (i % GE):CW * (i % GE) + CW, T * q:T * q + T],
                                                  bank(6)[CW * q:CW * q + CW, 0:T])
                        ins.then_inc(S("y_copied_d"), 1)
                        if i % GE in (1, 2):
                            take_gathered(l, grp + 1, i % GE - 1, (i // GE + 1) % 2)
                        if i % GE == 2:
                            slot_id = cst[:, bass.ds(C_SLOT + grp, 1)]
                            link(dve.scalar_tensor_tensor(out=e_sc2, in0=e_rows[:, 0, :], scalar=slot_id,
                                                          in1=e_rows[:, 2, :], op0=ALU.is_equal, op1=ALU.mult))
                            link(dve.scalar_tensor_tensor(out=e_sc, in0=e_rows[:, 1, :], scalar=slot_id,
                                                          in1=e_rows[:, 3, :], op0=ALU.is_equal, op1=ALU.mult))
                            dve.tensor_tensor(e_sc, e_sc, e_sc2, ALU.add).then_inc(S("sc_ready"), 1)
                link.leave(ITERS)
                count = dve.value_load(flag[0:1, l:l + 1], min_val=0, max_val=T)
                with dve.If(count > CAP):
                    with dve.Fori(0, NE) as e:
                        for c in range(TC):
                            dve.wait_ge(S(f"o_silu{l}"), TC * e + c + 1)
                            dve.wait_ge(S(f"o_up{l}"), TC * e + c + 1)
                            dve.scalar_tensor_tensor(out=o_sil[:, c, :], in0=o_sil[:, c, :],
                                                     scalar=r_wo[:, c, bass.ds(e, 1)], in1=bank(6 + c),
                                                     op0=ALU.mult, op1=ALU.mult).then_inc(S(f"o_h{l}"), 1)
                            dve.wait_ge(S(f"o_turned{l}"), TC * e + c + 1)
                            dve.tensor_copy(o_hT, bank(4, 4, P)).then_inc(S(f"o_hT{l}"), 1)
                    dve.wait_ge(S(f"o_down{l}"), NE + 1)
                dve.wait_ge(S("scattered"), (NGRP + 1) * (l + 1))
                for c in range(TC):
                    dve.tensor_copy(x_sb[:, c, 0:512], bank(2 * c)).then_inc(S("y_taken_d"), 1)

            def add_ple(l):
                def add(c, n):
                    dve.wait_ge(S("sig_ready"), 4 * l + 2 * c + n + 1)
                    dve.wait_ge(S("pw_ready"), 4 * l + 2 * c + n + 1)
                    g = p_gate[:, c, 512 * n:512 * n + 512]
                    link(dve.tensor_tensor(g, g, bank(2 * c + n), ALU.mult))
                    x_half = x_sb[:, c, 512 * n:512 * n + 512]
                    dve.tensor_tensor(x_half, x_half, g, ALU.add).then_inc(S("x_added"), 1)
                return add

            experts(0)
            norm_together(2)
            norm_staged(3, add_ple(0), lambda: None)

            dve.wait_ge(S("lat_sq"), 4)
            link(dve.tensor_scalar(m_ss[:, 0, :], m_ss[:, 0, :], 1.0 / QL, EPS, ALU.mult, ALU.add))
            dve.tensor_scalar(m_ss[:, 1, :], m_ss[:, 1, :], 1.0 / KVL, EPS, ALU.mult, ALU.add).then_inc(S("lat_var"), 2)
            dve.wait_ge(S("lat_root"), 1)
            link(dve.reciprocal(m_rs, m_rs))
            for c in range(TC):
                for j, (a, b) in enumerate(((0, QL), (QL, QL + KVL))):
                    dve.tensor_scalar(m_lat[:, c, a:b], m_lat[:, c, a:b], m_rs[:, j, c:c + 1], None,
                                      ALU.mult).then_inc(S("ln_ready"), 1)
            cos = part(cst, C_COS, TC, HALF)
            sin = part(cst, C_SIN, TC, HALF)
            link(dve.memset(m_kr[:, :, 0:NOPE], 0.0))
            k1, k2 = m_lat[:, :, QL + KVL:QL + KVL + HALF], m_lat[:, :, QL + KVL + HALF:MLA_IN]
            for o, (u, v, op) in enumerate((((k1, cos), (k2, sin), ALU.subtract), ((k1, sin), (k2, cos), ALU.add))):
                link(dve.tensor_tensor(m_t[0], u[0], u[1], ALU.mult))
                link(dve.tensor_tensor(m_t[1], v[0], v[1], ALU.mult))
                ins = dve.tensor_tensor(m_kr[:, :, NOPE + HALF * o:NOPE + HALF * o + HALF], m_t[0], m_t[1], op)
                if o == 0:
                    link(ins)
            ins.then_inc(S("kr_ready"), 1)
            dve.wait_ge(S("lnT"), 1)
            qg, kvg = part(wts, W_QG, QL // P), wts[:, W_KVG:W_KVG + 1]
            dve.tensor_tensor(m_qlT, bank(2, 2, T), qg.unsqueeze(2).to_broadcast([P, 2, T]),
                              ALU.mult).then_inc(S("lnT_copied"), 1)
            dve.tensor_scalar(m_kvT, bank(3)[:, 0:T], kvg, None, ALU.mult).then_inc(S("lnT_copied"), 1)
            dve.tensor_copy(m_kT[NOPE:QK, :, :],
                            bank(3)[NOPE:QK, T:2 * T].unsqueeze(1).to_broadcast([ROPE, MH, T])
                            ).then_inc(S("lnT_copied"), 1)
            dve.wait_ge(S("q_ready"), 1)
            dve.tensor_copy(m_q[:, 0, :], ps[:, 4:7, :].rearrange("p a b -> p (a b)")).then_inc(S("q_copied_d"), 1)
            dve.wait_ge(S("q_copied_d"), 1)
            for c in range(TC):
                if c == 1:
                    dve.wait_ge(S("q_copied_a"), 1)
                qh = m_q[:, c, :].rearrange("p (h n) -> p h n", n=QK)
                q1, q2 = qh[:, :, NOPE:NOPE + HALF], qh[:, :, NOPE + HALF:QK]
                cb = cos[:, c, :].unsqueeze(1).to_broadcast([P, MH, HALF])
                sn = sin[:, c, :].unsqueeze(1).to_broadcast([P, MH, HALF])
                t = m_rope
                link(dve.tensor_tensor(t[0], q1, cb, ALU.mult))
                link(dve.tensor_tensor(t[1], q2, sn, ALU.mult))
                link(dve.tensor_tensor(t[2], q1, sn, ALU.mult))
                link(dve.tensor_tensor(t[3], q2, cb, ALU.mult))
                dve.tensor_tensor(q1, t[0], t[1], ALU.subtract).then_inc(S("q_rot"), 1)
                dve.tensor_tensor(q2, t[2], t[3], ALU.add).then_inc(S("q_rot"), 1)
                dve.wait_ge(S("q_rot"), 2 * (c + 1))
            for c in range(TC):
                dve.wait_ge(S("mv_ready"), c + 1)
                b = 4 if c == 0 else 0
                dve.tensor_copy(m_v[:, c, :], ps[:, b:b + 2, :].rearrange("p a b -> p (a b)")).then_inc(S("mv_copied"), 1)
            for j in range(0, MH // 2, 2):
                dve.wait_ge(S("qT_ready"), j + 1)
                dve.tensor_copy(m_qT[0:QK, 2 * j:2 * j + 2, :], bank(2, 2, T)[0:QK, :, :]).then_inc(S("qT_copied_d"), 1)
            causal = cst[:, C_CAUSAL:C_CAUSAL + 384].unsqueeze(1).to_broadcast([P, 2, 384])

            def m_scores(j):
                dve.wait_ge(S("m_s_ready"), j + 1)
                src = ps[:, 0:2, 0:384] if j % 2 == 0 else ps[:, 5:7, 0:384]
                link(dve.tensor_tensor(m_s[j % 2], src, causal, ALU.add))
                link(dve.tensor_reduce(m_mx[:, 0, :], m_s[j % 2][:, :, 0:P], AX.X, ALU.max))
                link(dve.tensor_reduce(m_mx[:, 1, :], m_s[j % 2][:, :, P:3 * P], AX.X, ALU.max))
                if j >= 1:
                    dve.wait_ge(S("m_exp"), j)
                dve.tensor_scalar(m_nmx, m_mx, -MLA_SCALE, None, ALU.mult).then_inc(S("m_nmx"), 1)

            m_scores(0)
            for j in range(MH // 2):
                if j + 1 < MH // 2:
                    m_scores(j + 1)
                dve.wait_ge(S("m_exp"), j + 1)
                link(dve.reciprocal(m_den[j % 2], m_den[j % 2]))
                for h2 in range(2):
                    for c, (a, b) in enumerate(((0, P), (P, 3 * P))):
                        ins = dve.tensor_scalar(m_s[j % 2][:, h2, a:b], m_s[j % 2][:, h2, a:b],
                                                m_den[j % 2][:, c, h2:h2 + 1], None, ALU.mult)
                ins.then_inc(S("m_p"), 1)
                dve.wait_ge(S("m_pT_ready"), j + 1)
                dve.tensor_copy(m_pT[j % 2][:, 0, :], bank(2)[:, 0:384]).then_inc(S("m_pT_copied_d"), 1)

            experts(1)
            norm_together(5)
            add = add_ple(1)
            for c in range(TC):
                for n in range(2):
                    add(c, n)
                    if n == 0:
                        square(6, c)
                roots(6, c, c + 1)
                if c == 0:
                    dve.wait_ge(S("f_gain_in"), 16)
                dve.scalar_tensor_tensor(out=x_sb[:, c, :], in0=x_sb[:, c, :], scalar=rstd[:, c:c + 1], in1=f_gain,
                                         op0=ALU.mult, op1=ALU.mult).then_inc(S("final_ready"), 1)

        @block.tensor
        def _(pe):
            def turn_rows(i, c):
                if i == 0 and c == 0:
                    pe.wait_ge(S("cst_in"), 16)
                for b in range(2):
                    pe.wait_ge(S("hs_a" if b else "hs_d"), TC * i + c + 1)
                    for k in range(4):
                        mm = pe.transpose(bank(4 + 2 * c + b)[:, k * P:(k + 1) * P], hs[:, c, 4 * b + k, :], ident)
                    mm.then_inc(S("hT_turned"), 1)

            def three_pass(dst, w_hi, w_lo, x_hi, x_lo, first, last):
                pe.matmul(dst, w_hi, x_hi, start=first, stop=False)
                pe.matmul(dst, w_hi, x_lo, start=False, stop=False)
                return pe.matmul(dst, w_lo, x_hi, start=False, stop=last)

            def project_qk(h, g, buf, first=False):
                pe.wait_ge(S("w_qk_low"), GROUPS * h + g + 1)
                if g == 2:
                    pe.wait_ge(S("qk_copied"), GROUPS * h + 1)
                elif not first:
                    pe.wait_ge(S("v_copied"), TC * h - 1 + g)
                hi, lo = w_qk_hi[(GROUPS * buf + g) % 2], w_qk_lo[buf][g]
                for which in range(2):
                    cols = slice(which * DH, (which + 1) * DH)
                    for k in range(KD):
                        mm = three_pass(bank(proj_bank(buf, g))[:, which * T:which * T + T], hi[:, k, cols],
                                        lo[:, k, cols], hT_hi[:, k, :], hT_lo[:, k, :], k == 0, k == KD - 1)
                mm.then_inc(S("qk_ready"), 1)

            def project_v(h, buf):
                pe.wait_ge(S("w_v_low"), h + 1)
                lo = w_v_lo[buf]
                for c in range(TC):
                    pe.wait_ge(S("qk_copied"), GROUPS * h + 2 + c)
                    rows = slice(c * P, (c + 1) * P)
                    for k in range(KD):
                        mm = three_pass(bank(proj_bank(buf, GROUPS + c))[:, 0:GROUPS * DH], hT_hi[:, k, rows],
                                        hT_lo[:, k, rows], w_v_hi[:, k, :], lo[:, k, :], k == 0, k == KD - 1)
                    mm.then_inc(S("v_ready"), 1)

            def scores(h, buf, first=False):
                pe.wait_ge(S("qk_copied"), GROUPS * h + GROUPS)
                if not first:
                    pe.wait_ge(S("s_taken"), h)
                for g in range(GROUPS):
                    q, k = a_qk[buf][:, g, 0:T], a_qk[buf][:, g, T:2 * T]
                    dst = bank(3)[:, 2 * P * g:2 * P * g + 2 * P] if g < 2 else bank(4)[:, 0:2 * P]
                    pe.matmul(bank(2)[:, P * g:P * g + P], q[:, 0:P], k[:, 0:P], start=True, stop=True)
                    mm = pe.matmul(dst, q[:, P:T], k, start=True, stop=True)
                mm.then_inc(S("s_ready"), 1)

            def turn(h, first=False):
                pe.wait_ge(S("p_ready"), 2 * h + 2)
                for b in range(3):
                    if b == 2:
                        pe.wait_ge(S("pT_copied_a"), 2 * h + 1)
                    elif not first:
                        pe.wait_ge(S("pT_copied_a" if b == 0 else "pT_copied_d"), 2 * h if b == 0 else h)
                    for g in range(GROUPS):
                        src = a_s0[:, g, :] if b == 0 else a_s1[:, g, (b - 1) * P:b * P]
                        mm = pe.transpose(bank(6 if b == 1 else 5)[:, g * P:(g + 1) * P], src, ident)
                    mm.then_inc(S("pT_ready"), 1)

            def weigh(h, buf, first=False):
                pe.wait_ge(S("v_copied"), TC * h + TC)
                pe.wait_ge(S("pT_copied_a"), 2 * h + 2)
                pe.wait_ge(S("pT_copied_d"), h + 1)
                if not first:
                    pe.wait_ge(S("o_copied"), h)
                for g in range(GROUPS):
                    pe.matmul(bank(7)[:, 0:P], a_v[buf][:, g, 0:P], a_pT[:, g, :], start=(g == 0), stop=(g == GROUPS - 1))
                for g in range(GROUPS):
                    for kc in range(2):
                        mm = pe.matmul(bank(7)[:, P:2 * P], a_v[buf][:, g, kc * P:(kc + 1) * P],
                                       a_pT[:, 3 + 3 * kc + g, :], start=(g == 0 and kc == 0),
                                       stop=(g == GROUPS - 1 and kc == 1))
                mm.then_inc(S("o_ready"), 1)

            def step(h_att, h_proj, buf, first=False):
                scores(h_att, 1 - buf, first)
                project_qk(h_proj, 0, buf)
                project_qk(h_proj, 1, buf)
                turn(h_att, first)
                project_qk(h_proj, 2, buf)
                weigh(h_att, 1 - buf, first)
                project_v(h_proj, buf)

            for c in range(TC):
                turn_rows(0, c)
            pe.wait_ge(S("hT_low"), TC)
            for g in range(GROUPS):
                project_qk(0, g, 0, first=True)
            project_v(0, 0)
            step(0, 1, 1, first=True)
            with pe.Fori(0, HEADS // 2 - 1) as it:
                step(2 * it + 1, 2 * it + 2, 0)
                step(2 * it + 2, 2 * it + 3, 1)
            def mix_part(l, o, c, n, ks, last=True):
                t = (Tiles.DSA_OUT, Tiles.MLA_OUT)[l] + n
                for k in ks:
                    mm = pe.matmul(bank(2 * c + n), o[:, k, c * P:(c + 1) * P], tile(t, KD, 512)[:, k, :],
                                   start=(k == 0), stop=(k == KD - 1))
                if last:
                    mm.then_inc(S("mix_out"), 1)

            for n in range(2):
                wait_tile(pe, Tiles.DSA_OUT + n)
            scores(HEADS - 1, 1)
            pe.wait_ge(S("v_copied"), TC * HEADS)
            pe.wait_ge(S("o_copied"), HEADS - 1)
            mix_part(0, a_o, 0, 0, range(KD - 1), last=False)
            turn(HEADS - 1)
            mix_part(0, a_o, 0, 1, range(KD - 1), last=False)
            weigh(HEADS - 1, 1)
            pe.wait_ge(S("o_copied"), HEADS)

            def gather(l, grp, half):
                for k in range(4):
                    for c in range(TC):
                        mm = pe.matmul(bank(7)[:, k * P:(k + 1) * P], hs[:, c, 4 * half + k, :],
                                       e_oneh[:, c, bass.ds(P * grp, P)], start=(c == 0), stop=(c == TC - 1))
                mm.then_inc(S("gathered"), 1)

            def experts(l):
                i, o = 3 * l + 1, (a_o, m_o)[l]
                low = cst[:, C_LOW:C_LOW + P]
                all_ones = ones.to_broadcast([P, P])

                def logits(c):
                    pe.wait_ge(S("hT_ready"), 4 * i + 2 * c + 2)
                    pe.wait_ge(S("router_in"), 16 * (l + 1))
                    for k in range(KD):
                        mm = pe.matmul(bank(4)[:, c * NR:(c + 1) * NR], hT[:, k, c * P:(c + 1) * P], r_w[:, k, :],
                                       start=(k == 0), stop=(k == KD - 1))
                    mm.then_inc(S("logits_ready"), 1)

                def ranks(c):
                    pe.wait_ge(S("choice_ready"), TC * l + c + 1)
                    terms = [(all_ones, d) for d in range(c)] + [(low, c)]
                    sums = [(NE * c, terms)] + ([(2 * NE, [(all_ones, d) for d in range(TC)])] if c == TC - 1 else [])
                    for at, terms in sums:
                        for n, (w, m) in enumerate((w, m[:, d, :]) for w, d in terms for m in (r_m0, r_m1)):
                            mm = pe.matmul(bank(5)[:, at:at + NE], w, m, start=(n == 0), stop=(n == 2 * len(terms) - 1))
                    mm.then_inc(S("ranks_ready"), 1)

                def seed(c):
                    pe.wait_ge(S("x_added"), 8 * l + 2 * c + 2)
                    for n in range(2):
                        mm = pe.matmul(bank(2 * c + n), ident, x_sb[:, c, 512 * n:512 * n + 512], start=True, stop=True)
                    return mm

                for n in range(2):
                    mix_part(l, o, 0, n, [KD - 1])
                mix_part(l, o, 1, 0, range(KD))
                turn_rows(i, 0)
                mix_part(l, o, 1, 1, range(KD // 2), last=False)
                logits(0)
                mix_part(l, o, 1, 1, range(KD // 2, KD))
                ranks(0)
                seed(0)
                turn_rows(i, 1)
                logits(1)
                seed(1).then_inc(S("scattered"), 1)
                ranks(1)
                pe.wait_ge(S("oneh_first"), TC * (l + 1))
                gather(l, 0, 0)
                pe.wait_ge(S("flag_ready"), l + 1)
                for a in range(4):
                    for c in range(TC):
                        col = (slot_of, wgt)[a // 2][:, c, a % 2:a % 2 + 1]
                        mm = pe.matmul(bank(5 + a // 2)[:, (a % 2) * T + c * P:(a % 2) * T + (c + 1) * P],
                                       col.to_broadcast([P, P]), ident, start=True, stop=True)
                mm.then_inc(S("rows_ready"), 1)
                pe.wait_ge(S("xT_ready"), 2 * (NGRP + 1) * l + 1)
                gather(l, 0, 1)
                pe.wait_ge(S("rows_copied"), l + 1)
                base = Tiles.MOE[l]
                xt0 = 2 * (NGRP + 1) * l
                with pe.Fori(0, ITERS) as it:
                    for i in range(BODY):
                        e = NE * l + BODY * it + i
                        grp = (BODY // GE) * it + i // GE
                        t = base + 3 * i
                        more = (3 * BODY // RING) * it
                        xT = e_xT[(i // GE) % 2][:, :, CW * (i % GE):CW * (i % GE) + CW]
                        if i % GE == 0:
                            pe.wait_ge(S("xT_ready"), xt0 + 2 * grp + 2)
                        for j, b in ((0, 4), (1, 5)):
                            wait_tile(pe, t + j, more)
                            for k in range(KD):
                                for q in range(4):
                                    mm = pe.matmul(bank(b)[CW * q:CW * q + CW, 0:P], xT[:, k, :],
                                                   tile(t + j, KD, FF)[:, k, P * q:P * q + P],
                                                   start=(k == 0), stop=(k == KD - 1))
                            mm.then_inc(S("gate_ready" if j == 0 else "up_ready"), 1)
                        pe.wait_ge(S("h_ready"), e + 1)
                        pe.transpose(bank(5)[:, P:2 * P], e_h, ident).then_inc(S("hT_e"), 1)
                        pe.wait_ge(S("hT_copied"), e + 1)
                        wait_tile(pe, t + 2, more)
                        for j in range(FF // P):
                            for q in range(4):
                                mm = pe.matmul(bank(6)[CW * q:CW * q + CW, 0:T], e_hT[:, CW * j:CW * j + CW],
                                               tile(t + 2, FF // P, D)[:, j, T * q:T * q + T],
                                               start=(j == 0), stop=(j == FF // P - 1))
                        mm.then_inc(S("down_ready"), 1)
                        if i % GE in (1, 2):
                            pe.wait_ge(S("oneh_ready"), TC * (l + 1))
                            pe.wait_ge(S("xT_ready"), xt0 + 2 * grp + 2 + (i % GE - 1))
                            gather(l, grp + 1, i % GE - 1)
                        pe.wait_ge(S("y_copied_d"), e + 1)
                        pe.wait_ge(S("y_copied_a"), e + 1)
                        if i % GE == GE - 1:
                            pe.wait_ge(S("sc_ready"), NGRP * l + grp + 1)
                            for c in range(TC):
                                for n in range(2):
                                    mm = pe.matmul(bank(2 * c + n), e_sc[:, c * P:(c + 1) * P],
                                                   e_y[:, 512 * n:512 * n + 512], start=False, stop=True,
                                                   skip_group_check=True)
                            mm.then_inc(S("scattered"), 1)

                pe.wait_ge(S("flag_ready"), l + 1)
                count = pe.value_load(flag[0:1, l:l + 1], min_val=0, max_val=T)
                with pe.If(count > CAP):
                    with pe.Fori(0, NE) as e:
                        for j, b in ((0, 4), (1, 6)):
                            pe.wait_ge(S(f"o_landed{l}"), 16 * (3 * e + j + 1))
                            for c in range(TC):
                                for k in range(KD):
                                    mm = pe.matmul(bank(b + c), hT[:, k, c * P:(c + 1) * P], e_wide[:, k, :],
                                                   start=(k == 0), stop=(k == KD - 1))
                                mm.then_inc(S(f"o_gate{l}" if j == 0 else f"o_up{l}"), 1)
                        pe.wait_ge(S(f"o_landed{l}"), 16 * (3 * e + 3))
                        for c in range(TC):
                            pe.wait_ge(S(f"o_h{l}"), TC * e + c + 1)
                            for j in range(FF // P):
                                mm = pe.transpose(bank(4)[:, j * P:(j + 1) * P], o_sil[:, c, j * P:(j + 1) * P], ident)
                            mm.then_inc(S(f"o_turned{l}"), 1)
                            pe.wait_ge(S(f"o_hT{l}"), TC * e + c + 1)
                            for n in range(2):
                                for j in range(FF // P):
                                    mm = pe.matmul(bank(2 * c + n), o_hT[:, j, :], e_wide_d[:, j, 512 * n:512 * n + 512],
                                                   start=False, stop=True, skip_group_check=True)
                        mm.then_inc(S(f"o_down{l}"), 1)

            def ple(l):
                pe.wait_ge(S("pT_in"), 16 * (l + 1))
                wait_tile(pe, Tiles.PLE[l])
                for c in range(TC):
                    pe.wait_ge(S("y_taken_d"), TC * l + c + 1)
                    pe.wait_ge(S("y_taken_a"), TC * l + c + 1)
                    for n in range(2):
                        for k in range(PLE // P):
                            mm = pe.matmul(bank(2 * c + n), e_pT[:, k, c * P:(c + 1) * P],
                                           tile(Tiles.PLE[l], PLE // P, D)[:, k, 512 * n:512 * n + 512],
                                           start=(k == 0), stop=(k == PLE // P - 1))
                        mm.then_inc(S("pw_ready"), 1)
                    turn_rows(3 * l + 2, c)
                for c in range(TC):
                    pe.wait_ge(S("hT_ready"), 4 * (3 * l + 2) + 2 * c + 2)
                    for n in range(2):
                        if c == 0:
                            wait_tile(pe, Tiles.PLE[l] + 1 + n)
                        for k in range(KD):
                            mm = pe.matmul(bank(4 + 2 * c + n), hT[:, k, c * P:(c + 1) * P],
                                           tile(Tiles.PLE[l] + 1 + n, KD, 512)[:, k, :],
                                           start=(k == 0), stop=(k == KD - 1))
                        mm.then_inc(S("pg_ready"), 1)
                        if l == 0 and c == 1 and n == 0:
                            turn_rows(3, 0)

            experts(0)
            ple(0)

            wait_tile(pe, Tiles.MLA)
            for c in range(TC):
                if c == 1:
                    turn_rows(3, 1)
                pe.wait_ge(S("hT_ready"), 12 + 2 * c + 2)
                for k in range(KD):
                    mm = pe.matmul(bank(c)[:, 0:MLA_IN], hT[:, k, c * P:(c + 1) * P],
                                   tile(Tiles.MLA, KD, MLA_IN)[:, k, :], start=(k == 0), stop=(k == KD - 1))
                mm.then_inc(S("lat_ready"), 1)
            pe.wait_ge(S("ln_ready"), 4)
            for c in range(TC):
                for k in range(QL // P):
                    pe.transpose(bank(2, 2, T)[:, k, c * P:(c + 1) * P], m_lat[:, c, k * P:(k + 1) * P], ident)
                pe.transpose(bank(3)[:, c * P:(c + 1) * P], m_lat[:, c, QL:QL + KVL], ident)
            pe.wait_ge(S("kr_ready"), 1)
            for c in range(TC):
                mm = pe.transpose(bank(3)[0:QK, T + c * P:T + (c + 1) * P], m_kr[:, c, :], ident)
            mm.then_inc(S("lnT"), 1)
            pe.wait_ge(S("lnT_copied"), 3)
            wait_tile(pe, Tiles.MLA + 1)
            for c in range(TC):
                b = 4 if c == 0 else 0
                for n in range(3):
                    for k in range(QL // P):
                        mm = pe.matmul(bank(b + n), m_qlT[:, k, c * P:(c + 1) * P],
                                       tile(Tiles.MLA + 1, QL // P, MH * QK)[:, k, 512 * n:512 * n + 512],
                                       start=(k == 0), stop=(k == QL // P - 1))
                mm.then_inc(S("q_ready"), 1)
            wait_tile(pe, Tiles.MLA + 2)
            kvb = tile(Tiles.MLA + 2, MH, NOPE + MV)
            for j in range(MH // 2):
                if j >= 2:
                    pe.wait_ge(S("k_copied"), j - 1)
                for h2 in range(2):
                    mm = pe.matmul(bank(3 + 4 * (j % 2), 2, T)[0:NOPE, h2, :], kvb[:, 2 * j + h2, 0:NOPE], m_kvT,
                                   start=True, stop=True)
                mm.then_inc(S("k_ready"), 1)
            for c in range(TC):
                b = 4 if c == 0 else 0
                pe.wait_ge(S("q_copied_d" if c == 0 else "q_copied_a"), 1)
                for n in range(2):
                    mm = pe.matmul(bank(b + n), m_kvT[:, c * P:(c + 1) * P],
                                   kvb[:, 8 * n:8 * n + 8, NOPE:NOPE + MV], start=True, stop=True)
                mm.then_inc(S("mv_ready"), 1)
            pe.wait_ge(S("q_rot"), 4)
            for j in range(MH // 2):
                if j >= 2:
                    pe.wait_ge(S("qT_copied_a" if j % 2 else "qT_copied_d"), j // 2)
                for h2 in range(2):
                    for c in range(TC):
                        mm = pe.transpose(bank(6 if j % 2 else 2, 2, T)[0:QK, h2, c * P:(c + 1) * P],
                                          m_q[:, c, QK * (2 * j + h2):QK * (2 * j + h2) + QK], ident)
                mm.then_inc(S("qT_ready"), 1)
            pe.wait_ge(S("qT_copied_a"), MH // 4)
            pe.wait_ge(S("qT_copied_d"), MH // 4)
            pe.wait_ge(S("k_copied"), MH // 2)
            pe.wait_ge(S("mv_copied"), TC)

            def m_scores(j):
                for h2 in range(2):
                    q, k = m_qT[0:QK, 2 * j + h2, :], m_kT[0:QK, 2 * j + h2, :]
                    b = (5 if j % 2 else 0) + h2
                    pe.matmul(bank(b)[:, 0:P], q[:, 0:P], k[:, 0:P], start=True, stop=True)
                    mm = pe.matmul(bank(b)[:, P:3 * P], q[:, P:T], k, start=True, stop=True)
                mm.then_inc(S("m_s_ready"), 1)

            m_scores(0)
            for j in range(MH // 2):
                if j + 1 < MH // 2:
                    m_scores(j + 1)
                else:
                    for n in range(2):
                        wait_tile(pe, Tiles.MLA_OUT + n)
                    pe.wait_ge(S("m_o_copied"), j)
                    mix_part(1, m_o, 0, 0, range(KD - 1), last=False)
                pe.wait_ge(S("m_p"), j + 1)
                if j >= 1:
                    pe.wait_ge(S("m_pT_copied_a"), j)
                    pe.wait_ge(S("m_pT_copied_d"), j)
                for h2 in range(2):
                    for b in range(3):
                        mm = pe.transpose(bank(2 + h2)[:, b * P:(b + 1) * P], m_s[j % 2][:, h2, b * P:(b + 1) * P], ident)
                mm.then_inc(S("m_pT_ready"), 1)
                if j == MH // 2 - 1:
                    mix_part(1, m_o, 0, 1, range(KD - 1), last=False)
                pe.wait_ge(S("m_pT_copied_a"), j + 1)
                pe.wait_ge(S("m_pT_copied_d"), j + 1)
                if j >= 1:
                    pe.wait_ge(S("m_o_copied"), j)
                for h2 in range(2):
                    dst = bank(4)[MV * h2:MV * h2 + MV, :]
                    v = [m_v[:, c, MV * (2 * j + h2):MV * (2 * j + h2) + MV] for c in range(TC)]
                    pT = m_pT[j % 2][:, h2, :]
                    pe.matmul(dst[:, 0:P], v[0], pT[:, 0:P], start=True, stop=True)
                    pe.matmul(dst[:, P:T], v[0], pT[:, P:2 * P], start=True, stop=False)
                    mm = pe.matmul(dst[:, P:T], v[1], pT[:, 2 * P:3 * P], start=False, stop=True)
                mm.then_inc(S("m_o_ready"), 1)
            pe.wait_ge(S("m_o_copied"), MH // 2)
            experts(1)
            ple(1)


def kernel(**inputs):
    import concourse.bacc as bacc
    from concourse.bass_utils import run_bass_kernel_spmd

    a = {n: np.ascontiguousarray(v) for n, v in inputs.items()}
    gains = [a[n][l] for l in range(2) for n in ("norm_mix", "norm_moe", "norm_ple")]
    routers = [np.concatenate([a["moe_w_group"][l], a["moe_w_expert"][l]], axis=1) for l in range(2)]
    arrays = {
        "x": a["x"],
        "consts": shape_constants(),
        "distances": distance_table(),
        "gains": np.ascontiguousarray(np.concatenate(
            [g.reshape(P, KD) for g in gains]
            + [a["mla_q_norm"].reshape(-1, P).T, a["mla_kv_norm"].reshape(-1, P).T], axis=1)),
        "routers": np.stack([r.reshape(P, KD * NR) for r in routers]),
        "rows": np.concatenate([a["moe_b_group"][0], a["moe_b_expert"][0], a["moe_b_group"][1],
                                a["moe_b_expert"][1], a["norm_final"]]).reshape(1, -1),
        "p_t": np.ascontiguousarray(a["p"][:, 0].transpose(0, 2, 1)),
    }
    for n in ("dsa_w_in", "dsa_w_out", "mla_w_in", "mla_w_qb", "mla_w_kvb", "mla_w_out", "moe_w_gate", "moe_w_up",
              "moe_w_down", "ple_w", "ple_w_gate"):
        arrays[n] = a[n]
    nc = bacc.Bacc("TRN2", target_bir_lowering=False, num_devices=1)
    args = {n: nc.dram_tensor(n, v.shape, mybir.dt.from_np(v.dtype), kind="ExternalInput").ap()
            for n, v in arrays.items()}
    args["out"] = nc.dram_tensor("out", a["x"].shape, F32, kind="ExternalOutput").ap()
    build(nc, **args)
    r = run_bass_kernel_spmd(nc, [arrays], core_ids=[0])
    return r.results[0]["out"]
```

```python
from contextlib import ExitStack

import numpy as np

import concourse.bass as bass
from concourse import mybir

F32 = mybir.dt.float32
F32R = mybir.dt.float32r
I32 = mybir.dt.int32
U32 = mybir.dt.uint32
ALU = mybir.AluOpType
ACT = mybir.ActivationFunctionType
AX = mybir.AxisListType

P = 128
T = 256
TC = T // P
D = 1024
KD = D // P
EPS = 1e-6
BIG = 1.0e30

GROUPS, HEADS, DH = 3, 8, 128
PATTERNS = ((128, 1), (512, 4), (2048, 16))
DSA_SCALE = DH ** -0.5
MH, NOPE, ROPE, MV = 16, 64, 32, 64
QK = NOPE + ROPE
QL, KVL = 256, 128
MLA_IN = QL + KVL + ROPE
MLA_SCALE = QK ** -0.5
HALF = ROPE // 2
NG, EPG, NE, FF = 4, 8, 32, 512
NR = NG + NE
CW = 32
CAP = 32
GE = P // CW
NGRP = NE // GE
NSLOT = (NGRP + 1) * P
BODY = 8
ITERS = NE // BODY
PLE = 256

RING = 8
SLOT = 4096
BESIDE = 3
DSLOTS = 6
DTILES = GROUPS + 1
QK_TILE = KD * 2 * DH
V_TILE = KD * GROUPS * DH
HEAD_AREA = GROUPS * QK_TILE + V_TILE
HI_V = 0
HI_QK = HI_V + V_TILE
ODD_HEADS = HI_QK + QK_TILE
EVEN_HEADS = ODD_HEADS + HEAD_AREA
HI_OUT = 2
assert EVEN_HEADS <= (DSLOTS - HI_OUT) * SLOT and EVEN_HEADS + HEAD_AREA <= DSLOTS * SLOT


class Tiles:
    DSA_OUT = 0
    MOE = [DSA_OUT + 2, 0]
    PLE = [MOE[0] + 3 * NE, 0]
    MLA = PLE[0] + 3
    MLA_OUT = MLA + 3
    MOE[1] = MLA_OUT + 2
    PLE[1] = MOE[1] + 3 * NE

    @staticmethod
    def slot(t):
        return (t + DSLOTS) % RING

    @staticmethod
    def fills(t):
        return t // RING + 1

    @staticmethod
    def free(t):
        if t >= RING:
            return Tiles.used(t - RING)
        if t < Tiles.MOE[0]:
            return None
        if Tiles.slot(t) < DSLOTS - HI_OUT:
            return "v_ready", TC * HEADS
        return "mix_out", TC + 1 + Tiles.slot(t) - (DSLOTS - HI_OUT)

    @staticmethod
    def used(t):
        if t < Tiles.MOE[0]:
            return "mix_out", TC + 1 + t - Tiles.DSA_OUT
        if Tiles.MLA <= t < Tiles.MLA_OUT:
            return ("lat_ready", "q_ready", "mv_ready")[t - Tiles.MLA], TC
        if Tiles.MLA_OUT <= t < Tiles.MOE[1]:
            return "mix_out", 3 * TC + 1 + t - Tiles.MLA_OUT
        l = 1 if t >= Tiles.MOE[1] else 0
        if t < Tiles.PLE[l]:
            n = t - Tiles.MOE[l]
            return ("gate_ready", "up_ready", "down_ready")[n % 3], NE * l + n // 3 + 1
        n = t - Tiles.PLE[l]
        return ("pw_ready", 2 * TC * (l + 1)) if n == 0 else ("pg_ready", 2 * TC * l + TC * n)


C_ID, C_LOW, C_CAUSAL = 0, 128, 256
C_SLOPE = C_CAUSAL + 384
C_SLOT = C_SLOPE + GROUPS * HEADS
C_EID = C_SLOT + NGRP
C_GID = C_EID + NE
C_COS = C_GID + NE
C_SIN = C_COS + TC * HALF
C_END = C_SIN + TC * HALF
W_GAIN = 0
W_QG = 6 * KD
W_KVG = W_QG + QL // P
W_END = W_KVG + 1


def shape_constants():
    c = np.zeros((P, C_END), np.float32)
    p = np.arange(P)
    c[:, C_ID:C_ID + P] = np.eye(P)
    c[:, C_LOW:C_LOW + P] = p[:, None] < p[None, :]
    tri = np.where(p[None, :] <= p[:, None], 0.0, -BIG)
    c[:, C_CAUSAL:C_CAUSAL + P] = tri
    c[:, C_CAUSAL + 2 * P:C_CAUSAL + 3 * P] = tri
    n = GROUPS * HEADS
    slopes = 2.0 ** (-8.0 * np.arange(1, n + 1) / n)
    c[:, C_SLOPE:C_SLOPE + n] = (slopes / DSA_SCALE).reshape(GROUPS, HEADS).T.reshape(1, n)
    c[:, C_SLOT:C_SLOT + NGRP] = 1 + p[:, None] + P * np.arange(NGRP)[None, :]
    c[:, C_EID:C_EID + NE] = np.arange(NE)
    c[:, C_GID:C_GID + NE] = np.arange(NE) // EPG
    inv = 10000.0 ** (-np.arange(HALF, dtype=np.float32) / HALF)
    ang = (np.arange(T, dtype=np.float32)[:, None] * inv.astype(np.float32)).reshape(TC, P, HALF).transpose(1, 0, 2)
    c[:, C_COS:C_COS + TC * HALF] = np.cos(ang).reshape(P, -1)
    c[:, C_SIN:C_SIN + TC * HALF] = np.sin(ang).reshape(P, -1)
    return c


def distance_table():
    d = np.zeros((P, GROUPS, 2 * P), np.float32)
    delta = np.arange(P)[:, None] + P - np.arange(2 * P)[None, :]
    for g, (window, dil) in enumerate(PATTERNS):
        seen = (delta >= 0) & (delta <= window) & (delta % dil == 0)
        d[:, g] = np.where(seen, -delta, -BIG)
    return d.reshape(P, -1)


class Link:

    def __init__(self, eng, sem):
        self.eng, self.sem, self.n, self.base = eng, sem, 0, 0

    def __call__(self, ins):
        self.n += 1
        ins.then_inc(self.sem, 1)
        self.eng.wait_ge(self.sem, self.base + self.n)

    def enter(self, it, per):
        self.base, self.before, self.per = it * per, self.n, per

    def leave(self, passes):
        assert self.n - self.before == self.per, (self.n - self.before, self.per)
        self.base, self.n = 0, self.before + passes * self.per


def build(nc, x, out, consts, distances, gains, routers, rows, p_t, dsa_w_in, dsa_w_out, mla_w_in, mla_w_qb,
          mla_w_kvb, mla_w_out, moe_w_gate, moe_w_up, moe_w_down, ple_w, ple_w_gate):
    ctx = ExitStack()
    with ctx:
        def sb(name, shape, dt=F32):
            return ctx.enter_context(nc.sbuf_tensor(name, shape, dt))

        sems = {}

        def S(name):
            if name not in sems:
                sems[name] = ctx.enter_context(nc.semaphore(name))
            return sems[name]

        def sb_at(name, shape):
            at = -(-nc.sbuf_base // 32) * 32
            return sb(name, shape), at

        def one_pass(name, base, at, *dims):
            return nc.alloc_sbuf_tensor_at(name, [P, *dims], F32R, offset=base + 4 * at)[(slice(None),) * (1 + len(dims))]

        ring, ring_at = sb_at("ring", [P, RING, SLOT])
        x_sb = sb("x_sb", [P, TC, D])
        hs, hs_at = sb_at("hs", [P, TC, KD, P])
        hT, hT_at = sb_at("hT", [P, KD, T])
        cst = sb("cst", [P, C_END])
        wts = sb("wts", [P, W_END])
        small = sb("small", [P, 256])
        small_u = sb("small_u", [P, 64], U32)
        flag = sb("flag", [1, 2], I32)
        SCR = 13056
        scr, scr_at = sb_at("scr", [P, SCR])
        ps = ctx.enter_context(nc.psum_tensor("ps", [P, 8, 512], F32))

        ident = cst[:, C_ID:C_ID + P]

        def part(ap, at, *dims):
            n = 1
            for d in dims:
                n *= d
            v = ap[:, at:at + n]
            if len(dims) == 2:
                v = v.rearrange("p (a b) -> p a b", b=dims[1])
            elif len(dims) == 3:
                v = v.rearrange("p (a b c) -> p a b c", b=dims[1], c=dims[2])
            return v

        def scratch(at, *dims):
            return part(scr, at, *dims)

        def tile(t, k, n, at=0):
            return ring[:, Tiles.slot(t), :][:, at:at + k * n].rearrange("p (k n) -> p k n", n=n)

        landed = [S(f"landed_{s}") for s in range(RING)]
        landed_dsa = [S(f"landed_dsa_{s}") for s in range(2 * DTILES)]

        def wait_tile(eng, t, more=0):
            eng.wait_ge(landed[Tiles.slot(t)], 16 * (Tiles.fills(t) + more))

        a_qk = [scratch(0, GROUPS, 512), scratch(1536, GROUPS, 512)]
        a_v = [scratch(3072, GROUPS, T), scratch(3840, GROUPS, T)]
        a_s0 = scratch(4608, GROUPS, P)
        a_s1 = scratch(4992, GROUPS, 2 * P)
        a_o = scratch(5760, HEADS, T)
        a_pT = scratch(7808, 9, P)
        a_dist = scratch(8960, GROUPS, 2 * P)
        ring_flat = ring[:, :, :].rearrange("p s n -> p (s n)")

        def qk_at(par, g):
            return (EVEN_HEADS, ODD_HEADS)[par] + QK_TILE * g

        def v_at(par):
            return (EVEN_HEADS, ODD_HEADS)[par] + GROUPS * QK_TILE

        w_qk = [[part(ring_flat, qk_at(par, g), KD, 2 * DH) for g in range(GROUPS)] for par in range(2)]
        w_v = [part(ring_flat, v_at(par), KD, GROUPS * DH) for par in range(2)]
        w_qk_lo = [[one_pass(f"w_qk_lo_{par}_{g}", ring_at, qk_at(par, g), KD, 2 * DH) for g in range(GROUPS)]
                   for par in range(2)]
        w_v_lo = [one_pass(f"w_v_lo_{par}", ring_at, v_at(par), KD, GROUPS * DH) for par in range(2)]
        w_qk_hi = [one_pass("w_qk_hi_0", ring_at, HI_QK, KD, 2 * DH), one_pass("w_qk_hi_1", scr_at, 10496, KD, 2 * DH)]
        w_v_hi = one_pass("w_v_hi", ring_at, HI_V, KD, GROUPS * DH)
        w_out_hi = [one_pass(f"w_out_hi_{n}", ring_at, SLOT * (DSLOTS - HI_OUT + n), KD, 512) for n in range(2)]
        w_out_lo = [one_pass(f"w_out_lo_{n}", ring_at, SLOT * Tiles.slot(Tiles.DSA_OUT + n), KD, 512) for n in range(2)]
        a_o_hi = one_pass("a_o_hi", scr_at, 10496, HEADS, T)
        a_o_lo = one_pass("a_o_lo", scr_at, 5760, HEADS, T)
        hT_hi = one_pass("hT_hi", hs_at, 0, TC, KD, P)
        hT_lo = one_pass("hT_lo", hT_at, 0, KD, T)
        m_qT = scratch(0, MH, T)
        m_kT = scratch(4096, MH, T)
        m_q = scratch(8192, TC, MH * QK)
        m_pT = [scratch(8192, 2, 384), scratch(8960, 2, 384)]
        m_o = scratch(9728, KD, T)
        m_lat = scratch(11264, TC, MLA_IN)
        m_kr = scratch(12096, TC, QK)
        hs_flat = hs[:, :, :, :].rearrange("p c k t -> p (c k t)")
        m_qlT = part(hs_flat, 0, QL // P, T)
        m_kvT = hs_flat[:, 512:512 + T]
        m_s = [part(hs_flat, 0, 2, 384), part(hs_flat, 768, 2, 384), scratch(11776, 2, 384)]
        m_rope_k = scratch(12288, 8, HALF)
        m_rope = [scratch(11264 + T * j, MH, HALF) for j in range(4)]
        m_v = hT[:, :, :].rearrange("p k t -> p (k t)").rearrange("p (c n) -> p c n", c=TC)
        e_oneh = scratch(0, TC, NSLOT)
        e_xT = [scratch(2304, KD, P), scratch(3328, KD, P)]
        e_wide = scratch(0, KD, 512)
        e_wide_d = scratch(0, FF // P, D)
        e_y = scratch(4352, D)
        e_iota = scratch(5376, NSLOT)
        e_rows = scratch(6528, 4, T)
        e_sc = scratch(7552, T)
        e_sc2 = scratch(9224, T)
        e_sil = scratch(7808, P)
        e_h = scratch(7936, P)
        e_hT = scratch(8064, P)
        r_lg = scratch(8192, TC, NR)
        r_em = scratch(8264, TC, NE)
        r_m0 = scratch(8328, TC, NE)
        r_m1 = scratch(8392, TC, NE)
        r_m = scratch(8456, TC, NE)
        r_wo = scratch(8520, TC, NE)
        r_junk = scratch(8584, P)
        e_pT = scratch(8712, PLE // P, T)
        p_gate = scratch(9224, TC, D)
        g_hi = [one_pass(f"g_hi_{n}", scr_at, 4096 * n, KD, 512) for n in range(2)]
        assert all(Tiles.slot(Tiles.PLE[0] + n) == Tiles.slot(Tiles.PLE[1] + n) for n in range(3))
        g_lo = [one_pass(f"g_lo_{n}", ring_at, SLOT * Tiles.slot(Tiles.PLE[0] + 1 + n), KD, 512) for n in range(2)]
        o_sil = scratch(9224, TC, 512)
        o_hT = scratch(10248, 4, P)
        r_w = scratch(12544, KD, NR)
        r_b = scratch(12544 + KD * NR, 2 * NR)
        junk_d, junk_a = [scratch(1024 * c, 512) for c in range(TC)], [scratch(1024 * c + 512, 512) for c in range(TC)]
        junk_pd, junk_pa = [p_gate[:, c, 0:512] for c in range(TC)], [p_gate[:, c, 512:D] for c in range(TC)]
        f_gain = scratch(11272, D)

        ss = part(small, 0, TC, 2)
        rstd = small[:, 134:136]
        root = small[:, 138:140]
        spare = iter(range(140, 200))
        a_mx, a_nmx, a_den = small[:, 4:6], small[:, 6:8], small[:, 8:10]
        m_ss = part(small, 12, TC, 2)
        m_rs = part(small, 16, TC, 2)
        m_mx = part(small, 20, 2, 2)
        m_nmx = [part(small, 200 + 4 * j, 2, 2) for j in range(3)]
        m_den = [part(small, 212 + 4 * j, 2, 2) for j in range(3)]
        gp8 = part(small, 40, TC, 8)
        gm8 = part(small, 56, TC, 8)
        ev8 = part(small, 72, TC, 8)
        ngm = small[:, 88:90]
        gsum = small[:, 90:92]
        eg4 = small[:, 92:96]
        gif = small[:, 96:98]
        ef = part(small, 98, TC, 2)
        dif = small[:, 102:104]
        rr = part(small, 104, TC, 2)
        fits = part(small, 108, TC, 2)
        wgt = part(small, 112, TC, 2)
        wov = part(small, 116, TC, 2)
        slot_of = part(small, 120, TC, 2)
        cmax = small[:, 124:125]
        w_in = part(small, 128, TC, 2)
        den1 = small[:, 132:134]
        ones = small[:, 136:137]
        m_t = [[m_rope_k[:, 4 * c + n, :] for n in range(4)] for c in range(TC)]
        gi8 = part(small_u, 0, TC, 8)
        ei8 = part(small_u, 16, TC, 8)

        def bank(b, *dims):
            v = ps[:, b, :]
            return v if not dims else part(v, 0, *dims)

        block = ctx.enter_context(nc.Block())

        dsa_in_v = dsa_w_in.rearrange("(p k) (g w n) -> g p k w n", k=KD, g=GROUPS, w=3)
        kp = lambda w, n: w.rearrange("(p k) (n j) -> n p k j", k=KD, j=n)
        dsa_out_v = dsa_w_out.rearrange("(k p) (n j) -> n p k j", p=P, j=512)
        mla_out_v = mla_w_out.rearrange("(k p) (n j) -> n p k j", p=P, j=512)

        @block.sync
        def _(sp):
            def wait_free(t, more=0):
                if Tiles.free(t) is not None:
                    sem, value = Tiles.free(t)
                    sp.wait_ge(S(sem), value + more)

            def load(t, src, k, n):
                wait_free(t)
                sp.dma_start(tile(t, k, n), src).then_inc(landed[Tiles.slot(t)], 16)

            def load_head(par, h, before=None):
                for g in range(GROUPS):
                    if before is not None:
                        sp.wait_ge(S("qk_ready"), GROUPS * before + g + 1)
                    for w in range(2):
                        sp.dma_start(w_qk[par][g][:, :, w * DH:(w + 1) * DH],
                                     dsa_in_v[g][:, :, w, bass.ds(DH * h, DH)]
                                     ).then_inc(landed_dsa[DTILES * par + g], 16)
                if before is not None:
                    sp.wait_ge(S("v_ready"), TC * before + TC)
                for g in range(GROUPS):
                    sp.dma_start(w_v[par][:, :, g * DH:(g + 1) * DH],
                                 dsa_in_v[g][:, :, 2, bass.ds(DH * h, DH)]
                                 ).then_inc(landed_dsa[DTILES * par + GROUPS], 16)

            for c in range(TC):
                sp.dma_start(x_sb[:, c, :], x[0, c * P:(c + 1) * P, :]).then_inc(S(f"x_in_{c}"), 16)
                if c == 0:
                    sp.dma_start(cst[:, C_ID:C_LOW], consts[:, C_ID:C_LOW]).then_inc(S("ident_in"), 16)
            for h in range(2):
                load_head(h, h)
            for n in range(2):
                load(Tiles.DSA_OUT + n, dsa_out_v[n], KD, 512)
            with sp.Fori(0, HEADS // 2 - 1) as it:
                for par in range(2):
                    load_head(par, 2 * it + 2 + par, before=2 * it + par)

            def expert_weights(l, e, j):
                one = (moe_w_gate, moe_w_up, moe_w_down)[j][l, bass.ds(e, 1), :, :]
                if j == 2:
                    return one.rearrange("e (j p) n -> p (e j) n", p=P)
                return one.rearrange("e (p k) n -> p (e k) n", k=KD)

            def load_expert_tile(l, n, it=0):
                t, j = Tiles.MOE[l] + n, n % 3
                wait_free(t, BODY * it)
                k, width = (FF // P, D) if j == 2 else (KD, FF)
                sp.dma_start(tile(t, k, width), expert_weights(l, n // 3 + BODY * it, j)
                             ).then_inc(landed[Tiles.slot(t)], 16)

            def load_experts(l):
                for n in range(RING):
                    load_expert_tile(l, n)
                with sp.Fori(0, ITERS - 1) as it:
                    for n in range(RING, RING + 3 * BODY):
                        load_expert_tile(l, n, it)
                for n in range(RING + 3 * BODY * (ITERS - 1), 3 * NE):
                    load_expert_tile(l, n)

            def load_ple(l):
                load(Tiles.PLE[l], ple_w[l].rearrange("(k p) n -> p k n", p=P), PLE // P, D)
                for n in range(2):
                    load(Tiles.PLE[l] + 1 + n, kp(ple_w_gate[l], 512)[n], KD, 512)

            def load_overflow(l):
                sp.wait_ge(S("flag_ready"), l + 1)
                count = sp.value_load(flag[0:1, l:l + 1], min_val=0, max_val=T)
                with sp.If(count > CAP):
                    sp.wait_ge(S("scattered"), (NGRP + 1) * (l + 1))
                    sp.sem_inc(S(f"o_down{l}"), 1)
                    with sp.Fori(0, NE) as e:
                        for j in range(3):
                            if j == 0:
                                sp.wait_ge(S(f"o_down{l}"), e + 1)
                            else:
                                sp.wait_ge(S(f"o_gate{l}" if j == 1 else f"o_up{l}"), TC * e + TC)
                            sp.dma_start(e_wide_d if j == 2 else e_wide, expert_weights(l, e, j)
                                         ).then_inc(S(f"o_landed{l}"), 16)

            load_experts(0)
            load_overflow(0)
            load_ple(0)
            load(Tiles.MLA, mla_w_in.rearrange("(p k) n -> p k n", k=KD), KD, MLA_IN)
            load(Tiles.MLA + 1, mla_w_qb.rearrange("(k p) n -> p k n", p=P), QL // P, MH * QK)
            load(Tiles.MLA + 2, mla_w_kvb.rearrange("(k p) n -> p k n", p=P), 1, MH * (NOPE + MV))
            for n in range(2):
                load(Tiles.MLA_OUT + n, mla_out_v[n], KD, 512)
            load_experts(1)
            load_overflow(1)
            load_ple(1)
            for c in range(TC):
                sp.wait_ge(S("final_ready"), c + 1)
                sp.dma_start(out[0, c * P:(c + 1) * P, :], x_sb[:, c, :]).then_inc(S("stored"), 16)
            sp.wait_ge(S("stored"), 16 * TC)

        @block.gpsimd
        def _(pool):
            pool.dma_start(wts[:, :], gains).then_inc(S("wts_in"), 16)
            pool.dma_start(cst[:, C_LOW:C_END], consts[:, C_LOW:C_END]).then_inc(S("cst_in"), 16)
            pool.dma_start(a_dist, distances.rearrange("p (g n) -> p g n", g=GROUPS)).then_inc(S("dist_in"), 16)
            pool.memset(gp8, -BIG).then_inc(S("fills"), 1)
            pool.memset(ones, 1.0).then_inc(S("fills"), 1)
            pool.dma_start(r_b, rows[0:1, 0:2 * NR].partition_broadcast(P)).then_inc(S("bias_in"), 16)
            for l in range(2):
                if l == 1:
                    pool.wait_ge(S("logits_ready"), TC)
                pool.dma_start(r_w, routers[l].rearrange("p (k n) -> p k n", k=KD)).then_inc(S("router_in"), 16)
                pool.wait_ge(S("mix_out"), 4 * (l + 1))
                pool.iota(e_iota, [[1, NSLOT]], base=1, channel_multiplier=0,
                          allow_small_or_imprecise_dtypes=True).then_inc(S("iota_ready"), 1)
                pool.dma_start(e_pT, p_t[l].rearrange("(k p) t -> p k t", p=P)).then_inc(S("pT_in"), 16)
                if l == 1:
                    pool.dma_start(f_gain, rows[0:1, 2 * NR:2 * NR + D].partition_broadcast(P)
                                   ).then_inc(S("f_gain_in"), 16)
                for c in range(TC):
                    pool.wait_ge(S("hT_high"), TC * (l + 1) + c + 1)
                    pool.tensor_tensor(hT_lo[:, :, c * P:(c + 1) * P], hT[:, :, c * P:(c + 1) * P],
                                       hT_hi[:, c, :, :].bitcast(F32), ALU.subtract).then_inc(S("hT_low"), 1)

        def dsa_fills(h, par, dmas):
            return 16 * dmas if isinstance(h, int) and h < 2 else 16 * dmas // 2 * (h - par) + 16 * dmas

        def proj_bank(par, n):
            return ((GROUPS + TC) * par + n) % 2

        def wait_x(eng, i, c, n):
            if i == 0:
                eng.wait_ge(S(f"x_in_{c}"), 16)
            elif i in (2, 5):
                eng.wait_ge(S("y_taken_a" if n else "y_taken_d"), TC * (i // 3) + c + 1)
            else:
                at = 2 * c + n if i in (1, 4) else 2 * n + c
                eng.wait_ge(S("x_added"), 4 * {1: 0, 3: 1, 4: 2, 6: 3}[i] + at + 1)

        @block.scalar
        def _(act):
            def table(func):
                at = next(spare)
                act.activation(small[0:1, at:at + 1], ones[0:1, :], func)

            def square(i, c):
                wait_x(act, i, c, 1)
                act.activation((junk_a if i in (0, 1, 4) else junk_pa)[c], x_sb[:, c, 512:D], ACT.Square, accum_out=ss[:, c, 1:2]).then_inc(S("sq_a"), 1)

            def scale(i, c):
                act.activation(hs[:, c, 4:8, :], x_sb[:, c, :].rearrange("p (t k) -> p k t", k=KD)[:, 4:8, :],
                               ACT.Copy, scale=rstd[:, c:c + 1]).then_inc(S("hs_a"), 1)

            def norm_together(i):
                for c in range(TC):
                    square(i, c)
                act.wait_ge(S("var_ready"), TC * i + TC)
                act.activation(root, root, ACT.Sqrt, scale=1.0 / D).then_inc(S("root_ready"), TC)
                act.wait_ge(S("rstd_ready"), TC * i + TC)
                for c in range(TC):
                    scale(i, c)

            def norm_chunk(i, c):
                square(i, c)
                act.wait_ge(S("var_ready"), TC * i + c + 1)
                act.activation(root[:, c:c + 1], root[:, c:c + 1], ACT.Sqrt, scale=1.0 / D).then_inc(S("root_ready"), 1)
                if i < 6:
                    act.wait_ge(S("rstd_ready"), TC * i + c + 1)
                    scale(i, c)

            def high_qk(h, g, par, first=False):
                n = GROUPS * h + g
                act.wait_ge(landed_dsa[DTILES * par + g], dsa_fills(h, par, 2))
                if not first:
                    act.wait_ge(S("qk_ready"), n - 1)
                act.copy(w_qk_hi[(GROUPS * par + g) % 2], w_qk[par][g]).then_inc(S("w_qk_high"), 1)

            def high_v(h, par, first=False):
                act.wait_ge(landed_dsa[DTILES * par + GROUPS], dsa_fills(h, par, GROUPS))
                if not first:
                    act.wait_ge(S("v_ready"), TC * h)
                act.copy(w_v_hi, w_v[par]).then_inc(S("w_v_high"), 1)

            def copy_qk(h, g, buf, first=False):
                act.wait_ge(S("qk_ready"), GROUPS * h + g + 1)
                if g == 0 and not first:
                    act.wait_ge(S("s_ready"), h - 1)
                act.copy(a_qk[buf][:, g, :], bank(proj_bank(buf, g))).then_inc(S("qk_copied"), 1)

            def attend(h):
                act.wait_ge(S("nmx_ready"), h + 1)
                s0 = a_s0.rearrange("p g n -> p (g n)")
                s1 = a_s1.rearrange("p g n -> p (g n)")
                act.activation(s0, s0, ACT.Exp, bias=a_nmx[:, 0:1], scale=DSA_SCALE,
                               accum_out=a_den[:, 0:1]).then_inc(S("e_ready"), 1)
                act.activation(s1, s1, ACT.Exp, bias=a_nmx[:, 1:2], scale=DSA_SCALE,
                               accum_out=a_den[:, 1:2]).then_inc(S("e_ready"), 1)

            def copy_pT(h):
                for b in (0, 2):
                    act.wait_ge(S("pT_ready"), 3 * h + b + 1)
                    act.copy(a_pT[:, 3 * b:3 * b + 3, :], bank(5, 4, P)[:, 0:3, :]).then_inc(S("pT_copied_a"), 1)

            def copy_o(h):
                act.wait_ge(S("o_ready"), h + 1)
                act.copy(a_o[:, bass.ds(h, 1), :].rearrange("p h t -> p (h t)"),
                         bank(7)[:, 0:T]).then_inc(S("o_copied"), 1)

            def step(h_att, h_proj, buf, first=False, last=False):
                attend(h_att)
                copy_qk(h_proj, 0, buf, first)
                high_qk(h_proj, 2, buf)
                high_v(h_proj, buf)
                copy_qk(h_proj, 1, buf)
                copy_pT(h_att)
                if not last:
                    high_qk(h_proj + 1, 0, 1 - buf)
                else:
                    act.wait_ge(S("v_ready"), TC * (HEADS - 1))
                    for n in range(2):
                        wait_tile(act, Tiles.DSA_OUT + n)
                        act.copy(w_out_hi[n], tile(Tiles.DSA_OUT + n, KD, 512)).then_inc(S("w_out_high"), 1)
                copy_qk(h_proj, 2, buf)
                if not last:
                    high_qk(h_proj + 1, 1, 1 - buf)
                copy_o(h_att)
                if last:
                    act.wait_ge(S("o_copied"), HEADS - 1)
                    act.copy(a_o_hi[:, 0:HEADS - 1, :], a_o[:, 0:HEADS - 1, :]).then_inc(S("o_high"), 1)

            act.wait_ge(S("fills"), 2)
            table(ACT.Sqrt)
            for c in range(TC):
                norm_chunk(0, c)
            for c in range(TC):
                act.wait_ge(S("hT_ready"), 2 * c + 2)
                act.copy(hT_hi[:, c, :, :], hT[:, :, c * P:(c + 1) * P]).then_inc(S("hT_high"), 1)
                if c == 0:
                    high_qk(0, 0, 0, first=True)
            high_qk(0, 1, 0, first=True)
            copy_qk(0, 0, 0, first=True)
            high_qk(0, 2, 0)
            high_v(0, 0, first=True)
            copy_qk(0, 1, 0, first=True)
            high_qk(1, 0, 1)
            copy_qk(0, 2, 0, first=True)
            high_qk(1, 1, 1)
            step(0, 1, 1, first=True)
            with act.Fori(0, HEADS // 2 - 2) as it:
                step(2 * it + 1, 2 * it + 2, 0)
                step(2 * it + 2, 2 * it + 3, 1)
            step(HEADS - 3, HEADS - 2, 0)
            step(HEADS - 2, HEADS - 1, 1, last=True)
            attend(HEADS - 1)
            copy_pT(HEADS - 1)
            act.wait_ge(S("o_ready"), HEADS)
            act.copy(a_o_hi[:, HEADS - 1, :], bank(7)[:, 0:T]).then_inc(S("o_high"), 1)

            def experts(l):
                for c in range(TC):
                    act.wait_ge(S("ngm_ready"), 2 * l + c + 1)
                    act.activation(eg4, r_lg[:, c, 0:NG], ACT.Exp, bias=ngm[:, c:c + 1],
                                   accum_out=gsum[:, c:c + 1]).then_inc(S("gsum_ready"), 1)
                    act.wait_ge(S("gsum_ready"), 2 * l + c + 1)
                act.wait_ge(S("dif_ready"), l + 1)
                act.activation(dif, dif, ACT.Exp).then_inc(S("dexp_ready"), 1)
                act.wait_ge(S("rows_ready"), l + 1)
                act.copy(e_rows.rearrange("p a t -> p (a t)"),
                         ps[:, 5:7, :].rearrange("p a b -> p (a b)")).then_inc(S("rows_copied"), 1)
                table(ACT.Silu)
                with act.Fori(0, ITERS) as it:
                    for i in range(BODY):
                        e = NE * l + BODY * it + i
                        act.wait_ge(S("gate_ready"), e + 1)
                        act.activation(e_sil, bank(4)[:, 0:P], ACT.Silu).then_inc(S("silu_ready"), 1)
                        act.wait_ge(S("down_ready"), e + 1)
                        if i % GE == 0:
                            grp = (NGRP + 1) * l + (BODY // GE) * it + i // GE
                            act.wait_ge(S("scattered"), grp + 1)
                        for q in (2, 3):
                            ins = act.copy(e_y[CW * (i % GE):CW * (i % GE) + CW, T * q:T * q + T],
                                           bank(6)[CW * q:CW * q + CW, 0:T])
                        ins.then_inc(S("y_copied_a"), 1)
                act.wait_ge(S("flag_ready"), l + 1)
                count = act.value_load(flag[0:1, l:l + 1], min_val=0, max_val=T)
                with act.If(count > CAP):
                    with act.Fori(0, NE) as e:
                        for c in range(TC):
                            act.wait_ge(S(f"o_gate{l}"), TC * e + c + 1)
                            act.activation(o_sil[:, c, :], bank(4 + c), ACT.Silu).then_inc(S(f"o_silu{l}"), 1)
                    act.wait_ge(S(f"o_down{l}"), NE + 1)
                table(ACT.Sqrt)
                for c in range(TC):
                    act.wait_ge(S("scattered" if c else "scattered_0"), (NGRP + c) * (l + 1))
                    act.copy(x_sb[:, c, 512:D], bank(2 * c + 1)).then_inc(S("y_taken_a"), 1)

            def ple(l):
                def high_gate(n):
                    t = Tiles.PLE[l] + 1 + n
                    wait_tile(act, t)
                    act.copy(g_hi[n], tile(t, KD, 512)).then_inc(S("g_high"), 1)

                def sigmoid(c, n):
                    act.wait_ge(S("pg_ready"), 4 * l + 2 * n + c + 1)
                    act.activation(p_gate[:, c, 512 * n:512 * n + 512], bank(4 + 2 * c + n),
                                   ACT.Sigmoid).then_inc(S("sig_ready"), 1)

                i = 3 * l + 2
                norm_together(i)
                high_gate(0)
                for c in range(TC):
                    act.wait_ge(S("hT_ready"), 4 * i + 2 * c + 2)
                    act.copy(hT_hi[:, c, :, :], hT[:, :, c * P:(c + 1) * P]).then_inc(S("hT_high"), 1)
                high_gate(1)
                table(ACT.Sigmoid)
                for c, n in ((0, 0), (1, 0), (0, 1)):
                    sigmoid(c, n)
                table(ACT.Sqrt)
                norm_chunk(3 * l + 3, 0)
                sigmoid(1, 1)
                table(ACT.Sqrt)
                norm_chunk(3 * l + 3, 1)

            table(ACT.Sqrt)
            for c in range(TC):
                norm_chunk(1, c)
            experts(0)
            ple(0)

            for c in range(TC):
                act.wait_ge(S("lat_ready"), c + 1)
                for j, (a, b) in enumerate(((0, QL), (QL, QL + KVL))):
                    ins = act.activation(junk_pa[c][:, a:b], bank(c)[:, a:b], ACT.Square, accum_out=m_ss[:, c, j:j + 1])
                ins.then_inc(S("lat_sq"), 1)
                act.wait_ge(S("lat_var"), c + 1)
                act.activation(m_rs[:, c, :], m_ss[:, c, :], ACT.Sqrt).then_inc(S("lat_root"), 1)
            act.wait_ge(S("lnT_copied"), 4)
            act.copy(m_kT[NOPE:QK, :, :], bank(3)[NOPE:QK, T:2 * T].unsqueeze(1).to_broadcast([ROPE, MH, T])
                     ).then_inc(S("kr_spread"), 1)
            act.wait_ge(S("q_ready"), 2)
            act.copy(m_q[:, 1, :], ps[:, 0:3, :].rearrange("p a b -> p (a b)")).then_inc(S("q_copied_a"), 1)
            for j in range(MH // 2):
                act.wait_ge(S("k_ready"), j + 1)
                act.copy(m_kT[0:NOPE, 2 * j, :], bank(3 + 4 * (j % 2))[0:NOPE, 0:T]).then_inc(S("k_copied"), 1)
            def m_exps(j):
                act.wait_ge(S("m_nmx"), j + 1)
                for h2 in range(2):
                    for c, (a, b) in enumerate(((0, P), (P, 3 * P))):
                        ins = act.activation(m_s[j % 3][:, h2, a:b], m_s[j % 3][:, h2, a:b], ACT.Exp,
                                             bias=m_nmx[j % 3][:, c, h2:h2 + 1], scale=MLA_SCALE,
                                             accum_out=m_den[j % 3][:, c, h2:h2 + 1])
                ins.then_inc(S("m_exp"), 1)

            def m_copy_o(j):
                act.wait_ge(S("m_o_ready"), j + 1)
                act.copy(m_o[:, j, :], bank(4)[:, 0:T]).then_inc(S("m_o_copied"), 1)

            table(ACT.Exp)
            for j in range(1, MH // 2, 2):
                act.wait_ge(S("qT_ready"), j + 1)
                act.copy(m_qT[0:QK, 2 * j:2 * j + 2, :], bank(7, 2, T)[0:QK, :, :]).then_inc(S("qT_copied_a"), 1)
                if j in (5, 7):
                    m_exps((j - 5) // 2)
            for j in range(MH // 2):
                act.wait_ge(S("m_pT_ready"), j + 1)
                act.copy(m_pT[j % 2][:, 1, :], bank(3)[:, 0:384]).then_inc(S("m_pT_copied_a"), 1)
                if j + 2 < MH // 2:
                    m_exps(j + 2)
                if j >= 1:
                    m_copy_o(j - 1)
            m_copy_o(MH // 2 - 1)

            table(ACT.Sqrt)
            for c in range(TC):
                norm_chunk(4, c)
            experts(1)
            ple(1)

        @block.vector
        def _(dve):
            link = Link(dve, S("dve_link"))

            def square(i, c):
                wait_x(dve, i, c, 0)
                dve.tensor_tensor_reduce(out=(junk_d if i in (0, 1, 4) else junk_pd)[c], in0=x_sb[:, c, 0:512], in1=x_sb[:, c, 0:512], scale=1.0,
                                         scalar=0.0, op0=ALU.mult, op1=ALU.add,
                                         accum_out=ss[:, c, 0:1]).then_inc(S("sq_d"), 1)

            def roots(i, a, b):
                dve.wait_ge(S("sq_d"), TC * i + b)
                dve.wait_ge(S("sq_a"), TC * i + b)
                dve.scalar_tensor_tensor(out=root[:, a:b], in0=ss[:, a:b, 0], scalar=EPS * D, in1=ss[:, a:b, 1],
                                         op0=ALU.add, op1=ALU.add).then_inc(S("var_ready"), b - a)
                dve.wait_ge(S("root_ready"), TC * i + b)
                dve.reciprocal(rstd[:, a:b], root[:, a:b]).then_inc(S("rstd_ready"), b - a)
                dve.wait_ge(S("rstd_ready"), TC * i + b)

            def scale(i, c):
                dve.tensor_scalar(hs[:, c, 0:4, :], x_sb[:, c, :].rearrange("p (t k) -> p k t", k=KD)[:, 0:4, :],
                                  rstd[:, c:c + 1], None, ALU.mult).then_inc(S("hs_d"), 1)

            def gains_on(i, c):
                if i == 0:
                    dve.wait_ge(S("wts_in"), 16)
                gain = part(wts, W_GAIN + i * KD, KD)
                for b in range(2):
                    dve.wait_ge(S("hT_turned"), 4 * i + 2 * c + b + 1)
                    dve.tensor_tensor(hT[:, 4 * b:4 * b + 4, c * P:(c + 1) * P], bank(4 + 2 * c + b, 4, P),
                                      gain[:, 4 * b:4 * b + 4].unsqueeze(2).to_broadcast([P, 4, P]),
                                      ALU.mult).then_inc(S("hT_ready"), 1)

            def norm_together(i):
                for c in range(TC):
                    square(i, c)
                roots(i, 0, TC)
                for c in range(TC):
                    scale(i, c)
                for c in range(TC):
                    gains_on(i, c)

            def norm_staged(i, add, between, after=None):
                for c in range(TC):
                    for n in range(2):
                        add(c, n)
                        if n == 0:
                            square(i, c)
                        if c == 1 and n == 0:
                            gains_on(i, 0)
                            between()
                    roots(i, c, c + 1)
                    scale(i, c)
                if after is not None:
                    after()
                gains_on(i, 1)

            def low_qk(h, g, par):
                dve.wait_ge(S("w_qk_high"), GROUPS * h + g + 1)
                dve.tensor_tensor(w_qk_lo[par][g], w_qk[par][g],
                                  w_qk_hi[(GROUPS * par + g) % 2].bitcast(F32), ALU.subtract).then_inc(S("w_qk_low"), 1)

            def low_v(h, par):
                dve.wait_ge(S("w_v_high"), h + 1)
                dve.tensor_tensor(w_v_lo[par], w_v[par], w_v_hi.bitcast(F32),
                                  ALU.subtract).then_inc(S("w_v_low"), 1)

            def copy_v(h, buf, first=False):
                for c in range(TC):
                    dve.wait_ge(S("v_ready"), TC * h + c + 1)
                    if c == 0 and not first:
                        dve.wait_ge(S("o_ready"), h - 1)
                    dve.tensor_copy(a_v[buf][:, :, c * P:(c + 1) * P],
                                    bank(proj_bank(buf, GROUPS + c), 4, P)[:, 0:GROUPS, :]).then_inc(S("v_copied"), 1)

            def softmax_head(h):
                dve.wait_ge(S("s_ready"), h + 1)
                for g in range(GROUPS):
                    slope = cst[:, bass.ds(C_SLOPE + GROUPS * h + g, 1)]
                    src = bank(3)[:, 2 * P * g:2 * P * g + 2 * P] if g < 2 else bank(4)[:, 0:2 * P]
                    dve.scalar_tensor_tensor(out=a_s0[:, g, :], in0=a_dist[:, g, P:2 * P], scalar=slope,
                                             in1=bank(2)[:, P * g:P * g + P], op0=ALU.mult, op1=ALU.add)
                    ins = dve.scalar_tensor_tensor(out=a_s1[:, g, :], in0=a_dist[:, g, :], scalar=slope,
                                                   in1=src, op0=ALU.mult, op1=ALU.add)
                ins.then_inc(S("s_taken"), 1)
                dve.wait_ge(S("s_taken"), h + 1)
                dve.tensor_reduce(a_mx[:, 0:1], a_s0.rearrange("p g n -> p (g n)"), AX.X, ALU.max)
                link(dve.tensor_reduce(a_mx[:, 1:2], a_s1.rearrange("p g n -> p (g n)"), AX.X, ALU.max))
                dve.tensor_scalar(a_nmx, a_mx, -DSA_SCALE, None, ALU.mult).then_inc(S("nmx_ready"), 1)

            def softmax_tail(h):
                dve.wait_ge(S("e_ready"), 2 * h + 2)
                link(dve.reciprocal(a_den, a_den))
                s0 = a_s0.rearrange("p g n -> p (g n)")
                s1 = a_s1.rearrange("p g n -> p (g n)")
                dve.tensor_scalar(s0, s0, a_den[:, 0:1], None, ALU.mult).then_inc(S("p_ready"), 1)
                dve.tensor_scalar(s1, s1, a_den[:, 1:2], None, ALU.mult).then_inc(S("p_ready"), 1)

            def copy_pT(h):
                dve.wait_ge(S("pT_ready"), 3 * h + 2)
                dve.tensor_copy(a_pT[:, 3:6, :], bank(6, 4, P)[:, 0:3, :]).then_inc(S("pT_copied_d"), 1)

            def step(h_att, h_proj, buf, first=False, last=False):
                softmax_head(h_att)
                softmax_tail(h_att)
                low_qk(h_proj, 2, buf)
                low_v(h_proj, buf)
                copy_pT(h_att)
                if not last:
                    low_qk(h_proj + 1, 0, 1 - buf)
                    low_qk(h_proj + 1, 1, 1 - buf)
                else:
                    for n in range(2):
                        dve.wait_ge(S("w_out_high"), n + 1)
                        dve.tensor_tensor(w_out_lo[n], tile(Tiles.DSA_OUT + n, KD, 512), w_out_hi[n].bitcast(F32),
                                          ALU.subtract).then_inc(S("w_out_low"), 1)
                    dve.wait_ge(S("o_high"), 1)
                    dve.tensor_tensor(a_o_lo[:, 0:HEADS - 1, :], a_o[:, 0:HEADS - 1, :],
                                      a_o_hi[:, 0:HEADS - 1, :].bitcast(F32), ALU.subtract).then_inc(S("o_low"), 1)
                copy_v(h_proj, buf, first)

            for c in range(TC):
                square(0, c)
                roots(0, c, c + 1)
                scale(0, c)
            for c in range(TC):
                gains_on(0, c)
            for c in range(TC):
                dve.wait_ge(S("hT_high"), c + 1)
                dve.tensor_tensor(hT_lo[:, :, c * P:(c + 1) * P], hT[:, :, c * P:(c + 1) * P],
                                  hT_hi[:, c, :, :].bitcast(F32), ALU.subtract).then_inc(S("hT_low"), 1)
            for g in range(GROUPS):
                low_qk(0, g, 0)
            low_v(0, 0)
            low_qk(1, 0, 1)
            low_qk(1, 1, 1)
            copy_v(0, 0, first=True)
            dve.wait_ge(S("cst_in"), 16)
            dve.wait_ge(S("dist_in"), 16)
            step(0, 1, 1, first=True)
            with dve.Fori(0, HEADS // 2 - 2) as it:
                link.enter(it, 4)
                step(2 * it + 1, 2 * it + 2, 0)
                step(2 * it + 2, 2 * it + 3, 1)
            link.leave(HEADS // 2 - 2)
            step(HEADS - 3, HEADS - 2, 0)
            step(HEADS - 2, HEADS - 1, 1, last=True)
            softmax_head(HEADS - 1)
            softmax_tail(HEADS - 1)
            copy_pT(HEADS - 1)
            dve.wait_ge(S("o_high"), 2)
            dve.tensor_tensor(a_o_lo[:, HEADS - 1, :], bank(7)[:, 0:T], a_o_hi[:, HEADS - 1, :].bitcast(F32),
                              ALU.subtract).then_inc(S("o_low"), 1)

            def add_mixed(l):
                def add(c, n):
                    dve.wait_ge(S("mix_out"), 4 * l + 2 * c + n + 1)
                    x_half = x_sb[:, c, 512 * n:512 * n + 512]
                    dve.tensor_tensor(x_half, x_half, bank(2 * c + n), ALU.add).then_inc(S("x_added"), 1)
                return add

            def choose(l, c):
                if c == 0:
                    dve.wait_ge(S("bias_in"), 16)
                    dve.wait_ge(S("fills"), 2)
                dve.wait_ge(S("logits_ready"), TC * l + c + 1)
                lg, bias = bank(4)[:, c * NR:(c + 1) * NR], r_b[:, l * NR:(l + 1) * NR]
                dve.tensor_tensor(r_lg[:, c, :], lg, bias, ALU.add)
                link(dve.tensor_tensor(gp8[:, c, 0:NG], lg[:, 0:NG], bias[:, 0:NG], ALU.add))
                link(dve.max(gm8[:, c, :], gp8[:, c, :]))
                dve.tensor_scalar(ngm[:, c:c + 1], gm8[:, c, 0:1], -1.0, None, ALU.mult).then_inc(S("ngm_ready"), 1)
                link(dve.max_index(gi8[:, c, :], gm8[:, c, :], gp8[:, c, :]))
                link(dve.tensor_copy(gif[:, c:c + 1], gi8[:, c, 0:1]))
                link(dve.tensor_scalar(r_em[:, c, :], cst[:, C_GID:C_GID + NE], gif[:, c:c + 1], BIG,
                                       ALU.is_equal, ALU.mult))
                link(dve.scalar_tensor_tensor(out=r_em[:, c, :], in0=r_em[:, c, :], scalar=-BIG,
                                              in1=r_lg[:, c, NG:NR], op0=ALU.add, op1=ALU.add))
                link(dve.max(ev8[:, c, :], r_em[:, c, :]))
                link(dve.max_index(ei8[:, c, :], ev8[:, c, :], r_em[:, c, :]))
                link(dve.tensor_copy(ef[:, c, :], ei8[:, c, 0:2]))
                for a, m in enumerate((r_m0, r_m1)):
                    ins = dve.tensor_scalar(m[:, c, :], cst[:, C_EID:C_EID + NE], ef[:, c, a:a + 1], None, ALU.is_equal)
                link(ins)
                dve.tensor_tensor(r_m[:, c, :], r_m0[:, c, :], r_m1[:, c, :], ALU.add).then_inc(S("choice_ready"), 1)

            def one_hot(c, a, b):
                link(dve.tensor_scalar(e_oneh[:, c, a:b], e_iota[:, a:b], slot_of[:, c, 0:1], None, ALU.is_equal))
                return dve.scalar_tensor_tensor(out=e_oneh[:, c, a:b], in0=e_iota[:, a:b], scalar=slot_of[:, c, 1:2],
                                                in1=e_oneh[:, c, a:b], op0=ALU.is_equal, op1=ALU.add)

            def place(l, c):
                dve.wait_ge(S("choice_ready"), TC * l + c + 1)
                dve.wait_ge(S("ranks_ready"), TC * l + c + 1)
                for a, m in enumerate((r_m0, r_m1)):
                    ins = dve.tensor_tensor_reduce(out=r_junk[:, NE * a:NE * a + NE], in0=bank(5)[:, NE * c:NE * c + NE],
                                                   in1=m[:, c, :], scale=1.0, scalar=0.0, op0=ALU.mult,
                                                   op1=ALU.add, accum_out=rr[:, c, a:a + 1])
                link(ins)
                dve.tensor_scalar(fits[:, c, :], rr[:, c, :], float(CAP), None, ALU.is_lt)
                link(dve.scalar_tensor_tensor(out=slot_of[:, c, :], in0=ef[:, c, :], scalar=float(CW), in1=rr[:, c, :],
                                              op0=ALU.mult, op1=ALU.add))
                link(dve.scalar_tensor_tensor(out=slot_of[:, c, :], in0=slot_of[:, c, :], scalar=1.0,
                                              in1=fits[:, c, :], op0=ALU.add, op1=ALU.mult))
                if c == 0:
                    dve.wait_ge(S("iota_ready"), l + 1)
                one_hot(c, 0, P).then_inc(S("oneh_first"), 1)

            def weigh_choices(l):
                dve.wait_ge(S("dexp_ready"), l + 1)
                dve.wait_ge(S("gsum_ready"), 2 * l + 2)
                link(dve.scalar_tensor_tensor(out=den1, in0=dif, scalar=1.0, in1=gsum, op0=ALU.add, op1=ALU.mult))
                link(dve.reciprocal(w_in[:, :, 0], den1))
                link(dve.tensor_tensor(w_in[:, :, 1], w_in[:, :, 0], dif, ALU.mult))
                link(dve.tensor_tensor(wgt, w_in, fits, ALU.mult))
                dve.tensor_tensor(wov, w_in, wgt, ALU.subtract).then_inc(S("slots_ready"), 1)
                dve.wait_ge(S("slots_ready"), l + 1)

            def later_slots(l):
                for c in range(TC):
                    one_hot(c, P, NSLOT).then_inc(S("oneh_ready"), 1)
                dve.wait_ge(S("counts_ready"), l + 1)
                link(dve.tensor_reduce(cmax[0:1, :], bank(7)[0:1, 0:NE], AX.X, ALU.max))
                dve.tensor_copy(flag[0:1, l:l + 1], cmax[0:1, :]).then_inc(S("flag_ready"), 1)
                for c in range(TC):
                    link(dve.tensor_scalar(r_wo[:, c, :], r_m0[:, c, :], wov[:, c, 0:1], None, ALU.mult))
                    link(dve.scalar_tensor_tensor(out=r_wo[:, c, :], in0=r_m1[:, c, :], scalar=wov[:, c, 1:2],
                                                  in1=r_wo[:, c, :], op0=ALU.mult, op1=ALU.add))

            def take_gathered(l, grp, half, buf, src=bank(7, 4, P)):
                gain = part(wts, W_GAIN + (3 * l + 1) * KD, KD)
                dve.wait_ge(S("gathered"), (2 * (NGRP + 1)) * l + 2 * grp + half + 1)
                dve.tensor_tensor(e_xT[buf][:, 4 * half:4 * half + 4, :], src,
                                  gain[:, 4 * half:4 * half + 4].unsqueeze(2).to_broadcast([P, 4, P]),
                                  ALU.mult).then_inc(S("xT_ready"), 1)

            def experts(l):
                norm_staged(3 * l + 1, add_mixed(l), lambda: choose(l, 0), lambda: place(l, 0))
                choose(l, 1)
                dve.tensor_tensor(dif, ev8[:, :, 1], ev8[:, :, 0], ALU.subtract).then_inc(S("dif_ready"), 1)
                place(l, 1)
                weigh_choices(l)
                for half in range(2):
                    take_gathered(l, 0, half, 0, bank(4 if half else 7, 4, P))
                later_slots(l)
                dve.wait_ge(S("rows_copied"), l + 1)
                with dve.Fori(0, ITERS) as it:
                    link.enter(it, 2 * BODY // GE)
                    for i in range(BODY):
                        e = NE * l + BODY * it + i
                        grp = (BODY // GE) * it + i // GE
                        dve.wait_ge(S("silu_ready"), e + 1)
                        dve.wait_ge(S("up_ready"), e + 1)
                        dve.tensor_tensor(e_h, e_sil, bank(5)[:, 0:P], ALU.mult).then_inc(S("h_ready"), 1)
                        dve.wait_ge(S("hT_e"), e + 1)
                        dve.tensor_copy(e_hT, bank(5)[:, P:2 * P]).then_inc(S("hT_copied"), 1)
                        dve.wait_ge(S("down_ready"), e + 1)
                        if i % GE == 0:
                            dve.wait_ge(S("scattered"), (NGRP + 1) * l + grp + 1)
                        for q in (0, 1):
                            ins = dve.tensor_copy(e_y[CW * (i % GE):CW * (i % GE) + CW, T * q:T * q + T],
                                                  bank(6)[CW * q:CW * q + CW, 0:T])
                        ins.then_inc(S("y_copied_d"), 1)
                        if i % GE in (1, 2):
                            take_gathered(l, grp + 1, i % GE - 1, (i // GE + 1) % 2)
                        if i % GE == 2:
                            slot_id = cst[:, bass.ds(C_SLOT + grp, 1)]
                            link(dve.scalar_tensor_tensor(out=e_sc2, in0=e_rows[:, 0, :], scalar=slot_id,
                                                          in1=e_rows[:, 2, :], op0=ALU.is_equal, op1=ALU.mult))
                            link(dve.scalar_tensor_tensor(out=e_sc, in0=e_rows[:, 1, :], scalar=slot_id,
                                                          in1=e_rows[:, 3, :], op0=ALU.is_equal, op1=ALU.mult))
                            dve.tensor_tensor(e_sc, e_sc, e_sc2, ALU.add).then_inc(S("sc_ready"), 1)
                link.leave(ITERS)
                count = dve.value_load(flag[0:1, l:l + 1], min_val=0, max_val=T)
                with dve.If(count > CAP):
                    with dve.Fori(0, NE) as e:
                        for c in range(TC):
                            dve.wait_ge(S(f"o_silu{l}"), TC * e + c + 1)
                            dve.wait_ge(S(f"o_up{l}"), TC * e + c + 1)
                            dve.scalar_tensor_tensor(out=o_sil[:, c, :], in0=o_sil[:, c, :],
                                                     scalar=r_wo[:, c, bass.ds(e, 1)], in1=bank(6 + c),
                                                     op0=ALU.mult, op1=ALU.mult).then_inc(S(f"o_h{l}"), 1)
                            dve.wait_ge(S(f"o_turned{l}"), TC * e + c + 1)
                            dve.tensor_copy(o_hT, bank(4, 4, P)).then_inc(S(f"o_hT{l}"), 1)
                    dve.wait_ge(S(f"o_down{l}"), NE + 1)
                for c in range(TC):
                    dve.wait_ge(S("scattered" if c else "scattered_0"), (NGRP + c) * (l + 1))
                    dve.tensor_copy(x_sb[:, c, 0:512], bank(2 * c)).then_inc(S("y_taken_d"), 1)

            def add_ple(l):
                def add(c, n):
                    dve.wait_ge(S("sig_ready"), 4 * l + 2 * n + c + 1)
                    dve.wait_ge(S("pw_ready"), 4 * l + 2 * c + n + 1)
                    g = p_gate[:, c, 512 * n:512 * n + 512]
                    link(dve.tensor_tensor(g, g, bank(2 * c + n), ALU.mult))
                    x_half = x_sb[:, c, 512 * n:512 * n + 512]
                    dve.tensor_tensor(x_half, x_half, g, ALU.add).then_inc(S("x_added"), 1)
                return add

            def ple(l, finish):
                norm_together(3 * l + 2)
                for n in range(2):
                    dve.wait_ge(S("g_high"), 2 * l + n + 1)
                    dve.tensor_tensor(g_lo[n], tile(Tiles.PLE[l] + 1 + n, KD, 512), g_hi[n].bitcast(F32),
                                      ALU.subtract).then_inc(S("g_low"), 1)
                add, i = add_ple(l), 3 * l + 3
                for c in range(TC):
                    add(c, 0)
                    square(i, c)
                for c in range(TC):
                    add(c, 1)
                    roots(i, c, c + 1)
                    finish(c)

            def finish_first(c):
                scale(3, c)
                gains_on(3, c)

            experts(0)
            ple(0, finish_first)

            cos = part(cst, C_COS, TC, HALF)
            sin = part(cst, C_SIN, TC, HALF)
            qg, kvg = part(wts, W_QG, QL // P), wts[:, W_KVG:W_KVG + 1]

            def lat_norm(c):
                dve.wait_ge(S("lat_sq"), c + 1)
                link(dve.tensor_scalar(m_ss[:, c, 0:1], m_ss[:, c, 0:1], 1.0 / QL, EPS, ALU.mult, ALU.add))
                dve.tensor_scalar(m_ss[:, c, 1:2], m_ss[:, c, 1:2], 1.0 / KVL, EPS, ALU.mult,
                                  ALU.add).then_inc(S("lat_var"), 1)
                dve.wait_ge(S("lat_root"), c + 1)
                link(dve.reciprocal(m_rs[:, c, :], m_rs[:, c, :]))
                for j, (a, b) in enumerate(((0, QL), (QL, QL + KVL))):
                    dve.tensor_scalar(m_lat[:, c, a:b], bank(c)[:, a:b], m_rs[:, c, j:j + 1], None,
                                      ALU.mult).then_inc(S("ln_ready"), 1)
                k1, k2 = bank(c)[:, QL + KVL:QL + KVL + HALF], bank(c)[:, QL + KVL + HALF:MLA_IN]
                t, kr = m_t[c], m_kr[:, c, :]
                cc, sn = cos[:, c, :], sin[:, c, :]
                dve.memset(kr[:, 0:NOPE], 0.0)
                dve.tensor_tensor(t[0], k1, cc, ALU.mult)
                dve.tensor_tensor(t[1], k2, sn, ALU.mult)
                dve.tensor_tensor(t[2], k1, sn, ALU.mult)
                link(dve.tensor_tensor(t[3], k2, cc, ALU.mult))
                dve.tensor_tensor(kr[:, NOPE:NOPE + HALF], t[0], t[1], ALU.subtract)
                dve.tensor_tensor(kr[:, NOPE + HALF:QK], t[2], t[3], ALU.add).then_inc(S("kr_ready"), 1)

            def lat_gains(c):
                dve.wait_ge(S("lnT"), c + 1)
                cols = slice(c * P, (c + 1) * P)
                dve.tensor_tensor(m_qlT[:, :, cols], bank(2, 2, T)[:, :, cols],
                                  qg.unsqueeze(2).to_broadcast([P, 2, P]), ALU.mult).then_inc(S("lnT_copied"), 1)
                dve.tensor_scalar(m_kvT[:, cols], bank(3)[:, cols], kvg, None, ALU.mult).then_inc(S("lnT_copied"), 1)

            for c in range(TC):
                lat_norm(c)
                lat_gains(c)
            dve.wait_ge(S("q_ready"), 1)
            dve.tensor_copy(m_q[:, 0, :], ps[:, 4:7, :].rearrange("p a b -> p (a b)")).then_inc(S("q_copied_d"), 1)
            dve.wait_ge(S("q_copied_d"), 1)
            for c in range(TC):
                if c == 1:
                    for j in range(MH // 2):
                        dve.wait_ge(S("k_ready"), j + 1)
                        dve.tensor_copy(m_kT[0:NOPE, 2 * j + 1, :], bank(3 + 4 * (j % 2))[NOPE:2 * NOPE, 0:T]
                                        ).then_inc(S("kb_copied"), 1)
                    dve.wait_ge(S("q_copied_a"), 1)
                qh = m_q[:, c, :].rearrange("p (h n) -> p h n", n=QK)
                q1, q2 = qh[:, :, NOPE:NOPE + HALF], qh[:, :, NOPE + HALF:QK]
                cb = cos[:, c, :].unsqueeze(1).to_broadcast([P, MH, HALF])
                sn = sin[:, c, :].unsqueeze(1).to_broadcast([P, MH, HALF])
                t = m_rope
                dve.tensor_tensor(t[0], q1, cb, ALU.mult)
                dve.tensor_tensor(t[1], q2, sn, ALU.mult)
                dve.tensor_tensor(t[2], q1, sn, ALU.mult)
                link(dve.tensor_tensor(t[3], q2, cb, ALU.mult))
                dve.tensor_tensor(q1, t[0], t[1], ALU.subtract)
                dve.tensor_tensor(q2, t[2], t[3], ALU.add).then_inc(S("q_rot"), 1)
                dve.wait_ge(S("q_rot"), c + 1)
            for c in range(TC):
                dve.wait_ge(S("mv_ready"), c + 1)
                b = 4 if c == 0 else 0
                dve.tensor_copy(m_v[:, c, :], ps[:, b:b + 2, :].rearrange("p a b -> p (a b)")).then_inc(S("mv_copied"), 1)
            causal = cst[:, C_CAUSAL:C_CAUSAL + 384].unsqueeze(1).to_broadcast([P, 2, 384])

            def m_scores(j):
                dve.wait_ge(S("m_s_ready"), j + 1)
                src = ps[:, 0:2, 0:384] if j % 2 == 0 else ps[:, 5:7, 0:384]
                link(dve.tensor_tensor(m_s[j % 3], src, causal, ALU.add))
                dve.tensor_reduce(m_mx[:, 0, :], m_s[j % 3][:, :, 0:P], AX.X, ALU.max)
                link(dve.tensor_reduce(m_mx[:, 1, :], m_s[j % 3][:, :, P:3 * P], AX.X, ALU.max))
                dve.tensor_scalar(m_nmx[j % 3], m_mx, -MLA_SCALE, None, ALU.mult).then_inc(S("m_nmx"), 1)

            def m_probs(j):
                dve.wait_ge(S("m_exp"), j + 1)
                link(dve.reciprocal(m_den[j % 3], m_den[j % 3]))
                for h2 in range(2):
                    for c, (a, b) in enumerate(((0, P), (P, 3 * P))):
                        ins = dve.tensor_scalar(m_s[j % 3][:, h2, a:b], m_s[j % 3][:, h2, a:b],
                                                m_den[j % 3][:, c, h2:h2 + 1], None, ALU.mult)
                ins.then_inc(S("m_p"), 1)

            for j in range(MH // 2):
                if j % 2 == 0:
                    dve.wait_ge(S("qT_ready"), j + 1)
                    dve.tensor_copy(m_qT[0:QK, 2 * j:2 * j + 2, :], bank(2, 2, T)[0:QK, :, :]
                                    ).then_inc(S("qT_copied_d"), 1)
                elif j in (3, 5):
                    m_scores((j - 3) // 2)
            m_probs(0)
            for j in range(MH // 2):
                if j + 2 < MH // 2:
                    m_scores(j + 2)
                if j + 1 < MH // 2:
                    m_probs(j + 1)
                dve.wait_ge(S("m_pT_ready"), j + 1)
                dve.tensor_copy(m_pT[j % 2][:, 0, :], bank(2)[:, 0:384]).then_inc(S("m_pT_copied_d"), 1)

            experts(1)

            def finish_last(c):
                if c == 0:
                    dve.wait_ge(S("f_gain_in"), 16)
                dve.scalar_tensor_tensor(out=x_sb[:, c, :], in0=x_sb[:, c, :], scalar=rstd[:, c:c + 1], in1=f_gain,
                                         op0=ALU.mult, op1=ALU.mult).then_inc(S("final_ready"), 1)

            ple(1, finish_last)

        @block.tensor
        def _(pe):
            def turn_rows(i, c):
                if i == 0 and c == 0:
                    pe.wait_ge(S("ident_in"), 16)
                for b in range(2):
                    pe.wait_ge(S("hs_a" if b else "hs_d"), TC * i + c + 1)
                    for k in range(4):
                        mm = pe.transpose(bank(4 + 2 * c + b)[:, k * P:(k + 1) * P], hs[:, c, 4 * b + k, :], ident)
                    mm.then_inc(S("hT_turned"), 1)

            def three_pass(dst, w_hi, w_lo, x_hi, x_lo, first, last):
                pe.matmul(dst, w_hi, x_hi, start=first, stop=False)
                pe.matmul(dst, w_hi, x_lo, start=False, stop=False)
                return pe.matmul(dst, w_lo, x_hi, start=False, stop=last)

            def project_qk(h, g, buf, first=False):
                pe.wait_ge(S("w_qk_low"), GROUPS * h + g + 1)
                if g == 2:
                    pe.wait_ge(S("qk_copied"), GROUPS * h + 1)
                elif not first:
                    pe.wait_ge(S("v_copied"), TC * h - 1 + g)
                hi, lo = w_qk_hi[(GROUPS * buf + g) % 2], w_qk_lo[buf][g]
                for which in range(2):
                    cols = slice(which * DH, (which + 1) * DH)
                    for k in range(KD):
                        mm = three_pass(bank(proj_bank(buf, g))[:, which * T:which * T + T], hi[:, k, cols],
                                        lo[:, k, cols], hT_hi[:, :, k, :], hT_lo[:, k, :], k == 0, k == KD - 1)
                mm.then_inc(S("qk_ready"), 1)

            def project_v(h, buf):
                pe.wait_ge(S("w_v_low"), h + 1)
                lo = w_v_lo[buf]
                for c in range(TC):
                    pe.wait_ge(S("qk_copied"), GROUPS * h + 2 + c)
                    rows = slice(c * P, (c + 1) * P)
                    for k in range(KD):
                        mm = three_pass(bank(proj_bank(buf, GROUPS + c))[:, 0:GROUPS * DH], hT_hi[:, c, k, :],
                                        hT_lo[:, k, rows], w_v_hi[:, k, :], lo[:, k, :], k == 0, k == KD - 1)
                    mm.then_inc(S("v_ready"), 1)

            def scores(h, buf, first=False):
                pe.wait_ge(S("qk_copied"), GROUPS * h + GROUPS)
                if not first:
                    pe.wait_ge(S("s_taken"), h)
                for g in range(GROUPS):
                    q, k = a_qk[buf][:, g, 0:T], a_qk[buf][:, g, T:2 * T]
                    dst = bank(3)[:, 2 * P * g:2 * P * g + 2 * P] if g < 2 else bank(4)[:, 0:2 * P]
                    pe.matmul(bank(2)[:, P * g:P * g + P], q[:, 0:P], k[:, 0:P], start=True, stop=True)
                    mm = pe.matmul(dst, q[:, P:T], k, start=True, stop=True)
                mm.then_inc(S("s_ready"), 1)

            def turn(h, first=False):
                pe.wait_ge(S("p_ready"), 2 * h + 2)
                for b in range(3):
                    if b == 2:
                        pe.wait_ge(S("pT_copied_a"), 2 * h + 1)
                    elif not first:
                        pe.wait_ge(S("pT_copied_a" if b == 0 else "pT_copied_d"), 2 * h if b == 0 else h)
                    for g in range(GROUPS):
                        src = a_s0[:, g, :] if b == 0 else a_s1[:, g, (b - 1) * P:b * P]
                        mm = pe.transpose(bank(6 if b == 1 else 5)[:, g * P:(g + 1) * P], src, ident)
                    mm.then_inc(S("pT_ready"), 1)

            def weigh(h, buf, first=False):
                pe.wait_ge(S("v_copied"), TC * h + TC)
                pe.wait_ge(S("pT_copied_a"), 2 * h + 2)
                pe.wait_ge(S("pT_copied_d"), h + 1)
                if not first:
                    pe.wait_ge(S("o_copied"), h)
                for g in range(GROUPS):
                    pe.matmul(bank(7)[:, 0:P], a_v[buf][:, g, 0:P], a_pT[:, g, :], start=(g == 0), stop=(g == GROUPS - 1))
                for g in range(GROUPS):
                    for kc in range(2):
                        mm = pe.matmul(bank(7)[:, P:2 * P], a_v[buf][:, g, kc * P:(kc + 1) * P],
                                       a_pT[:, 3 + 3 * kc + g, :], start=(g == 0 and kc == 0),
                                       stop=(g == GROUPS - 1 and kc == 1))
                mm.then_inc(S("o_ready"), 1)

            def step(h_att, h_proj, buf, first=False):
                scores(h_att, 1 - buf, first)
                project_qk(h_proj, 0, buf)
                project_qk(h_proj, 1, buf)
                turn(h_att, first)
                project_qk(h_proj, 2, buf)
                weigh(h_att, 1 - buf, first)
                project_v(h_proj, buf)

            for c in range(TC):
                turn_rows(0, c)
            pe.wait_ge(S("hT_high"), TC)
            pe.wait_ge(S("w_qk_high"), 1)
            for w, h in ((w_qk_hi[0], hT_hi), (w_qk_hi[0], hT_lo), (w_qk_lo[0][0], hT_hi)):
                if h is hT_lo:
                    pe.wait_ge(S("hT_low"), TC)
                if w is not w_qk_hi[0]:
                    pe.wait_ge(S("w_qk_low"), 1)
                for which in range(2):
                    for k in range(KD):
                        first = w is w_qk_hi[0] and h is hT_hi and which == 0 and k == 0
                        last = w is not w_qk_hi[0] and k == KD - 1
                        mm = pe.matmul(bank(proj_bank(0, 0))[:, which * T:which * T + T],
                                       w[:, k, which * DH:(which + 1) * DH],
                                       h[:, k, :] if h is hT_lo else h[:, :, k, :], start=first, stop=last,
                                       skip_group_check=True)
            mm.then_inc(S("qk_ready"), 1)
            for g in range(1, GROUPS):
                project_qk(0, g, 0, first=True)
            project_v(0, 0)
            step(0, 1, 1, first=True)
            with pe.Fori(0, HEADS // 2 - 1) as it:
                step(2 * it + 1, 2 * it + 2, 0)
                step(2 * it + 2, 2 * it + 3, 1)
            def mix_part(l, c, n, ks, last=True):
                rows = slice(c * P, (c + 1) * P)
                for k in ks:
                    if l == 0:
                        mm = three_pass(bank(2 * c + n), a_o_hi[:, k, rows], a_o_lo[:, k, rows], w_out_hi[n][:, k, :],
                                        w_out_lo[n][:, k, :], k == 0, k == KD - 1)
                    else:
                        mm = pe.matmul(bank(2 * c + n), m_o[:, k, rows], tile(Tiles.MLA_OUT + n, KD, 512)[:, k, :],
                                       start=(k == 0), stop=(k == KD - 1))
                if last:
                    mm.then_inc(S("mix_out"), 1)

            scores(HEADS - 1, 1)
            pe.wait_ge(S("v_copied"), TC * HEADS)
            pe.wait_ge(S("w_out_low"), 2)
            pe.wait_ge(S("o_low"), 1)
            for n in range(2):
                mix_part(0, 0, n, range(KD - 1), last=False)
            turn(HEADS - 1)
            mix_part(0, 1, 0, range(BESIDE), last=False)
            weigh(HEADS - 1, 1)
            pe.wait_ge(S("o_low"), 2)

            def gather(l, grp, half):
                for k in range(4):
                    for c in range(TC):
                        mm = pe.matmul(bank(7)[:, k * P:(k + 1) * P], hs[:, c, 4 * half + k, :],
                                       e_oneh[:, c, bass.ds(P * grp, P)], start=(c == 0), stop=(c == TC - 1))
                mm.then_inc(S("gathered"), 1)

            def gather_first(c, half):
                for k in range(4):
                    mm = pe.matmul(bank(4 if half else 7)[:, k * P:(k + 1) * P], hs[:, c, 4 * half + k, :],
                                   e_oneh[:, c, 0:P], start=(c == 0 and k == 0), stop=(c == TC - 1),
                                   skip_group_check=True)
                return mm

            def experts(l):
                i = 3 * l + 1
                low = cst[:, C_LOW:C_LOW + P]
                all_ones = ones.to_broadcast([P, P])

                def logits(c):
                    pe.wait_ge(S("hT_ready"), 4 * i + 2 * c + 2)
                    pe.wait_ge(S("router_in"), 16 * (l + 1))
                    for k in range(KD):
                        mm = pe.matmul(bank(4)[:, c * NR:(c + 1) * NR], hT[:, k, c * P:(c + 1) * P], r_w[:, k, :],
                                       start=(k == 0), stop=(k == KD - 1))
                    mm.then_inc(S("logits_ready"), 1)

                def count(dst, terms):
                    for n, (w, d) in enumerate(terms):
                        mm = pe.matmul(dst, w, r_m[:, d, :], start=(n == 0), stop=(n == len(terms) - 1))
                    return mm

                def ranks(c):
                    pe.wait_ge(S("choice_ready"), TC * l + c + 1)
                    count(bank(5)[:, NE * c:NE * c + NE], [(all_ones, d) for d in range(c)] + [(low, c)]).then_inc(S("ranks_ready"), 1)

                def seed(c):
                    pe.wait_ge(S("x_added"), 8 * l + 2 * c + 2)
                    for n in range(2):
                        mm = pe.matmul(bank(2 * c + n), ident, x_sb[:, c, 512 * n:512 * n + 512], start=True, stop=True)
                    return mm

                for n in range(2):
                    mix_part(l, 0, n, [KD - 1])
                turn_at, logits_at = (2, 6) if l == 0 else (0, KD // 2)
                mix_part(l, 1, 0, range(KD) if l else range(BESIDE, KD))
                mix_part(l, 1, 1, range(turn_at), last=False)
                turn_rows(i, 0)
                mix_part(l, 1, 1, range(turn_at, logits_at), last=False)
                logits(0)
                mix_part(l, 1, 1, range(logits_at, KD))
                ranks(0)
                seed(0)
                turn_rows(i, 1)
                seed(1).then_inc(S("scattered"), 1)
                logits(1)
                pe.wait_ge(S("oneh_first"), TC * l + 1)
                gather_first(0, 0)
                ranks(1)
                gather_first(0, 1)
                pe.wait_ge(S("oneh_first"), TC * (l + 1))
                for half in range(2):
                    gather_first(1, half).then_inc(S("gathered"), 1)
                pe.wait_ge(S("slots_ready"), l + 1)
                for a in range(4):
                    for c in range(TC):
                        col = (slot_of, wgt)[a // 2][:, c, a % 2:a % 2 + 1]
                        mm = pe.matmul(bank(5 + a // 2)[:, (a % 2) * T + c * P:(a % 2) * T + (c + 1) * P],
                                       col.to_broadcast([P, P]), ident, start=True, stop=True)
                mm.then_inc(S("rows_ready"), 1)
                pe.wait_ge(S("xT_ready"), 2 * (NGRP + 1) * l + 1)
                count(bank(7)[:, 0:NE], [(all_ones, d) for d in range(TC)]).then_inc(S("counts_ready"), 1)
                base = Tiles.MOE[l]
                xt0 = 2 * (NGRP + 1) * l
                with pe.Fori(0, ITERS) as it:
                    for i in range(BODY):
                        e = NE * l + BODY * it + i
                        grp = (BODY // GE) * it + i // GE
                        t = base + 3 * i
                        more = (3 * BODY // RING) * it
                        xT = e_xT[(i // GE) % 2][:, :, CW * (i % GE):CW * (i % GE) + CW]
                        if i % GE == 0:
                            pe.wait_ge(S("xT_ready"), xt0 + 2 * grp + 2)
                        for j, b in ((0, 4), (1, 5)):
                            wait_tile(pe, t + j, more)
                            if i == 0 and j == 1:
                                pe.wait_ge(S("rows_copied"), l + 1)
                            for k in range(KD):
                                for q in range(4):
                                    mm = pe.matmul(bank(b)[CW * q:CW * q + CW, 0:P], xT[:, k, :],
                                                   tile(t + j, KD, FF)[:, k, P * q:P * q + P],
                                                   start=(k == 0), stop=(k == KD - 1))
                            mm.then_inc(S("gate_ready" if j == 0 else "up_ready"), 1)
                        pe.wait_ge(S("h_ready"), e + 1)
                        pe.transpose(bank(5)[:, P:2 * P], e_h, ident).then_inc(S("hT_e"), 1)
                        pe.wait_ge(S("hT_copied"), e + 1)
                        wait_tile(pe, t + 2, more)
                        for j in range(FF // P):
                            for q in range(4):
                                mm = pe.matmul(bank(6)[CW * q:CW * q + CW, 0:T], e_hT[:, CW * j:CW * j + CW],
                                               tile(t + 2, FF // P, D)[:, j, T * q:T * q + T],
                                               start=(j == 0), stop=(j == FF // P - 1))
                        mm.then_inc(S("down_ready"), 1)
                        if i == 1:
                            pe.wait_ge(S("flag_ready"), l + 1)
                        if i % GE in (1, 2):
                            pe.wait_ge(S("oneh_ready"), TC * (l + 1))
                            pe.wait_ge(S("xT_ready"), xt0 + 2 * grp + 2 + (i % GE - 1))
                            gather(l, grp + 1, i % GE - 1)
                        pe.wait_ge(S("y_copied_d"), e + 1)
                        pe.wait_ge(S("y_copied_a"), e + 1)
                        if i % GE == GE - 1:
                            pe.wait_ge(S("sc_ready"), NGRP * l + grp + 1)
                            for c in range(TC):
                                for n in range(2):
                                    mm = pe.matmul(bank(2 * c + n), e_sc[:, c * P:(c + 1) * P],
                                                   e_y[:, 512 * n:512 * n + 512], start=False, stop=True,
                                                   skip_group_check=True)
                                mm.then_inc(S("scattered" if c == TC - 1 else "scattered_0"), 1)

                pe.wait_ge(S("flag_ready"), l + 1)
                count = pe.value_load(flag[0:1, l:l + 1], min_val=0, max_val=T)
                with pe.If(count > CAP):
                    with pe.Fori(0, NE) as e:
                        for j, b in ((0, 4), (1, 6)):
                            pe.wait_ge(S(f"o_landed{l}"), 16 * (3 * e + j + 1))
                            for c in range(TC):
                                for k in range(KD):
                                    mm = pe.matmul(bank(b + c), hT[:, k, c * P:(c + 1) * P], e_wide[:, k, :],
                                                   start=(k == 0), stop=(k == KD - 1))
                                mm.then_inc(S(f"o_gate{l}" if j == 0 else f"o_up{l}"), 1)
                        pe.wait_ge(S(f"o_landed{l}"), 16 * (3 * e + 3))
                        for c in range(TC):
                            pe.wait_ge(S(f"o_h{l}"), TC * e + c + 1)
                            for j in range(FF // P):
                                mm = pe.transpose(bank(4)[:, j * P:(j + 1) * P], o_sil[:, c, j * P:(j + 1) * P], ident)
                            mm.then_inc(S(f"o_turned{l}"), 1)
                            pe.wait_ge(S(f"o_hT{l}"), TC * e + c + 1)
                            for n in range(2):
                                for j in range(FF // P):
                                    mm = pe.matmul(bank(2 * c + n), o_hT[:, j, :], e_wide_d[:, j, 512 * n:512 * n + 512],
                                                   start=False, stop=True, skip_group_check=True)
                        mm.then_inc(S(f"o_down{l}"), 1)

            def ple(l):
                pe.wait_ge(S("pT_in"), 16 * (l + 1))
                wait_tile(pe, Tiles.PLE[l])
                for c in range(TC):
                    pe.wait_ge(S("y_taken_d"), TC * l + c + 1)
                    pe.wait_ge(S("y_taken_a"), TC * l + c + 1)
                    for n in range(2):
                        for k in range(PLE // P):
                            mm = pe.matmul(bank(2 * c + n), e_pT[:, k, c * P:(c + 1) * P],
                                           tile(Tiles.PLE[l], PLE // P, D)[:, k, 512 * n:512 * n + 512],
                                           start=(k == 0), stop=(k == PLE // P - 1))
                        mm.then_inc(S("pw_ready"), 1)
                    turn_rows(3 * l + 2, c)
                def gate(c, n, w, h, first=False, last=False):
                    for k in range(KD):
                        x_k = hT_hi[:, c, k, :] if h is hT_hi else hT_lo[:, k, c * P:(c + 1) * P]
                        mm = pe.matmul(bank(4 + 2 * c + n), x_k, w[n][:, k, :], start=(first and k == 0),
                                       stop=(last and k == KD - 1))
                    if last:
                        mm.then_inc(S("pg_ready"), 1)

                pe.wait_ge(S("g_high"), 2 * l + 1)
                for c in range(TC):
                    pe.wait_ge(S("hT_high"), TC * (l + 1) + c + 1)
                    gate(c, 0, g_hi, hT_hi, first=True)
                    pe.wait_ge(S("hT_low"), TC * (l + 1) + c + 1)
                    gate(c, 0, g_hi, hT_lo)
                pe.wait_ge(S("g_low"), 2 * l + 1)
                for c in range(TC):
                    gate(c, 0, g_lo, hT_hi, last=True)
                pe.wait_ge(S("g_low"), 2 * l + 2)
                for c in range(TC):
                    gate(c, 1, g_hi, hT_hi, first=True)
                    gate(c, 1, g_hi, hT_lo)
                    if l == 0 and c == 1:
                        turn_rows(3, 0)
                    gate(c, 1, g_lo, hT_hi, last=True)

            experts(0)
            ple(0)

            def turn_latents(c):
                cols = slice(c * P, (c + 1) * P)
                pe.wait_ge(S("ln_ready"), 2 * c + 2)
                for k in range(QL // P):
                    pe.transpose(bank(2, 2, T)[:, k, cols], m_lat[:, c, k * P:(k + 1) * P], ident)
                pe.transpose(bank(3)[:, cols], m_lat[:, c, QL:QL + KVL], ident)
                pe.wait_ge(S("kr_ready"), c + 1)
                pe.transpose(bank(3)[0:QK, T + c * P:T + (c + 1) * P], m_kr[:, c, :], ident).then_inc(S("lnT"), 1)

            def project_q(c):
                pe.wait_ge(S("lnT_copied"), 2 * c + 2)
                b = 4 if c == 0 else 0
                for n in range(3):
                    for k in range(QL // P):
                        mm = pe.matmul(bank(b + n), m_qlT[:, k, c * P:(c + 1) * P],
                                       tile(Tiles.MLA + 1, QL // P, MH * QK)[:, k, 512 * n:512 * n + 512],
                                       start=(k == 0), stop=(k == QL // P - 1))
                mm.then_inc(S("q_ready"), 1)

            wait_tile(pe, Tiles.MLA)
            for c in range(TC):
                if c == 1:
                    turn_rows(3, 1)
                pe.wait_ge(S("hT_ready"), 12 + 2 * c + 2)
                for k in range(KD):
                    mm = pe.matmul(bank(c)[:, 0:MLA_IN], hT[:, k, c * P:(c + 1) * P],
                                   tile(Tiles.MLA, KD, MLA_IN)[:, k, :], start=(k == 0), stop=(k == KD - 1))
                mm.then_inc(S("lat_ready"), 1)
            turn_latents(0)
            wait_tile(pe, Tiles.MLA + 1)
            project_q(0)
            turn_latents(1)
            project_q(1)
            pe.wait_ge(S("kr_spread"), 1)
            wait_tile(pe, Tiles.MLA + 2)
            kvb = tile(Tiles.MLA + 2, MH, NOPE + MV)
            for j in range(MH // 2):
                if j >= 2:
                    pe.wait_ge(S("k_copied"), j - 1)
                    pe.wait_ge(S("kb_copied"), j - 1)
                for h2 in range(2):
                    mm = pe.matmul(bank(3 + 4 * (j % 2))[NOPE * h2:NOPE * h2 + NOPE, 0:T],
                                   kvb[:, 2 * j + h2, 0:NOPE], m_kvT, start=True, stop=True)
                mm.then_inc(S("k_ready"), 1)
            for c in range(TC):
                b = 4 if c == 0 else 0
                pe.wait_ge(S("q_copied_d" if c == 0 else "q_copied_a"), 1)
                for n in range(2):
                    mm = pe.matmul(bank(b + n), m_kvT[:, c * P:(c + 1) * P],
                                   kvb[:, 8 * n:8 * n + 8, NOPE:NOPE + MV], start=True, stop=True)
                mm.then_inc(S("mv_ready"), 1)
            pe.wait_ge(S("q_rot"), TC)
            def m_scores(j):
                for h2 in range(2):
                    q, k = m_qT[0:QK, 2 * j + h2, :], m_kT[0:QK, 2 * j + h2, :]
                    b = (5 if j % 2 else 0) + h2
                    pe.matmul(bank(b)[:, 0:P], q[:, 0:P], k[:, 0:P], start=True, stop=True)
                    mm = pe.matmul(bank(b)[:, P:3 * P], q[:, P:T], k, start=True, stop=True)
                mm.then_inc(S("m_s_ready"), 1)

            pe.wait_ge(S("k_copied"), MH // 2)
            pe.wait_ge(S("kb_copied"), MH // 2)
            for j in range(MH // 2):
                if j >= 2:
                    pe.wait_ge(S("qT_copied_a" if j % 2 else "qT_copied_d"), j // 2)
                for h2 in range(2):
                    for c in range(TC):
                        mm = pe.transpose(bank(7 if j % 2 else 2, 2, T)[0:QK, h2, c * P:(c + 1) * P],
                                          m_q[:, c, QK * (2 * j + h2):QK * (2 * j + h2) + QK], ident)
                mm.then_inc(S("qT_ready"), 1)
                if j in (2, 4):
                    if j == 2:
                        pe.wait_ge(S("mv_copied"), TC)
                    if j == 4:
                        pe.wait_ge(S("qT_copied_a"), 1)
                    m_scores((j - 2) // 2)
            pe.wait_ge(S("qT_copied_a"), MH // 4)
            pe.wait_ge(S("qT_copied_d"), MH // 4)

            def m_turn(j):
                pe.wait_ge(S("m_p"), j + 1)
                if j >= 1:
                    pe.wait_ge(S("m_pT_copied_a"), j)
                    pe.wait_ge(S("m_pT_copied_d"), j)
                for h2 in range(2):
                    for b in range(3):
                        mm = pe.transpose(bank(2 + h2)[:, b * P:(b + 1) * P], m_s[j % 3][:, h2, b * P:(b + 1) * P], ident)
                mm.then_inc(S("m_pT_ready"), 1)

            def m_weigh(j):
                pe.wait_ge(S("m_pT_copied_a"), j + 1)
                pe.wait_ge(S("m_pT_copied_d"), j + 1)
                if j >= 1:
                    pe.wait_ge(S("m_o_copied"), j)
                for b, (q, k, start, stop) in enumerate(((0, 0, True, True), (1, 0, True, False), (1, 1, False, True))):
                    for h2 in range(2):
                        mm = pe.matmul(bank(4)[MV * h2:MV * h2 + MV, q * P:(q + 1) * P],
                                       m_v[:, k, MV * (2 * j + h2):MV * (2 * j + h2) + MV],
                                       m_pT[j % 2][:, h2, b * P:(b + 1) * P], start=start, stop=stop)
                mm.then_inc(S("m_o_ready"), 1)

            for j in range(MH // 2 - 1):
                if j + 2 < MH // 2:
                    pe.wait_ge(S("m_nmx"), j + 1)
                    m_scores(j + 2)
                m_turn(j)
                if j >= 1:
                    m_weigh(j - 1)
            m_turn(MH // 2 - 1)
            m_weigh(MH // 2 - 2)
            m_weigh(MH // 2 - 1)
            for n in range(2):
                wait_tile(pe, Tiles.MLA_OUT + n)
            pe.wait_ge(S("m_o_copied"), MH // 2 - 1)
            for n in range(2):
                mix_part(1, 0, n, range(KD - 1), last=False)
            pe.wait_ge(S("m_o_copied"), MH // 2)
            experts(1)
            ple(1)


def kernel(**inputs):
    import concourse.bacc as bacc
    from concourse.bass_utils import run_bass_kernel_spmd

    a = {n: np.ascontiguousarray(v) for n, v in inputs.items()}
    gains = [a[n][l] for l in range(2) for n in ("norm_mix", "norm_moe", "norm_ple")]
    routers = [np.concatenate([a["moe_w_group"][l], a["moe_w_expert"][l]], axis=1) for l in range(2)]
    arrays = {
        "x": a["x"],
        "consts": shape_constants(),
        "distances": distance_table(),
        "gains": np.ascontiguousarray(np.concatenate(
            [g.reshape(P, KD) for g in gains]
            + [a["mla_q_norm"].reshape(-1, P).T, a["mla_kv_norm"].reshape(-1, P).T], axis=1)),
        "routers": np.stack([r.reshape(P, KD * NR) for r in routers]),
        "rows": np.concatenate([a["moe_b_group"][0], a["moe_b_expert"][0], a["moe_b_group"][1],
                                a["moe_b_expert"][1], a["norm_final"]]).reshape(1, -1),
        "p_t": np.ascontiguousarray(a["p"][:, 0].transpose(0, 2, 1)),
    }
    for n in ("dsa_w_in", "dsa_w_out", "mla_w_in", "mla_w_qb", "mla_w_kvb", "mla_w_out", "moe_w_gate", "moe_w_up",
              "moe_w_down", "ple_w", "ple_w_gate"):
        arrays[n] = a[n]
    nc = bacc.Bacc("TRN2", target_bir_lowering=False, num_devices=1)
    args = {n: nc.dram_tensor(n, v.shape, mybir.dt.from_np(v.dtype), kind="ExternalInput").ap()
            for n, v in arrays.items()}
    args["out"] = nc.dram_tensor("out", a["x"].shape, F32, kind="ExternalOutput").ap()
    build(nc, **args)
    r = run_bass_kernel_spmd(nc, [arrays], core_ids=[0])
    return r.results[0]["out"]
```
